# Optimizing a Trainium2 kernel written in Bass

```python
import math
import jax, jax.numpy as jnp
from jax import lax
import numpy as np

D_MODEL = 1024
BATCH = 1
SEQ = 128
DEPTH = 2
DEC_BATCH = 1
DEC_SEQ = 512
PAST_LEN = 128

GRID_W = 64
NORM_EPS = 1e-6
M_HEADS = 4
M_DH = 128
M_W = M_HEADS * M_DH
M_CHUNK = 64
G_HEADS = 4
G_DH = 128
G_W = G_HEADS * G_DH
G_CHUNK = 64
CONV_K = 5
A_HEADS = 8
A_KV = 2
A_DH = 64
A_GROUP = A_HEADS // A_KV
A_QW = A_HEADS * A_DH
A_KW = A_KV * A_DH
WINDOW = 128
A_BLOCK = 128
W_LEN = A_BLOCK + 2 * WINDOW
A_SCALE = A_DH ** -0.5
ROPE_BASE = 10000.0
P_HEADS = 8
P_NKEYS = 128
P_EXPERTS = P_NKEYS * P_NKEYS
P_DQ = 256
P_TOPK = 16
P_TOKBLOCK = 128
IN_SPLITS = (M_W, M_W, M_W, 2 * M_HEADS, 2 * M_HEADS, M_W,
             3 * G_W, 2 * G_HEADS, 2 * G_HEADS, G_W,
             A_QW, A_KW, A_KW, 3 * D_MODEL)
N_IN = sum(IN_SPLITS)

kernel_name = "hybrid_mlstm_gdn_swa_peer_diffusion_step"

F32 = jnp.float32

def _split(x, sizes):
    idx = np.cumsum(sizes)[:-1].tolist()
    return jnp.split(x, idx, axis=-1)

def _rms(x, g):
    xf = x.astype(F32)
    y = xf * lax.rsqrt(jnp.mean(xf * xf, -1, keepdims=True) + NORM_EPS)
    return (y * g.astype(F32)).astype(x.dtype)

def _l2n(x):
    return x * lax.rsqrt(jnp.sum(x * x, -1, keepdims=True) + NORM_EPS)

def _flip(a):
    return jnp.flip(a, 1)

def _mlstm_scan(q, k, v, log_i, log_f, state):
    B, T, H, D = q.shape
    L = M_CHUNK
    nc = T // L

    def ch(a):
        a = a.reshape((B, nc, L) + a.shape[2:])
        return jnp.moveaxis(jnp.moveaxis(a, 3, 2), 1, 0)

    causal = jnp.tril(jnp.ones((L, L), bool))

    def step(carry, xs):
        C, n, m = carry
        qi, ki, vi, ii, fi = xs
        b = jnp.cumsum(fi, -1)
        dmat = jnp.where(causal, b[..., :, None] - b[..., None, :] + ii[..., None, :], -jnp.inf)
        m_inter = b + m[..., None]
        m_t = jnp.maximum(jnp.max(dmat, -1), m_inter)
        a_inter = jnp.exp(m_inter - m_t)
        s = jnp.einsum('bhld,bhsd->bhls', qi, ki) * jnp.exp(dmat - m_t[..., None])
        num = a_inter[..., None] * jnp.einsum('bhld,bhde->bhle', qi, C) + jnp.einsum('bhls,bhse->bhle', s, vi)
        den = a_inter * jnp.einsum('bhld,bhd->bhl', qi, n) + jnp.sum(s, -1)
        h = num / jnp.maximum(jnp.abs(den), jnp.exp(-m_t))[..., None]
        m_new = m_t[..., -1]
        dec = jnp.exp(b[..., -1] + m - m_new)
        wk = jnp.exp(b[..., -1:] - b + ii - m_new[..., None])
        C_new = dec[..., None, None] * C + jnp.einsum('bhs,bhsd,bhse->bhde', wk, ki, vi)
        n_new = dec[..., None] * n + jnp.einsum('bhs,bhsd->bhd', wk, ki)
        return (C_new, n_new, m_new), h

    state = tuple(s.astype(F32) for s in state)
    state, hs = lax.scan(step, state, (ch(q), ch(k), ch(v), ch(log_i), ch(log_f)))
    h = jnp.moveaxis(jnp.moveaxis(hs, 0, 1), 2, 3).reshape(B, T, H, D)
    return h, state

def _mlstm_branch(mq, mk, mv, mi, mf, mo, ig_b, fg_b, norm_g, C0, n0, m0):
    B, T, _ = mq.shape
    hd = lambda a: a.reshape(B, T, M_HEADS, M_DH).astype(F32)
    q, k, v = hd(mq), hd(mk) * (M_DH ** -0.5), hd(mv)
    log_i = mi.reshape(B, T, 2, M_HEADS).astype(F32) + ig_b.astype(F32)
    log_f = jax.nn.log_sigmoid(mf.reshape(B, T, 2, M_HEADS).astype(F32) + fg_b.astype(F32))
    h_f, st_f = _mlstm_scan(q, k, v, log_i[:, :, 0], log_f[:, :, 0], (C0[:, 0], n0[:, 0], m0[:, 0]))
    h_b, st_b = _mlstm_scan(_flip(q), _flip(k), _flip(v), _flip(log_i[:, :, 1]), _flip(log_f[:, :, 1]),
                            (C0[:, 1], n0[:, 1], m0[:, 1]))
    h = _rms(h_f + _flip(h_b), norm_g.reshape(M_HEADS, M_DH))
    out = (h.reshape(B, T, M_W) * jax.nn.sigmoid(mo.astype(F32))).astype(mq.dtype)
    new = tuple(jnp.stack([a, b], 1) for a, b in zip(st_f, st_b))
    return out, new

def _dwconv(x, w):
    return lax.conv_general_dilated(x, w[:, None, :].astype(x.dtype), window_strides=(1,),
                                    padding=[(CONV_K // 2, CONV_K // 2)],
                                    dimension_numbers=('NWC', 'WIO', 'NWC'),
                                    feature_group_count=x.shape[-1])

def _gdn_scan(q, k, v, g, beta, S0):
    B, T, H, DK = q.shape
    L = G_CHUNK
    nc = T // L
    ch = lambda a: jnp.moveaxis(a.reshape((B, nc, L) + a.shape[2:]), 3, 1)
    qc, kc, vc, gc, bc = ch(q), ch(k), ch(v), ch(g), ch(beta)
    gc = jnp.cumsum(gc, -1)
    diff = gc[..., :, None] - gc[..., None, :]
    strict = jnp.tril(jnp.ones((L, L), bool), -1)
    incl = jnp.tril(jnp.ones((L, L), bool))
    kk = jnp.einsum('bhnld,bhnsd->bhnls', kc, kc)
    A = jnp.where(strict, bc[..., None] * kk * jnp.exp(jnp.where(strict, diff, 0.0)), 0.0)
    rhs = jnp.concatenate([kc * (bc * jnp.exp(gc))[..., None], vc * bc[..., None]], -1)
    sol = lax.linalg.triangular_solve(A + jnp.eye(L, dtype=F32), rhs, left_side=True, lower=True,
                                      unit_diagonal=True)
    Wc, Uc = sol[..., :DK], sol[..., DK:]
    qk = jnp.einsum('bhnld,bhnsd->bhnls', qc, kc) * jnp.where(incl, jnp.exp(jnp.where(incl, diff, 0.0)), 0.0)
    qg = qc * jnp.exp(gc)[..., None]
    kdec = kc * jnp.exp(gc[..., -1:] - gc)[..., None]
    gl = jnp.exp(gc[..., -1])
    xs = tuple(jnp.moveaxis(a, 2, 0) for a in (qg, kdec, Wc, Uc, qk, gl))

    def step(S, xs):
        qg_i, kd_i, W_i, U_i, qk_i, gl_i = xs
        vn = U_i - jnp.einsum('bhld,bhde->bhle', W_i, S)
        o = jnp.einsum('bhld,bhde->bhle', qg_i, S) + jnp.einsum('bhls,bhse->bhle', qk_i, vn)
        S = gl_i[..., None, None] * S + jnp.einsum('bhld,bhle->bhde', kd_i, vn)
        return S, o

    S, os_ = lax.scan(step, S0.astype(F32), xs)
    o = jnp.moveaxis(jnp.moveaxis(os_, 0, 2), 1, 3).reshape(B, T, H, -1)
    return o, S

def _gdn_branch(gqkv, ga, gb, gz, conv_w, A_log, dt_bias, norm_g, S0):
    B, T, _ = gqkv.shape
    qkv = jax.nn.silu(_dwconv(gqkv, conv_w)).astype(F32)
    q, k, v = [a.reshape(B, T, G_HEADS, G_DH) for a in jnp.split(qkv, 3, -1)]
    q = _l2n(q) * (G_DH ** -0.5)
    k = _l2n(k)
    g = -jnp.exp(A_log.astype(F32)) * jax.nn.softplus(ga.reshape(B, T, 2, G_HEADS).astype(F32) + dt_bias.astype(F32))
    beta = jax.nn.sigmoid(gb.reshape(B, T, 2, G_HEADS).astype(F32))
    o_f, S_f = _gdn_scan(q, k, v, g[:, :, 0], beta[:, :, 0], S0[:, 0])
    o_b, S_b = _gdn_scan(_flip(q), _flip(k), _flip(v), _flip(g[:, :, 1]), _flip(beta[:, :, 1]), S0[:, 1])
    o = _rms(o_f + _flip(o_b), norm_g) * jax.nn.silu(gz.reshape(B, T, G_HEADS, G_DH).astype(F32))
    return o.reshape(B, T, G_W).astype(gqkv.dtype), jnp.stack([S_f, S_b], 1)

def _rope_2d(x):
    T = x.shape[1]
    rows = T // GRID_W
    row = jnp.repeat(jnp.arange(rows), GRID_W).astype(F32)
    col = jnp.tile(jnp.arange(GRID_W), rows).astype(F32)
    half = A_DH // 2
    inv = 1.0 / (ROPE_BASE ** (jnp.arange(0, half, 2, dtype=F32) / half))

    def rot(xa, pos):
        ang = pos[:, None] * inv[None, :]
        cos, sin = jnp.cos(ang)[None, :, None, :], jnp.sin(ang)[None, :, None, :]
        x1, x2 = xa[..., :half // 2], xa[..., half // 2:]
        return jnp.concatenate([x1 * cos - x2 * sin, x1 * sin + x2 * cos], -1)

    xf = x.astype(F32)
    return jnp.concatenate([rot(xf[..., :half], row), rot(xf[..., half:], col)], -1).astype(x.dtype)

def _sink_softmax(s, sink):
    sk = sink[None, :, :, None, None]
    m = jnp.maximum(jnp.max(s, -1, keepdims=True), sk)
    p = jnp.exp(s - m)
    return p / (jnp.sum(p, -1, keepdims=True) + jnp.exp(sk - m))

def _attn_dense(q, k, v, sink):
    B, P = q.shape[:2]
    nb = P // A_BLOCK
    qb = jnp.moveaxis(q.reshape(B, nb, A_BLOCK, A_KV, A_GROUP, A_DH), 1, 0)
    vf = v.astype(F32)

    def blk(qi):
        s = jnp.einsum('bqkgd,bpkd->bkgqp', qi, k).astype(F32) * A_SCALE
        return jnp.einsum('bkgqp,bpkd->bqkgd', _sink_softmax(s, sink), vf)

    o = lax.map(blk, qb)
    return jnp.moveaxis(o, 0, 1).reshape(B, P, A_QW)

def _attn_banded(q, k, v, k_ctx, v_ctx, sink):
    B, T = q.shape[:2]
    nb = T // A_BLOCK
    pad = ((0, 0), (WINDOW, WINDOW), (0, 0), (0, 0))
    k_pad, v_pad = jnp.pad(k, pad), jnp.pad(v.astype(F32), pad)
    vc = v_ctx.astype(F32)
    qb = jnp.moveaxis(q.reshape(B, nb, A_BLOCK, A_KV, A_GROUP, A_DH), 1, 0)

    def blk(args):
        qi, j = args
        start = j * A_BLOCK
        kw = lax.dynamic_slice_in_dim(k_pad, start, W_LEN, axis=1)
        vw = lax.dynamic_slice_in_dim(v_pad, start, W_LEN, axis=1)
        qpos = start + jnp.arange(A_BLOCK)
        kpos = start - WINDOW + jnp.arange(W_LEN)
        valid = (jnp.abs(qpos[:, None] - kpos[None, :]) <= WINDOW) & (kpos >= 0)[None, :] & (kpos < T)[None, :]
        s_loc = jnp.where(valid, jnp.einsum('bqkgd,bwkd->bkgqw', qi, kw).astype(F32) * A_SCALE, -jnp.inf)
        s_ctx = jnp.einsum('bqkgd,bpkd->bkgqp', qi, k_ctx).astype(F32) * A_SCALE
        p = _sink_softmax(jnp.concatenate([s_loc, s_ctx], -1), sink)
        return (jnp.einsum('bkgqw,bwkd->bqkgd', p[..., :W_LEN], vw)
                + jnp.einsum('bkgqp,bpkd->bqkgd', p[..., W_LEN:], vc))

    o = lax.map(blk, (qb, jnp.arange(nb)))
    return jnp.moveaxis(o, 0, 1).reshape(B, T, A_QW)

def _attn_branch(aq, ak, av, qn_g, kn_g, sink, ctx_kv):
    B, T, _ = aq.shape
    q = _rms(aq.reshape(B, T, A_HEADS, A_DH), qn_g)
    k = _rms(ak.reshape(B, T, A_KV, A_DH), kn_g)
    v = av.reshape(B, T, A_KV, A_DH)
    sk = sink.reshape(A_KV, A_GROUP).astype(F32)
    if ctx_kv is None:
        return _attn_dense(q, k, v, sk).astype(aq.dtype), (k, v)
    o = _attn_banded(_rope_2d(q), _rope_2d(k), v, ctx_kv[0], ctx_kv[1], sk)
    return o.astype(aq.dtype), None

def _peer(h, wq, keys, u, v):
    B, T, D = h.shape
    xb = h.reshape(-1, P_TOKBLOCK, D)

    def blk(xi):
        q = (xi @ wq).reshape(P_TOKBLOCK, P_HEADS, 2, P_DQ // 2)
        s = jnp.einsum('nhcd,hckd->nhck', q, keys).astype(F32)
        sv, si = lax.top_k(s, P_TOPK)
        cand = (sv[:, :, 0, :, None] + sv[:, :, 1, None, :]).reshape(P_TOKBLOCK, P_HEADS, P_TOPK * P_TOPK)
        cidx = (si[:, :, 0, :, None] * P_NKEYS + si[:, :, 1, None, :]).reshape(P_TOKBLOCK, P_HEADS, P_TOPK * P_TOPK)
        fv, fi = lax.top_k(cand, P_TOPK)
        eidx = jnp.take_along_axis(cidx, fi, -1)
        gw = jax.nn.softmax(fv, -1)
        ue = jnp.take(u, eidx, axis=0)
        ve = jnp.take(v, eidx, axis=0)
        act = jax.nn.gelu(jnp.einsum('nd,nhkd->nhk', xi, ue).astype(F32), approximate=False)
        return jnp.einsum('nhk,nhkd->nd', gw * act, ve.astype(F32))

    return lax.map(blk, xb).reshape(B, T, D).astype(h.dtype)

def _layer(x, cvec, p, cache):
    B, T, D = x.shape
    mod = (jax.nn.silu(cvec) @ p['ada_w'] + p['ada_b']).reshape(-1, 1, 6 * D)
    sh1, sc1, gt1, sh2, sc2, gt2 = jnp.split(mod, 6, -1)
    h = _rms(x, p['norm1_g']) * (1 + sc1) + sh1
    (mq, mk, mv, mi, mf, mo, gqkv, ga, gb, gz, aq, ak, av, gates) = _split(h @ p['w_in'], IN_SPLITS)
    if cache is None:
        C0 = jnp.zeros((B, 2, M_HEADS, M_DH, M_DH), F32)
        n0 = jnp.zeros((B, 2, M_HEADS, M_DH), F32)
        m0 = jnp.zeros((B, 2, M_HEADS), F32)
        S0 = jnp.zeros((B, 2, G_HEADS, G_DH, G_DH), F32)
        ctx_kv = None
    else:
        C0, n0, m0, S0, kc, vc = cache
        ctx_kv = (kc, vc)
    y_m, (C, n, m) = _mlstm_branch(mq, mk, mv, mi, mf, mo, p['m_ig_b'], p['m_fg_b'], p['m_norm_g'], C0, n0, m0)
    y_g, S = _gdn_branch(gqkv, ga, gb, gz, p['g_conv_w'], p['g_A_log'], p['g_dt_bias'], p['g_norm_g'], S0)
    y_a, new_kv = _attn_branch(aq, ak, av, p['a_qnorm_g'], p['a_knorm_g'], p['a_sink'], ctx_kv)
    g_m, g_g, g_a = jnp.split(jax.nn.sigmoid(gates), 3, -1)
    merged = g_m * (y_m @ p['w_br_m']) + g_g * (y_g @ p['w_br_g']) + g_a * (y_a @ p['w_br_a'])
    x = x + gt1 * (merged @ p['w_out'])
    h2 = _rms(x, p['norm2_g']) * (1 + sc2) + sh2
    x = x + gt2 * _peer(h2, p['p_wq'], p['p_keys'], p['p_u'], p['p_v'])
    if cache is None:
        return x, (C, n, m, S, new_kv[0], new_kv[1])
    return x, None

def setup_inputs(seed: int = 0) -> dict:
    key = jax.random.key(seed)
    ks = iter(jax.random.split(key, 48))
    D = D_MODEL
    nrm = lambda shape, s: jax.random.normal(next(ks), shape, F32) * s
    gain = lambda shape: 1.0 + nrm(shape, 0.02)
    dt = jnp.exp(jax.random.uniform(next(ks), (DEPTH, 2, G_HEADS), F32, math.log(1e-3), math.log(1e-1)))
    return {
        'x_prompt': nrm((BATCH, SEQ, D), 1.0),
        'x_sample': nrm((DEC_BATCH, DEC_SEQ, D), 1.0),
        'state_mlstm_C': nrm((DEC_BATCH, DEPTH, 2, M_HEADS, M_DH, M_DH), 0.05),
        'state_mlstm_n': nrm((DEC_BATCH, DEPTH, 2, M_HEADS, M_DH), 0.5),
        'state_mlstm_m': nrm((DEC_BATCH, DEPTH, 2, M_HEADS), 0.5),
        'state_gdn_S': nrm((DEC_BATCH, DEPTH, 2, G_HEADS, G_DH, G_DH), 0.1),
        'cache_attn_k': nrm((DEC_BATCH, DEPTH, PAST_LEN, A_KV, A_DH), 1.0),
        'cache_attn_v': nrm((DEC_BATCH, DEPTH, PAST_LEN, A_KV, A_DH), 1.0),
        'c': nrm((DEC_BATCH, D), 1.0),
        'c_ctx': nrm((D,), 1.0),
        'ada_w': nrm((DEPTH, D, 6 * D), 0.5 * D ** -0.5),
        'ada_b': nrm((DEPTH, 6 * D), 0.02),
        'norm1_g': gain((DEPTH, D)),
        'norm2_g': gain((DEPTH, D)),
        'w_in': nrm((DEPTH, D, N_IN), D ** -0.5),
        'm_ig_b': nrm((DEPTH, 2, M_HEADS), 0.1),
        'm_fg_b': jnp.broadcast_to(jnp.linspace(3.0, 6.0, M_HEADS, dtype=F32), (DEPTH, 2, M_HEADS)) + nrm((DEPTH, 2, M_HEADS), 0.1),
        'm_norm_g': gain((DEPTH, M_W)),
        'g_conv_w': nrm((DEPTH, CONV_K, 3 * G_W), CONV_K ** -0.5),
        'g_A_log': jnp.log(jax.random.uniform(next(ks), (DEPTH, 2, G_HEADS), F32, 1.0, 16.0)),
        'g_dt_bias': dt + jnp.log(-jnp.expm1(-dt)),
        'g_norm_g': gain((DEPTH, G_DH)),
        'a_qnorm_g': gain((DEPTH, A_DH)),
        'a_knorm_g': gain((DEPTH, A_DH)),
        'a_sink': nrm((DEPTH, A_HEADS), 0.5),
        'w_br_m': nrm((DEPTH, M_W, D), M_W ** -0.5),
        'w_br_g': nrm((DEPTH, G_W, D), G_W ** -0.5),
        'w_br_a': nrm((DEPTH, A_QW, D), A_QW ** -0.5),
        'w_out': nrm((DEPTH, D, D), D ** -0.5),
        'p_wq': nrm((DEPTH, D, P_HEADS * P_DQ), D ** -0.5),
        'p_keys': nrm((DEPTH, P_HEADS, 2, P_NKEYS, P_DQ // 2), (P_DQ // 2) ** -0.5),
        'p_u': nrm((DEPTH, P_EXPERTS, D), D ** -0.5),
        'p_v': nrm((DEPTH, P_EXPERTS, D), 0.3),
    }

def reference(x_prompt, x_sample, state_mlstm_C, state_mlstm_n, state_mlstm_m, state_gdn_S,
              cache_attn_k, cache_attn_v, c, c_ctx, ada_w, ada_b, norm1_g, norm2_g, w_in,
              m_ig_b, m_fg_b, m_norm_g, g_conv_w, g_A_log, g_dt_bias, g_norm_g,
              a_qnorm_g, a_knorm_g, a_sink, w_br_m, w_br_g, w_br_a, w_out,
              p_wq, p_keys, p_u, p_v):
    xp, xs = x_prompt, x_sample
    new_C, new_n, new_m, new_S, new_k, new_v = [], [], [], [], [], []
    for l in range(DEPTH):
        p = dict(ada_w=ada_w[l], ada_b=ada_b[l], norm1_g=norm1_g[l], norm2_g=norm2_g[l], w_in=w_in[l],
                 m_ig_b=m_ig_b[l], m_fg_b=m_fg_b[l], m_norm_g=m_norm_g[l], g_conv_w=g_conv_w[l],
                 g_A_log=g_A_log[l], g_dt_bias=g_dt_bias[l], g_norm_g=g_norm_g[l],
                 a_qnorm_g=a_qnorm_g[l], a_knorm_g=a_knorm_g[l], a_sink=a_sink[l],
                 w_br_m=w_br_m[l], w_br_g=w_br_g[l], w_br_a=w_br_a[l], w_out=w_out[l],
                 p_wq=p_wq[l], p_keys=p_keys[l], p_u=p_u[l], p_v=p_v[l])
        xp, st = _layer(xp, c_ctx, p, None)
        new_C.append(st[0]); new_n.append(st[1]); new_m.append(st[2])
        new_S.append(st[3]); new_k.append(st[4]); new_v.append(st[5])
        cache = (state_mlstm_C[:, l], state_mlstm_n[:, l], state_mlstm_m[:, l], state_gdn_S[:, l],
                 cache_attn_k[:, l], cache_attn_v[:, l])
        xs, _ = _layer(xs, c, p, cache)
    return (xp, xs, jnp.stack(new_C, 1), jnp.stack(new_n, 1), jnp.stack(new_m, 1),
            jnp.stack(new_S, 1), jnp.stack(new_k, 1), jnp.stack(new_v, 1))


_drawn_inputs = setup_inputs


def setup_inputs(seed=0):
    import zlib

    import numpy as np

    out = dict(_drawn_inputs(seed))
    spreads = {}
    factors = {'state_mlstm_C': 8.0,
     'state_mlstm_n': 4.282,
     'state_mlstm_m': 6.703,
     'state_gdn_S': 4.077,
     'cache_attn_k': 4.669,
     'cache_attn_v': 3.87,
     'norm2_g': 5.116,
     'm_norm_g': 8.0,
     'g_norm_g': 8.0,
     'a_qnorm_g': 8.0,
     'a_sink': 64.0}
    for name, (base, spread) in spreads.items():
        noise = np.random.default_rng([zlib.crc32(name.encode()), seed]).standard_normal(out[name].shape)
        drawn = base * np.exp(spread * noise) if base else spread * noise
        out[name] = __import__('jax').numpy.asarray(drawn.astype(out[name].dtype))
    for name, factor in factors.items():
        out[name] = (out[name] * factor).astype(out[name].dtype)
    return out
```

```python
import math
import numpy as np
import concourse.bass as bass
from concourse import mybir
from contextlib import ExitStack, contextmanager

P = 128
DM = 1024
KD = DM // P
DEPTH = 2
NT = 5
TOK = NT * P
NH = 4
DH = 128
EPS = 1e-6
O_MQ, O_MK, O_MV, O_MI, O_MO = 0, 512, 1024, 1536, 1552
O_GQKV, O_GA, O_GZ = 2064, 3600, 3616
O_AQ, O_GATE = 4128, 4896
N_IN = 7968
AH, AKV, ADH = 8, 2, 64
A_SCALE = ADH ** -0.5
PH, PK, PTOP = 8, 128, 16
NEXP = PK * PK
BIG = 1.0e30

_LAYOUT = [("ident", 128), ("ones", 128), ("maskF", 128), ("maskB", 128), ("strictF", 128), ("strictB", 128),
           ("lev", 7 * 128), ("levT", 7 * 128), ("sel", 4 * 128), ("sel16", 16), ("sgn", 1), ("isM", 1),
           ("resetF", 640), ("resetB", 640), ("cos", 4 * 64), ("sin", 4 * 64), ("amask", 512), ("amask4", 384),
           ("iota16", 16)]
COFF = {}
_o = 0
for _n, _w in _LAYOUT:
    COFF[_n] = (_o, _w)
    _o += _w
NCONST = _o


def constants():
    c = np.zeros((P, NCONST), np.float32)

    def put(name, a):
        o, w = COFF[name]
        c[:, o:o + w] = np.asarray(a, np.float32).reshape(P, w)

    r = np.arange(P)
    row, col = r[:, None], r[None, :]
    put("ident", row == col)
    put("ones", np.ones((P, P)))
    put("maskF", np.where(row <= col, 0.0, -BIG))
    put("maskB", np.where(row >= col, 0.0, -BIG))
    put("strictF", row < col)
    put("strictB", row > col)
    lev = np.stack([((row >> j) % 2 == 1) & ((row >> j) == (col >> j) + 1) for j in range(7)], 1)
    put("lev", lev)
    put("levT", np.transpose(lev, (2, 1, 0)))
    sel = np.zeros((P, 4, P))
    sel16 = np.zeros((P, 16))
    sgn = np.zeros(P)
    for q in range(4):
        for h in range(4):
            sel[32 * q + h, h, :] = 1
            sel16[32 * q + h, 4 * q + h] = 1
            sgn[32 * q + h] = 1 if q % 2 else -1
    put("sel", sel)
    put("sel16", sel16)
    put("sgn", sgn)
    put("isM", (r // 32) % 2 == 0)
    t = np.arange(TOK)
    put("resetF", np.broadcast_to(t % P != 0, (P, TOK)))
    put("resetB", np.broadcast_to(t % P != P - 1, (P, TOK)))
    inv = 1.0 / (10000.0 ** (np.arange(0, 32, 2) / 32.0))
    pos = np.arange(4 * P)
    ra, ca = (pos // 64)[:, None] * inv, (pos % 64)[:, None] * inv
    cos = np.concatenate([np.cos(ra), np.cos(ra), np.cos(ca), np.cos(ca)], 1)
    sin = np.concatenate([-np.sin(ra), np.sin(ra), -np.sin(ca), np.sin(ca)], 1)
    put("cos", cos.reshape(4, P, 64).transpose(1, 0, 2))
    put("sin", sin.reshape(4, P, 64).transpose(1, 0, 2))
    before = np.where(col >= row, 0.0, -BIG)
    after = np.where(col <= row, 0.0, -BIG)
    z = np.zeros((P, P))
    put("amask", np.concatenate([before, z, after, z], 1))
    put("amask4", np.concatenate([before, z, z], 1))
    put("iota16", np.broadcast_to(np.arange(16), (P, 16)))
    return c


def program(nc, A, outs, scratch):
    f32 = mybir.dt.float32
    i32 = mybir.dt.int32
    u32 = mybir.dt.uint32
    ALU = mybir.AluOpType
    ACT = mybir.ActivationFunctionType
    AX = mybir.AxisListType
    mm = nc.tensor.matmul
    tr = nc.tensor.transpose
    ds = bass.ds
    V, S, G = nc.vector, nc.scalar, nc.gpsimd

    y_prompt, y_sample, new_C, new_n, new_m, new_S, new_k, new_v = outs
    modd = scratch["mod"]
    stage_sems = []
    stage_scope = []
    top = ExitStack()
    with top:
        def sb(scope, name, shape, dt=f32):
            return scope.enter_context(nc.sbuf_tensor(name, shape, dt))

        def sem(name):
            s = stage_scope[-1].enter_context(nc.semaphore(name))
            stage_sems.append(s)
            return s

        @contextmanager
        def stage():
            with ExitStack() as scope:
                stage_scope.append(scope)
                stage_sems.clear()
                chain_sem.clear()
                yield
                with nc.Block() as block:
                    @block.gpsimd
                    def _(pool):
                        pool.dma_reset()
                        for s in stage_sems:
                            pool.sem_clear(s)
                stage_scope.pop()

        pb = [top.enter_context(nc.psum_tensor(f"pb{i}", [P, 512], f32)) for i in range(8)]
        x = sb(top, "x", [P, NT, DM])
        hT = sb(top, "hT", [P, KD, TOK])
        NCON = COFF["resetF"][0]
        con = sb(top, "con", [P, NCON])
        condT = sb(top, "condT", [P, KD, 2])
        lbase = sb(top, "lbase", [P, 1])

        def K(name):
            o, w = COFF[name]
            return con[:, o:o + w]

        ident, ones = K("ident"), K("ones")
        lev, levT = K("lev").rearrange("p (j s) -> p j s", j=7), K("levT").rearrange("p (j s) -> p j s", j=7)
        sel = K("sel").rearrange("p (h s) -> p h s", h=4)
        v4 = lambda a: a.rearrange("p (h s) -> p h s", h=4)

        def dram_cols(w, l, o, n):
            return w[l, :, o:o + n].rearrange("(k p) n -> p k n", p=P)

        chain_sem, chain_at = {}, {}

        def chain(name, eng):
            if name not in chain_sem:
                chain_sem[name], chain_at[name] = sem(f"{name}_chain"), 0

            def link(ins):
                chain_at[name] += 1
                ins.then_inc(chain_sem[name], 1)
                eng.wait_ge(chain_sem[name], chain_at[name])
            return link


        with stage():
            s_con = sem("constants_in")
            s_x = sem("x_in")
            s_cd = sem("cond_in")
            s_sil = sem("cond_done")
            s_lb = sem("base_cleared")
            with nc.Block() as block:
                @block.sync
                def _(sp):
                    sp.dma_start(con[:, :], A["consts"][:, 0:NCON]).then_inc(s_con, 16)
                    sp.dma_start(x[:, 0, :], A["x_prompt"][0, :, :]).then_inc(s_x, 16)
                    sp.dma_start(x[:, 1:NT, :], A["x_sample"][0, :, :].rearrange("(t p) d -> p t d", p=P)).then_inc(s_x, 16)
                    sp.wait_ge(s_con, 16)
                    sp.wait_ge(s_x, 32)

                @block.vector
                def _(dve):
                    V.memset(lbase[:, :], 0.0).then_inc(s_lb, 1)
                    dve.wait_ge(s_lb, 1)

                @block.scalar
                def _(act):
                    act.dma_start(condT[:, :, 0], A["c_ctx"].rearrange("(k p) -> p k", p=P), allow_slow_non_contiguous=True).then_inc(s_cd, 16)
                    act.dma_start(condT[:, :, 1], A["c"][0, :].rearrange("(k p) -> p k", p=P), allow_slow_non_contiguous=True).then_inc(s_cd, 16)
                    act.wait_ge(s_cd, 32)
                    S.activation(condT[:, :, :], condT[:, :, :], ACT.Silu).then_inc(s_sil, 1)

        yT = alpha = betar = cols = decbc = None

        def layer(l):
            nonlocal yT, alpha, betar, cols, decbc
            with stage():
                stage_modulation(l)
            with stage():
                stage_norm(0)
            with ExitStack() as mix:
                yT = sb(mix, "yT", [P, 3, 4, TOK])
                alpha = sb(mix, "alpha", [P, TOK])
                betar = sb(mix, "betar", [P, TOK])
                cols = sb(mix, "cols", [P, NT, 4, 16])
                decbc = sb(mix, "decbc", [P, NT, 16])
                for build in (stage_rows, stage_mlstm, stage_attention, stage_deltanet, stage_merge):
                    with stage():
                        build(l)
            stage_peer(l)

        def stage_modulation(l):
            ada_in = [sem(f"ada_in{i}") for i in range(3)]
            ada_b_in, ada_done, mod_done, mod_out = sem("ada_b_in"), sem("ada_done"), sem("mod_done"), sem("mod_out")

            NCH = 6 * DM // 512
            with ExitStack() as st:
                W = [sb(st, f"adaW{i}", [P, KD, 512]) for i in range(3)]
                bias = sb(st, "adaB", [2, 6 * DM])
                gains = sb(st, "adaG", [2, 2, DM])
                mod = sb(st, "mod", [2, 6 * DM])
                with nc.Block() as block:
                    @block.sync
                    def _(sp):
                        for n in range(NCH):
                            if n >= 3:
                                sp.wait_ge(ada_done, n - 2)
                            sp.dma_start(W[n % 3][:, :, :], dram_cols(A["ada_w"], l, n * 512, 512)).then_inc(ada_in[n % 3], 16)
                        sp.wait_ge(mod_done, NCH + 2)
                        sp.dma_start(modd, mod[:, :]).then_inc(mod_out, 16)
                        sp.wait_ge(mod_out, 16)

                    @block.scalar
                    def _(act):
                        for j in range(2):
                            act.dma_start(bias[j:j + 1, :], A["ada_b"][l, None, :]).then_inc(ada_b_in, 16)
                            act.dma_start(gains[j:j + 1, 0, :], A["norm1_g"][l, None, :]).then_inc(ada_b_in, 16)
                            act.dma_start(gains[j:j + 1, 1, :], A["norm2_g"][l, None, :]).then_inc(ada_b_in, 16)

                    @block.tensor
                    def _(pe):
                        for n in range(NCH):
                            pe.wait_ge(ada_in[n % 3], 16 * (n // 3 + 1))
                            if n >= 2:
                                pe.wait_ge(mod_done, n - 1)
                            for k in range(KD):
                                last = mm(pb[n % 2][0:2, :], condT[:, k, :], W[n % 3][:, k, :], start=(k == 0), stop=(k == KD - 1))
                            last.then_inc(ada_done, 1)

                    @block.vector
                    def _(dve):
                        dve.wait_ge(ada_b_in, 96)
                        for n in range(NCH):
                            dve.wait_ge(ada_done, n + 1)
                            c = slice(n * 512, (n + 1) * 512)
                            V.tensor_tensor(mod[:, c], pb[n % 2][0:2, :], bias[:, c], ALU.add).then_inc(mod_done, 1)
                        dve.wait_ge(mod_done, NCH)
                        for j, o in enumerate((1, 4)):
                            V.scalar_tensor_tensor(out=mod[:, o * DM:(o + 1) * DM], in0=mod[:, o * DM:(o + 1) * DM], scalar=1.0,
                                                   in1=gains[:, j, :], op0=ALU.add, op1=ALU.mult).then_inc(mod_done, 1)

        def stage_norm(which, h_keep=None):
            s_in, s_sq, s_ms, s_rt, s_rs, s_mul, s_h, s_tr, s_evA, s_evV = [
                sem(n) for n in ("nrm_in", "nrm_sq", "nrm_ms", "nrm_root", "nrm_rstd", "nrm_mul", "nrm_h", "nrm_tr", "nrm_evA", "nrm_evV")]

            with ExitStack() as st:
                AB = sb(st, f"modAB{which}", [P, 2, 2, DM])
                junk = sb(st, f"nrm_junk{which}", [P, 2, DM])
                h = h_keep if h_keep is not None else sb(st, "h", [P, NT, DM])
                ss = sb(st, f"nrm_ss{which}", [P, 3, 8])
                with nc.Block() as block:
                    @block.sync
                    def _(sp):
                        for j, part in enumerate((3 * which + 1, 3 * which)):
                            for g in range(2):
                                sp.dma_start(AB[:, j, g, :], modd[g:g + 1, part * DM:(part + 1) * DM].to_broadcast([P, DM])).then_inc(s_in, 16)

                    @block.scalar
                    def _(act):
                        for t in range(NT):
                            if t >= 2:
                                act.wait_ge(s_sq, t - 1)
                            S.activation(junk[:, t % 2, :], x[:, t, :], ACT.Square, accum_out=ss[:, 0, t:t + 1]).then_inc(s_sq, 1)
                        act.wait_ge(s_ms, 1)
                        S.activation(ss[:, 1, 0:NT], ss[:, 2, 0:NT], ACT.Sqrt).then_inc(s_rt, 1)
                        for t in range(NT):
                            act.wait_ge(s_tr, 2 * t + 1)
                            S.activation(hT[:, 0:4, t * P:(t + 1) * P], v4(pb[2 * (t % 2)][:, :]), ACT.Copy).then_inc(s_evA, 1)

                    @block.vector
                    def _(dve):
                        dve.wait_ge(s_sq, NT)
                        V.tensor_scalar(ss[:, 2, 0:NT], ss[:, 0, 0:NT], 1.0 / DM, EPS, ALU.mult, ALU.add).then_inc(s_ms, 1)
                        dve.wait_ge(s_rt, 1)
                        V.reciprocal(ss[:, 0, 0:NT], ss[:, 1, 0:NT]).then_inc(s_rs, 1)
                        dve.wait_ge(s_rs, 1)
                        dve.wait_ge(s_in, 64)
                        for t in range(NT + 1):
                            if t < NT:
                                g = min(t, 1)
                                V.scalar_tensor_tensor(out=h[:, t, :], in0=x[:, t, :], scalar=ss[:, 0, t:t + 1], in1=AB[:, 0, g, :],
                                                       op0=ALU.mult, op1=ALU.mult).then_inc(s_mul, 1)
                                dve.wait_ge(s_mul, t + 1)
                                V.tensor_tensor(h[:, t, :], h[:, t, :], AB[:, 1, g, :], ALU.add).then_inc(s_h, 1)
                            if t >= 1:
                                dve.wait_ge(s_tr, 2 * t)
                                V.tensor_copy(hT[:, 4:8, (t - 1) * P:t * P], v4(pb[2 * ((t - 1) % 2) + 1][:, :])).then_inc(s_evV, 1)

                    @block.tensor
                    def _(pe):
                        for t in range(NT):
                            pe.wait_ge(s_h, t + 1)
                            if t >= 2:
                                pe.wait_ge(s_evA, t - 1)
                                pe.wait_ge(s_evV, t - 1)
                            for j in range(2):
                                for k in range(4):
                                    last = tr(pb[2 * (t % 2) + j][:, k * P:(k + 1) * P], h[:, t, (4 * j + k) * P:(4 * j + k + 1) * P], ident)
                                last.then_inc(s_tr, 1)

        def stage_rows(l):
            (r_w, r_wz, r_wc, r_clr, r_small, r_p1, r_p2, r_absz, r_exp, r_one, r_ln, r_ea, r_sg, r_mm, r_em, r_ai0, r_ai,
             r_wk0, r_wk, r_dsel, r_dec, r_tr, r_col, r_mout) = [sem("row_" + n) for n in (
                "weights_in", "weights_zeroed", "weights_placed", "cleared", "small_in", "product1", "product2", "abs_z", "exp_done",
                "one_added", "ln_done", "exp_a", "sigmoid", "m_done", "exp_m", "ai_arg", "ai_done", "wk_arg", "wk_done", "dec_sel",
                "dec_bcast", "transposed", "cols_done", "m_out")]

            with ExitStack() as st:
                w16 = sb(st, "w16", [P, 2, KD, 16])
                w1 = sb(st, "w1", [P, KD, P])
                w2 = sb(st, "w2", [P, KD, P])
                small = sb(st, "small", [P, 4])
                sc2 = sb(st, "sc2", [P, 2])
                rst = sb(st, "rst", [P, 2, TOK])
                Z, e_, LF, LI, SG, m_, b, AI, WK, EM = [sb(st, "row_" + n, [P, TOK]) for n in
                                                       ("Z", "e", "LF", "LI", "SG", "m", "b", "AI", "WK", "EM")]
                mp = sb(st, "mp", [P, 3, NT])
                dsel = sb(st, "dsel", [P, NT, 16])
                seg = lambda a: a[:, :].rearrange("p (c s) -> p c s", c=NT)
                with nc.Block() as block:
                    @block.sync
                    def _(sp):
                        for j, o in enumerate((O_MI, O_GA)):
                            sp.dma_start(w16[:, j, :, :], dram_cols(A["w_in"], l, o, 16)).then_inc(r_w, 16)
                        for j, n in enumerate(("resetF", "resetB")):
                            sp.dma_start(rst[:, j, :], A["consts"][:, COFF[n][0]:COFF[n][0] + TOK]).then_inc(r_small, 16)
                        sp.wait_ge(r_clr, 1)
                        for q in range(4):
                            d, isg = q // 2, q % 2
                            column = lambda a: a[l, d, :].rearrange("(h o) -> h o", o=1)
                            r = slice(32 * q, 32 * q + 4)
                            if isg:
                                sp.dma_start(small[r, 0:1], column(A["g_dt_bias"])).then_inc(r_small, 16)
                                sp.dma_start(small[r, 2:3], column(A["g_A_log"])).then_inc(r_small, 16)
                            else:
                                sp.dma_start(small[r, 0:1], column(A["m_fg_b"])).then_inc(r_small, 16)
                                sp.dma_start(small[r, 1:2], column(A["m_ig_b"])).then_inc(r_small, 16)
                                sp.dma_start(small[r, 3:4], column(A["state_mlstm_m"][0])).then_inc(r_small, 16)
                        sp.wait_ge(r_mm, 4)
                        for d, (r, e) in enumerate(((0, P - 1), (64, 0))):
                            sp.dma_start(new_m[0, l, d, :].rearrange("(h o) -> h o", o=1), m_[r:r + 4, e:e + 1]).then_inc(r_mout, 16)
                        sp.wait_ge(r_mout, 32)

                    @block.gpsimd
                    def _(pool):
                        G.memset(w1[:, :, :], 0.0).then_inc(r_wz, 1)
                        G.memset(w2[:, :, :], 0.0).then_inc(r_wz, 1)
                        pool.wait_ge(r_wz, 2)
                        pool.wait_ge(r_w, 32)
                        for q in range(4):
                            d, isg = q // 2, q % 2
                            lo = w16[:, isg, :, 4 * d:4 * d + 4]
                            hi = w16[:, isg, :, 8 + 4 * d:12 + 4 * d]
                            soft, other = (lo, hi) if isg else (hi, lo)
                            G.tensor_copy(w1[:, :, 32 * q:32 * q + 4], soft).then_inc(r_wc, 1)
                            G.tensor_copy(w2[:, :, 32 * q:32 * q + 4], other).then_inc(r_wc, 1)

                    @block.tensor
                    def _(pe):
                        pe.wait_ge(r_wc, 8)
                        for j, (w, done) in enumerate(((w1, r_p1), (w2, r_p2))):
                            for i, (o, n) in enumerate(((0, P), (P, TOK - P))):
                                for k in range(KD):
                                    last = mm(pb[2 * j + i][:, 0:n], w[:, k, :], hT[:, k, o:o + n], start=(k == 0), stop=(k == KD - 1))
                                last.then_inc(done, 1)
                        pe.wait_ge(r_dsel, 1)
                        mm(pb[4][:, 0:80], ones, dsel[:, :, :].rearrange("p c r -> p (c r)"), start=True, stop=True).then_inc(r_dec, 1)
                        pe.wait_ge(r_wk, 1)
                        pe.wait_ge(r_em, 1)
                        pe.wait_ge(r_sg, 2)
                        for t in range(NT):
                            if t >= 2:
                                pe.wait_ge(r_col, t - 1)
                            for j, a in enumerate((AI, WK, EM, SG)):
                                last = tr(pb[5 + t % 2][:, j * P:(j + 1) * P], a[:, t * P:(t + 1) * P], ident)
                            last.then_inc(r_tr, 1)

                    @block.scalar
                    def _(act):
                        act.wait_ge(r_small, 16 * 12)
                        S.activation(sc2[:, 1:2], small[:, 2:3], ACT.Exp).then_inc(r_ea, 1)
                        act.wait_ge(r_absz, 1)
                        S.activation(e_[:, :], e_[:, :], ACT.Exp, scale=-1.0).then_inc(r_exp, 1)
                        act.wait_ge(r_one, 1)
                        S.activation(e_[:, :], e_[:, :], ACT.Ln).then_inc(r_ln, 1)
                        act.wait_ge(r_p2, 2)
                        S.activation(SG[:, 0:P], pb[2][:, 0:P], ACT.Sigmoid).then_inc(r_sg, 1)
                        S.activation(SG[:, P:TOK], pb[3][:, :], ACT.Sigmoid).then_inc(r_sg, 1)
                        act.wait_ge(r_mm, 4)
                        S.activation(EM[:, :], m_[:, :], ACT.Exp, scale=-1.0).then_inc(r_em, 1)
                        act.wait_ge(r_ai0, 1)
                        S.activation(AI[:, :], AI[:, :], ACT.Exp).then_inc(r_ai, 1)
                        act.wait_ge(r_wk0, 1)
                        S.activation(WK[:, :], WK[:, :], ACT.Exp).then_inc(r_wk, 1)

                    @block.vector
                    def _(dve):
                        link = chain("dve", dve)
                        link(V.memset(m_[:, :], 0.0))
                        V.memset(mp[:, :, :], 0.0)
                        V.memset(small[:, :], 0.0).then_inc(r_clr, 1)
                        dve.wait_ge(r_small, 16 * 12)
                        link(V.tensor_tensor(sc2[:, 0:1], small[:, 0:1], K("sgn"), ALU.mult))
                        dve.wait_ge(r_p1, 2)
                        V.tensor_scalar(Z[:, 0:P], pb[0][:, 0:P], K("sgn"), sc2[:, 0:1], ALU.mult, ALU.add)
                        link(V.tensor_scalar(Z[:, P:TOK], pb[1][:, :], K("sgn"), sc2[:, 0:1], ALU.mult, ALU.add))
                        V.scalar_tensor_tensor(out=e_[:, :], in0=Z[:, :], scalar=-1.0, in1=Z[:, :], op0=ALU.mult, op1=ALU.max).then_inc(r_absz, 1)
                        dve.wait_ge(r_exp, 1)
                        V.tensor_scalar(e_[:, :], e_[:, :], 1.0, None, ALU.add).then_inc(r_one, 1)
                        dve.wait_ge(r_ln, 1)
                        link(V.scalar_tensor_tensor(out=LF[:, :], in0=Z[:, :], scalar=0.0, in1=e_[:, :], op0=ALU.max, op1=ALU.add))
                        dve.wait_ge(r_ea, 1)
                        link(V.tensor_scalar(LF[:, :], LF[:, :], sc2[:, 1:2], -1.0, ALU.mult, ALU.mult))
                        dve.wait_ge(r_sg, 2)
                        for o, n, bank in ((0, P, 2), (P, TOK - P, 3)):
                            link(V.tensor_scalar(LI[:, o:o + n], pb[bank][:, 0:n], small[:, 1:2], K("isM"), ALU.add, ALU.mult))
                        scan = V.tensor_tensor_scan
                        for r, step in ((slice(0, 32), 1), (slice(64, 96), -1)):
                            for o, n, init in ((0, P, 0.0), (P, TOK - P, small[r, 3:4])):
                                a = slice(o, o + n) if step == 1 else slice(o + n - 1, o - 1 if o else None, -1)
                                scan(out=m_[r, a], data0=LF[r, a], data1=LI[r, a], initial=init, op0=ALU.add, op1=ALU.max).then_inc(r_mm, 1)
                        dve.wait_ge(r_mm, 4)
                        link(scan(out=b[0:64, :], data0=rst[0:64, 0, :], data1=LF[0:64, :], initial=0.0, op0=ALU.mult, op1=ALU.add))
                        link(scan(out=b[64:P, ::-1], data0=rst[64:P, 1, ::-1], data1=LF[64:P, ::-1], initial=0.0, op0=ALU.mult, op1=ALU.add))
                        V.tensor_tensor(alpha[:, :], b[:, :], m_[:, :], ALU.subtract)
                        link(V.tensor_tensor(betar[:, :], LI[:, :], b[:, :], ALU.subtract))
                        V.tensor_copy(mp[0:64, 0, 1:2], small[0:64, 3:4])
                        V.tensor_copy(mp[0:64, 0, 2:NT], seg(m_)[0:64, 1:NT - 1, P - 1])
                        V.tensor_copy(mp[64:P, 0, NT - 1:NT], small[64:P, 3:4])
                        V.tensor_copy(mp[64:P, 0, 1:NT - 1], seg(m_)[64:P, 2:NT, 0])
                        V.tensor_copy(mp[0:64, 1, :], seg(alpha)[0:64, :, P - 1])
                        link(V.tensor_copy(mp[64:P, 1, :], seg(alpha)[64:P, :, 0]))
                        V.tensor_tensor(seg(AI), seg(alpha), mp[:, 0, :, None].to_broadcast([P, NT, P]), ALU.add).then_inc(r_ai0, 1)
                        V.tensor_tensor(seg(WK), seg(betar), mp[:, 1, :, None].to_broadcast([P, NT, P]), ALU.add).then_inc(r_wk0, 1)
                        dve.wait_ge(r_ai, 1)
                        V.tensor_copy(mp[0:64, 2, :], seg(AI)[0:64, :, P - 1])
                        link(V.tensor_copy(mp[64:P, 2, :], seg(AI)[64:P, :, 0]))
                        V.tensor_tensor(dsel[:, :, :], K("sel16")[:, None, :].to_broadcast([P, NT, 16]),
                                        mp[:, 2, :, None].to_broadcast([P, NT, 16]), ALU.mult).then_inc(r_dsel, 1)
                        dve.wait_ge(r_dec, 1)
                        V.tensor_copy(decbc[:, :, :].rearrange("p c r -> p (c r)"), pb[4][:, 0:80])
                        for t in range(NT):
                            dve.wait_ge(r_tr, t + 1)
                            src = pb[5 + t % 2][:, :].rearrange("p (j q h) -> p j q h", j=4, q=4)[:, :, :, 0:4]
                            V.tensor_copy(cols[:, t, :, :].rearrange("p j (q h) -> p j q h", q=4), src).then_inc(r_col, 1)

        W_BUFS = 3

        def project(name, chunks, jobs):
            in_ = [sem(f"{name}_w_in{i}") for i in range(W_BUFS)]
            done, evA, evV = [sem(f"{name}_{n}") for n in ("product", "evac_act", "evac_dve")]
            on_act = [(j[5] in (ACT.Sigmoid, ACT.Silu)) or i % 2 == 0 for i, j in enumerate(jobs)]
            act_before = [sum(on_act[:i]) for i in range(len(jobs) + 1)]
            last_job = {j[0]: i for i, j in enumerate(jobs)}

            def run(l, Wb):
                with nc.Block() as block:
                    @block.sync
                    def _(sp):
                        for n, (w, o, width) in enumerate(chunks):
                            if n >= W_BUFS:
                                sp.wait_ge(done, last_job[n - W_BUFS] + 1)
                            sp.dma_start(Wb[n % W_BUFS][:, :, 0:width], dram_cols(w, l, o, width)).then_inc(in_[n % W_BUFS], 16)

                    @block.tensor
                    def _(pe):
                        seen = -1
                        for i, (n, kind, c, size, out, func) in enumerate(jobs):
                            if n != seen:
                                pe.wait_ge(in_[n % W_BUFS], 16 * (n // W_BUFS + 1))
                                seen = n
                            if i >= 8:
                                pe.wait_ge(evA if on_act[i - 8] else evV,
                                           act_before[i - 7] if on_act[i - 8] else i - 7 - act_before[i - 7])
                            W = Wb[n % W_BUFS]
                            for k in range(KD):
                                if kind == "rows":
                                    last = mm(pb[i % 8][:, 0:size], hT[:, k, c * P:(c + 1) * P], W[:, k, 0:size], start=(k == 0), stop=(k == KD - 1))
                                else:
                                    last = mm(pb[i % 8][:, 0:size[1]], W[:, k, c * P:(c + 1) * P], hT[:, k, size[0]:size[0] + size[1]],
                                              start=(k == 0), stop=(k == KD - 1))
                            last.then_inc(done, 1)

                    @block.scalar
                    def _(act):
                        for i, (n, kind, c, size, out, func) in enumerate(jobs):
                            if on_act[i]:
                                act.wait_ge(done, i + 1)
                                src = pb[i % 8][:, 0:size if kind == "rows" else size[1]]
                                src = src if kind == "cols" or len(out.shape) == 2 else v4(src)
                                if isinstance(func, float):
                                    S.activation(out, src, ACT.Copy, scale=func).then_inc(evA, 1)
                                else:
                                    S.activation(out, src, func).then_inc(evA, 1)

                    @block.vector
                    def _(dve):
                        for i, (n, kind, c, size, out, func) in enumerate(jobs):
                            if not on_act[i]:
                                dve.wait_ge(done, i + 1)
                                src = pb[i % 8][:, 0:size if kind == "rows" else size[1]]
                                src = src if kind == "cols" or len(out.shape) == 2 else v4(src)
                                V.tensor_scalar(out, src, func, None, ALU.mult).then_inc(evV, 1)
            return run

        FT, BT = (0, 1, 2, 3, 4), (0, 4, 3, 2, 1)

        def stage_mlstm(l):
            (m_st_in, m_zero, m_kt, m_ktev, m_D, m_KQ, m_dm, m_E, m_S, m_inter, m_is, m_intra, m_num, m_kw, m_upd, m_C, m_out, m_O) = [
                sem("m_" + n) for n in ("state_in", "zeroed", "k_transposed", "k_tokens", "D", "KQ", "masked", "E", "S", "inter",
                                        "inter_scaled", "intra", "num", "k_weighted", "update", "C", "state_out", "O")]
            with ExitStack() as st:
                qT = sb(st, "m_qT", [P, 4, TOK])
                kT = sb(st, "m_kT", [P, 4, TOK])
                kt = sb(st, "m_k", [P, NT, 4, DH])
                v1 = sb(st, "m_v1", [P, NT, 4, DH + 1])
                mo = sb(st, "m_o", [P, NT, 512])
                O = sb(st, "m_O", [P, NT, 512])
                chunks = [(A["w_in"], o, 512) for o in (O_MQ, O_MK, O_MV, O_MO)]
                jobs = []
                for n, (dst, scale) in enumerate(((qT, 1.0), (kT, DH ** -0.5))):
                    for c in range(4):
                        for o, w in ((0, P), (P, TOK - P)):
                            jobs.append((n, "cols", c, (o, w), dst[:, c, o:o + w], scale))
                jobs += [(2, "rows", t, 512, v1[:, t, :, 0:DH], 1.0) for t in range(NT)]
                jobs += [(3, "rows", t, 512, mo[:, t, :], ACT.Sigmoid) for t in range(NT)]
                with ExitStack() as wst:
                    Wb = [sb(wst, f"m_W{i}", [P, KD, 512]) for i in range(W_BUFS)]
                    project("mproj", chunks, jobs)(l, Wb)
                with ExitStack() as sc:
                    C = [[sb(sc, f"m_C{g}{d}", [P, 4, DH + 1]) for d in range(2)] for g in range(2)]
                    E = [sb(sc, f"m_E{d}", [P, 512]) for d in range(2)]
                    Sm = [sb(sc, f"m_S{d}", [P, 512]) for d in range(2)]
                    num = [sb(sc, f"m_num{d}", [P, 4, DH + 1]) for d in range(2)]
                    kw = [sb(sc, f"m_kw{d}", [P, 4, DH]) for d in range(2)]
                    den = [sb(sc, f"m_den{d}", [P, 4]) for d in range(2)]
                    bD, bKQ, bN = [pb[0], pb[4]], [pb[1], pb[5]], [(pb[2], pb[3]), (pb[6], pb[7])]
                    hp = lambda bank: bank[:, 0:2 * (DH + 1)].rearrange("p (h e) -> p h e", h=2)
                    tile = lambda d, p: (FT, BT)[d][p]
                    sl = lambda c: slice(c * P, (c + 1) * P)
                    units = [(p, d) for p in range(NT) for d in range(2)]
                    with nc.Block() as block:
                        @block.sync
                        def _(sp):
                            for d in range(2):
                                sp.dma_start(C[1][d][:, :, 0:DH], A["state_mlstm_C"][0, l, d, :, :, :].rearrange("h d e -> d h e")).then_inc(m_st_in, 16)
                                sp.dma_start(C[1][d][:, :, DH], A["state_mlstm_n"][0, l, d, :, :].rearrange("h d -> d h"),
                                             allow_slow_non_contiguous=True).then_inc(m_st_in, 16)
                            sp.wait_ge(m_C, 2)
                            for d in range(2):
                                sp.dma_start(new_C[0, l, d, :, :, :].rearrange("h d e -> d h e"), C[0][d][:, :, 0:DH]).then_inc(m_out, 16)
                                sp.dma_start(new_n[0, l, d, :, :].rearrange("h d -> d h"), C[0][d][:, :, DH],
                                             allow_slow_non_contiguous=True).then_inc(m_out, 16)
                            sp.wait_ge(m_out, 64)

                        @block.gpsimd
                        def _(pool):
                            for d in range(2):
                                G.memset(C[0][d][:, :, :], 0.0)
                            G.memset(v1[:, :, :, DH:DH + 1], 1.0)
                            G.memset(O[:, :, :], 0.0).then_inc(m_zero, 1)
                            for u, (p, d) in enumerate(units):
                                c = tile(d, p)
                                pool.wait_ge(m_ktev, NT)
                                if u >= 2:
                                    pool.wait_ge(m_upd, u - 1)
                                G.tensor_tensor(kw[d][:, :, :], kt[:, c, :, :],
                                                cols[:, c, 1, 8 * d:8 * d + 4, None].to_broadcast([P, 4, DH]), ALU.mult).then_inc(m_kw, 1)

                        @block.tensor
                        def _(pe):
                            for t in range(NT):
                                if t >= 2:
                                    pe.wait_ge(m_ktev, t - 1)
                                for h in range(4):
                                    last = tr(pb[6 + t % 2][:, h * P:(h + 1) * P], kT[:, h, sl(t)], ident)
                                last.then_inc(m_kt, 1)
                            pe.wait_ge(m_zero, 1)
                            for p in range(NT):
                                for d in range(2):
                                    u, c = 2 * p + d, tile(d, p)
                                    r = slice(64 * d, 64 * d + 32)
                                    if u >= 2:
                                        pe.wait_ge(m_dm, u - 1)
                                    elif u == 0:
                                        pe.wait_ge(m_ktev, NT)
                                    mm(bD[d][:, :], betar[r, sl(c)], sel[r, :, :].rearrange("p h s -> p (h s)"), start=True, stop=False)
                                    for h in range(4):
                                        last = mm(bD[d][:, sl(h)], sel[r, h, :], alpha[r, sl(c)], start=False, stop=(h == 3))
                                    last.then_inc(m_D, 1)
                                    if u >= 2:
                                        pe.wait_ge(m_S, u - 1)
                                    for h in range(4):
                                        last = mm(bKQ[d][:, sl(h)], kT[:, h, sl(c)], qT[:, h, sl(c)], start=True, stop=True)
                                    last.then_inc(m_KQ, 1)
                                if p == 1:
                                    pe.wait_ge(m_st_in, 64)
                                for d in range(2):
                                    u, c = 2 * p + d, tile(d, p)
                                    if u >= 2:
                                        pe.wait_ge(m_C, u - 1)
                                    for h in range(4):
                                        last = mm(hp(bN[d][h // 2])[:, h % 2, :], qT[:, h, sl(c)], C[min(p, 1)][d][:, h, :], start=True, stop=True)
                                    last.then_inc(m_inter, 1)
                                for d in range(2):
                                    u, c = 2 * p + d, tile(d, p)
                                    pe.wait_ge(m_S, u + 1)
                                    pe.wait_ge(m_is, u + 1)
                                    for h in range(4):
                                        last = mm(hp(bN[d][h // 2])[:, h % 2, :], Sm[d][:, sl(h)], v1[:, c, h, :], start=True, stop=True)
                                    last.then_inc(m_intra, 1)
                                for d in range(2):
                                    u, c = 2 * p + d, tile(d, p)
                                    pe.wait_ge(m_num, u + 1)
                                    pe.wait_ge(m_kw, u + 1)
                                    for h in range(4):
                                        last = mm(hp(bN[d][h // 2])[:, h % 2, :], kw[d][:, h, :], v1[:, c, h, :], start=True, stop=True)
                                    last.then_inc(m_upd, 1)

                        @block.scalar
                        def _(act):
                            for t in range(NT):
                                act.wait_ge(m_kt, t + 1)
                                S.activation(kt[:, t, :, :], v4(pb[6 + t % 2][:, :]), ACT.Copy).then_inc(m_ktev, 1)
                            for p in range(NT):
                                for d in range(2):
                                    act.wait_ge(m_dm, 2 * p + d + 1)
                                    S.activation(E[d][:, :], E[d][:, :], ACT.Exp).then_inc(m_E, 1)
                                for d in range(2):
                                    u, c = 2 * p + d, tile(d, p)
                                    act.wait_ge(m_inter, u + 1)
                                    if u >= 2:
                                        act.wait_ge(m_O, u - 1)
                                    for h in range(4):
                                        last = S.activation(num[d][:, h, :], hp(bN[d][h // 2])[:, h % 2, :], ACT.Copy,
                                                            scale=cols[:, c, 0, 8 * d + h:8 * d + h + 1])
                                    last.then_inc(m_is, 1)

                        @block.vector
                        def _(dve):
                            link = chain("dve", dve)
                            for p in range(NT):
                                for d in range(2):
                                    u = 2 * p + d
                                    dve.wait_ge(m_D, u + 1)
                                    mask = K("maskB" if d else "maskF")
                                    V.tensor_tensor(v4(E[d][:, :]), v4(bD[d][:, :]), mask[:, None, :].to_broadcast([P, 4, P]), ALU.min).then_inc(m_dm, 1)
                                for d in range(2):
                                    u = 2 * p + d
                                    dve.wait_ge(m_E, u + 1)
                                    dve.wait_ge(m_KQ, u + 1)
                                    V.tensor_tensor(Sm[d][:, :], E[d][:, :], bKQ[d][:, :], ALU.mult).then_inc(m_S, 1)
                                for d in range(2):
                                    u, c = 2 * p + d, tile(d, p)
                                    dve.wait_ge(m_intra, u + 1)
                                    for j in range(2):
                                        last = V.tensor_tensor(num[d][:, 2 * j:2 * j + 2, :], num[d][:, 2 * j:2 * j + 2, :], hp(bN[d][j]), ALU.add)
                                    last.then_inc(m_num, 1)
                                    dve.wait_ge(m_num, u + 1)
                                    dn = num[d][:, :, DH]
                                    link(V.scalar_tensor_tensor(out=den[d][:, :], in0=dn, scalar=-1.0, in1=dn, op0=ALU.mult, op1=ALU.max))
                                    link(V.tensor_tensor(den[d][:, :], den[d][:, :], cols[:, c, 2, 8 * d:8 * d + 4], ALU.max))
                                    link(V.reciprocal(den[d][:, :], den[d][:, :]))
                                    for h in range(4):
                                        o = O[:, c, sl(h)]
                                        last = V.scalar_tensor_tensor(out=o, in0=num[d][:, h, 0:DH], scalar=den[d][:, h:h + 1], in1=o,
                                                                      op0=ALU.mult, op1=ALU.add)
                                    last.then_inc(m_O, 1)
                                for d in range(2):
                                    u, c = 2 * p + d, tile(d, p)
                                    dve.wait_ge(m_upd, u + 1)
                                    Cd = C[min(p, 1)][d]
                                    for h in range(4):
                                        last = V.scalar_tensor_tensor(out=Cd[:, h, :], in0=Cd[:, h, :], scalar=decbc[:, c, 8 * d + h:8 * d + h + 1],
                                                                      in1=hp(bN[d][h // 2])[:, h % 2, :], op0=ALU.mult, op1=ALU.add)
                                    last.then_inc(m_C, 1)
                finish_mixer(0, l, O, mo, A["m_norm_g"], 512)

        def finish_mixer(which, l, O, gate, gain, width):
            s_in, s_sq, s_ms, s_rt, s_y, s_tr, s_ev = [sem(f"fin_{n}") for n in ("gain_in", "squared", "mean_square", "root", "gated", "transposed", "evac")]

            with ExitStack() as st:
                sq = sb(st, f"fin_sq{which}", [P, NT * 4, DH])
                g = sb(st, f"fin_g{which}", [P, width])
                ms = sb(st, f"fin_ms{which}", [P, NT * 4])
                Oh = O[:, :, :].rearrange("p t (h e) -> p (t h) e", h=4)
                with nc.Block() as block:
                    @block.sync
                    def _(sp):
                        sp.dma_start(g[:, :], gain[l, None, :].to_broadcast([P, width])).then_inc(s_in, 16)

                    @block.scalar
                    def _(act):
                        S.activation(sq[:, :, :], Oh, ACT.Square).then_inc(s_sq, 1)
                        act.wait_ge(s_ms, 1)
                        S.activation(ms[:, :], ms[:, :], ACT.Sqrt).then_inc(s_rt, 1)
                        for t in range(NT):
                            act.wait_ge(s_tr, t + 1)
                            S.activation(yT[:, which, :, t * P:(t + 1) * P], v4(pb[t % 2][:, :]), ACT.Copy).then_inc(s_ev, 1)

                    @block.vector
                    def _(dve):
                        link = chain("dve", dve)
                        dve.wait_ge(s_sq, 1)
                        link(V.tensor_reduce(ms[:, :], sq[:, :, :], AX.X, ALU.add))
                        V.tensor_scalar(ms[:, :], ms[:, :], 1.0 / DH, EPS, ALU.mult, ALU.add).then_inc(s_ms, 1)
                        dve.wait_ge(s_rt, 1)
                        link(V.reciprocal(ms[:, :], ms[:, :]))
                        dve.wait_ge(s_in, 16)
                        link(V.tensor_tensor(Oh, Oh, ms[:, :, None].to_broadcast([P, NT * 4, DH]), ALU.mult))
                        link(V.tensor_tensor(Oh, Oh, g[:, None, :].to_broadcast([P, NT * 4, DH]), ALU.mult) if width == DH else
                             V.tensor_tensor(O[:, :, :], O[:, :, :], g[:, None, :].to_broadcast([P, NT, 512]), ALU.mult))
                        for t in range(NT):
                            V.tensor_tensor(O[:, t, :], O[:, t, :], gate[:, t, :], ALU.mult).then_inc(s_y, 1)

                    @block.tensor
                    def _(pe):
                        for t in range(NT):
                            pe.wait_ge(s_y, t + 1)
                            if t >= 2:
                                pe.wait_ge(s_ev, t - 1)
                            for h in range(4):
                                last = tr(pb[t % 2][:, h * P:(h + 1) * P], O[:, t, h * P:(h + 1) * P], ident)
                            last.then_inc(s_tr, 1)

        QW, KVW = AH * ADH, AKV * ADH
        NQK = AH + AKV

        def stage_attention(l):
            (a_small, a_ctx, a_sq, a_ms, a_rt, a_nrm, a_rp, a_kv, a_dup, a_trq, a_evq, a_trk, a_evk, a_sc, a_msk, a_nm, a_df, a_ex, a_es, a_pt,
             a_pe, a_pv, a_o, a_ot, a_oe) = [sem("a_" + n) for n in (
                "small_in", "ctx_in", "squared", "mean_square", "root", "normed", "rotated", "kv_out", "k_doubled", "q_transposed", "q_evac",
                "k_transposed", "k_evac", "scores", "masked", "neg_max", "sink_diff", "exp", "exp_sink", "p_transposed", "p_evac", "pv", "o",
                "o_transposed", "o_evac")]
            with ExitStack() as st:
                a = sb(st, "a_qkv", [P, NT, QW + 2 * KVW])
                with ExitStack() as wst:
                    Wb = [sb(wst, f"a_W{i}", [P, KD, 512]) for i in range(W_BUFS)]
                    project("aproj", [(A["w_in"], O_AQ, QW), (A["w_in"], O_AQ + QW, 2 * KVW)],
                            [(0, "rows", t, QW, a[:, t, 0:QW], 1.0) for t in range(NT)] +
                            [(1, "rows", t, 2 * KVW, a[:, t, QW:], 1.0) for t in range(NT)])(l, Wb)
                rot = sb(st, "a_rot", [P, 2, 4, ADH])
                amask = sb(st, "a_mask", [P, 512 + 384])
                gq = sb(st, "a_gq", [P, ADH])
                gk = sb(st, "a_gk", [P, ADH])
                sink = sb(st, "a_sinks", [P, AH])
                kc = sb(st, "a_kc", [P, 2, KVW])
                sq = sb(st, "a_sq", [P, 2, NQK * ADH])
                ms = sb(st, "a_ms", [P, NT, NQK])
                kd = sb(st, "a_kd", [P, NT + 1, AKV, 2, ADH])
                qT = sb(st, "a_qT", [P, AH // 2, TOK])
                kT = sb(st, "a_kT", [P, AKV, TOK + P])
                with nc.Block() as block:
                    @block.sync
                    def _(sp):
                        sp.dma_start(gq[:, :], A["a_qnorm_g"][l, None, :].to_broadcast([P, ADH])).then_inc(a_small, 16)
                        sp.dma_start(gk[:, :], A["a_knorm_g"][l, None, :].to_broadcast([P, ADH])).then_inc(a_small, 16)
                        sp.dma_start(sink[:, :], A["a_sink"][l, None, :].to_broadcast([P, AH])).then_inc(a_small, 16)
                        for j, n in enumerate(("cos", "sin")):
                            sp.dma_start(rot[:, j, :, :].rearrange("p t e -> p (t e)"), A["consts"][:, COFF[n][0]:COFF[n][0] + 256]).then_inc(a_small, 16)
                        sp.dma_start(amask[:, :], A["consts"][:, COFF["amask"][0]:COFF["amask"][0] + 896]).then_inc(a_small, 16)
                        sp.dma_start(kc[:, 0, :], A["cache_attn_k"][0, l, :, :, :].rearrange("t h d -> t (h d)")).then_inc(a_ctx, 16)
                        sp.dma_start(kc[:, 1, :], A["cache_attn_v"][0, l, :, :, :].rearrange("t h d -> t (h d)")).then_inc(a_ctx, 16)
                        sp.wait_ge(a_nrm, 1)
                        sp.dma_start(new_k[0, l, :, :, :].rearrange("t h d -> t (h d)"), a[:, 0, QW:QW + KVW]).then_inc(a_kv, 16)
                        sp.dma_start(new_v[0, l, :, :, :].rearrange("t h d -> t (h d)"), a[:, 0, QW + KVW:]).then_inc(a_kv, 16)
                        sp.wait_ge(a_kv, 32)

                    @block.scalar
                    def _(act):
                        for t in range(NT):
                            if t >= 2:
                                act.wait_ge(a_ms, t - 1)
                            S.activation(sq[:, t % 2, :], a[:, t, 0:NQK * ADH], ACT.Square).then_inc(a_sq, 1)
                        act.wait_ge(a_ms, NT + 1)
                        S.activation(ms[:, :, :], ms[:, :, :], ACT.Sqrt).then_inc(a_rt, 1)
                        for t in range(NT):
                            act.wait_ge(a_trq, t + 1)
                            S.activation(qT[:, :, t * P:(t + 1) * P], v4(pb[t % 2][:, :]), ACT.Copy).then_inc(a_evq, 1)

                    @block.vector
                    def _(dve):
                        link = chain("dve", dve)
                        for t in range(NT):
                            dve.wait_ge(a_sq, t + 1)
                            V.tensor_reduce(ms[:, t, :], sq[:, t % 2, :].rearrange("p (h e) -> p h e", h=NQK), AX.X, ALU.add).then_inc(a_ms, 1)
                        dve.wait_ge(a_ms, NT)
                        V.tensor_scalar(ms[:, :, :], ms[:, :, :], 1.0 / ADH, EPS, ALU.mult, ALU.add).then_inc(a_ms, 1)
                        dve.wait_ge(a_rt, 1)
                        link(V.reciprocal(ms[:, :, :], ms[:, :, :]))
                        dve.wait_ge(a_small, 96)
                        for t in range(NT):
                            X = a[:, t, 0:NQK * ADH].rearrange("p (h e) -> p h e", h=NQK)
                            link(V.tensor_tensor(X, X, ms[:, t, :, None].to_broadcast([P, NQK, ADH]), ALU.mult))
                            V.tensor_tensor(X[:, 0:AH, :], X[:, 0:AH, :], gq[:, None, :].to_broadcast([P, AH, ADH]), ALU.mult)
                            V.tensor_tensor(X[:, AH:, :], X[:, AH:, :], gk[:, None, :].to_broadcast([P, AKV, ADH]), ALU.mult).then_inc(a_nrm, 1)
                            dve.wait_ge(a_nrm, t + 1)
                            if t > 0:
                                X4 = X.rearrange("p h (f j e) -> p h f j e", f=2, j=2)
                                Y4 = sq[:, t % 2, :].rearrange("p (h f j e) -> p h f j e", h=NQK, f=2, j=2)
                                sn = rot[:, 1, t - 1, :].rearrange("p (f j e) -> p f j e", f=2, j=2)
                                for j in range(2):
                                    link(V.tensor_tensor(Y4[:, :, :, j, :], X4[:, :, :, 1 - j, :],
                                                         sn[:, None, :, j, :].to_broadcast([P, NQK, 2, 16]), ALU.mult))
                                link(V.tensor_tensor(X, X, rot[:, 0, t - 1, None, :].to_broadcast([P, NQK, ADH]), ALU.mult))
                                V.tensor_tensor(a[:, t, 0:NQK * ADH], a[:, t, 0:NQK * ADH], sq[:, t % 2, :], ALU.add).then_inc(a_rp, 1)
                        for t in range(NT + 1):
                            dve.wait_ge(a_trk, t + 1)
                            V.tensor_copy(kT[:, :, t * P:(t + 1) * P], pb[2 + t % 2][:, 0:2 * P].rearrange("p (g s) -> p g s", g=AKV)).then_inc(a_evk, 1)

                    @block.gpsimd
                    def _(pool):
                        pool.wait_ge(a_ctx, 32)
                        for t in [NT] + list(range(NT)):
                            if t == 0:
                                pool.wait_ge(a_nrm, 1)
                            elif t < NT:
                                pool.wait_ge(a_rp, t)
                            src = (kc[:, 0, :] if t == NT else a[:, t, QW:QW + KVW]).rearrange("p (g e) -> p g e", g=AKV)
                            for j in range(2):
                                last = G.tensor_copy(kd[:, t, :, j, :], src)
                            last.then_inc(a_dup, 1)

                    @block.tensor
                    def _(pe):
                        for t in range(NT + 1):
                            pe.wait_ge(a_dup, NT + 1 if t == NT else t + 2)
                            if t < NT:
                                if t >= 2:
                                    pe.wait_ge(a_evq, t - 1)
                                for j in range(4):
                                    last = tr(pb[t % 2][:, j * P:(j + 1) * P], a[:, t, j * P:(j + 1) * P], ident)
                                last.then_inc(a_trq, 1)
                            if t >= 2:
                                pe.wait_ge(a_evk, t - 1)
                            for g in range(AKV):
                                last = tr(pb[2 + t % 2][:, g * P:(g + 1) * P], kd[:, t, g, :, :].rearrange("p j e -> p (j e)"), ident)
                            last.then_inc(a_trk, 1)

                with ExitStack() as sc_:
                    sc = sb(sc_, "a_sc", [P, 2, AH, 512])
                    pT = sb(sc_, "a_pT", [P, 2, 512])
                    Oa = sb(sc_, "a_O", [P, 2, 512])
                    mx = sb(sc_, "a_mx", [P, 2, 4, AH])
                    lo = (0, 1, 1, 2, 3)
                    hi = (0, 2, 3, 4, 4)
                    nloc = [(hi[t] - lo[t] + 1) * P for t in range(NT)]
                    nk = [nloc[t] + (P if t else 0) for t in range(NT)]
                    mask_at = (None, P, 0, 0, 512)
                    with nc.Block() as block:
                        @block.tensor
                        def _(pe):
                            def scores(t):
                                for h in range(AH):
                                    i = 8 * t + h
                                    if i >= 4:
                                        pe.wait_ge(a_msk, i - 3)
                                    r = slice(64 * (h % 2), 64 * (h % 2) + 64)
                                    q = qT[r, h // 2, t * P:(t + 1) * P]
                                    last = mm(pb[i % 4][:, 0:nloc[t]], q, kT[r, h // 4, lo[t] * P:(hi[t] + 1) * P], start=True, stop=True)
                                    if t:
                                        last = mm(pb[i % 4][:, nloc[t]:nk[t]], q, kT[r, h // 4, TOK:TOK + P], start=True, stop=True)
                                    last.then_inc(a_sc, 1)

                            def pv(t, h):
                                i = 8 * t + h
                                pe.wait_ge(a_pe, i + 1)
                                if h == 0 and t:
                                    pe.wait_ge(a_o, t)
                                n = nk[t] // P
                                for j in range(n):
                                    kt_ = lo[t] + j
                                    vv = kc[:, 1, :] if t and j == n - 1 else a[:, kt_, QW + KVW:]
                                    g = h // 4
                                    last = mm(pb[6][:, h * ADH:(h + 1) * ADH], pT[:, h % 2, j * P:(j + 1) * P], vv[:, g * ADH:(g + 1) * ADH],
                                              start=(j == 0), stop=(j == n - 1))
                                last.then_inc(a_pv, 1)

                            def o_transpose(t):
                                pe.wait_ge(a_o, t + 1)
                                if t:
                                    pe.wait_ge(a_oe, t)
                                for j in range(4):
                                    last = tr(pb[7][:, j * P:(j + 1) * P], Oa[:, t % 2, j * P:(j + 1) * P], ident)
                                last.then_inc(a_ot, 1)

                            scores(0)
                            for t in range(NT):
                                if t + 1 < NT:
                                    scores(t + 1)
                                if t:
                                    o_transpose(t - 1)
                                for h in range(AH):
                                    i = 8 * t + h
                                    pe.wait_ge(a_ex, i + 1)
                                    if i >= 2:
                                        pe.wait_ge(a_pe, i - 1)
                                    for j in range(nk[t] // P):
                                        last = tr(pb[4 + h % 2][:, j * P:(j + 1) * P], sc[:, t % 2, h, j * P:(j + 1) * P], ident)
                                    last.then_inc(a_pt, 1)
                                    if h:
                                        pv(t, h - 1)
                                pv(t, AH - 1)
                            o_transpose(NT - 1)

                        @block.vector
                        def _(dve):
                            link = chain("dve", dve)

                            def mask(t):
                                b = t % 2
                                if t >= 2:
                                    dve.wait_ge(a_pt, 8 * (t - 1))
                                for h in range(AH):
                                    i = 8 * t + h
                                    dve.wait_ge(a_sc, i + 1)
                                    if t:
                                        V.scalar_tensor_tensor(out=sc[:, b, h, 0:nk[t]], in0=pb[i % 4][:, 0:nk[t]], scalar=A_SCALE,
                                                               in1=amask[:, mask_at[t]:mask_at[t] + nk[t]], op0=ALU.mult, op1=ALU.add).then_inc(a_msk, 1)
                                    else:
                                        V.tensor_scalar(sc[:, b, h, 0:nk[t]], pb[i % 4][:, 0:nk[t]], A_SCALE, None, ALU.mult).then_inc(a_msk, 1)
                                dve.wait_ge(a_msk, 8 * t + 8)
                                link(V.tensor_reduce(mx[:, b, 0, :], sc[:, b, :, 0:nk[t]], AX.X, ALU.max))
                                link(V.tensor_tensor(mx[:, b, 0, :], mx[:, b, 0, :], sink[:, :], ALU.max))
                                V.tensor_tensor(mx[:, b, 1, :], sink[:, :], mx[:, b, 0, :], ALU.subtract).then_inc(a_df, 1)
                                dve.wait_ge(a_df, t + 1)
                                V.tensor_scalar(mx[:, b, 0, :], mx[:, b, 0, :], -1.0, None, ALU.mult).then_inc(a_nm, 1)

                            def o_evac(t):
                                dve.wait_ge(a_ot, t + 1)
                                V.tensor_copy(yT[:, 2, :, t * P:(t + 1) * P], v4(pb[7][:, :])).then_inc(a_oe, 1)

                            mask(0)
                            for t in range(NT):
                                b = t % 2
                                if t + 1 < NT:
                                    mask(t + 1)
                                if t:
                                    o_evac(t - 1)
                                dve.wait_ge(a_es, t + 1)
                                link(V.tensor_tensor(mx[:, b, 3, :], mx[:, b, 2, :], mx[:, b, 1, :], ALU.add))
                                link(V.reciprocal(mx[:, b, 3, :], mx[:, b, 3, :]))
                                dve.wait_ge(a_pv, 8 * t + 8)
                                V.tensor_tensor(Oa[:, b, :].rearrange("p (h e) -> p h e", h=AH), pb[6][:, :].rearrange("p (h e) -> p h e", h=AH),
                                                mx[:, b, 3, :, None].to_broadcast([P, AH, ADH]), ALU.mult).then_inc(a_o, 1)
                            o_evac(NT - 1)

                        @block.scalar
                        def _(act):
                            for t in range(NT):
                                b = t % 2
                                act.wait_ge(a_nm, t + 1)
                                for h in range(AH):
                                    S.activation(sc[:, b, h, 0:nk[t]], sc[:, b, h, 0:nk[t]], ACT.Exp, bias=mx[:, b, 0, h:h + 1],
                                                 accum_out=mx[:, b, 2, h:h + 1]).then_inc(a_ex, 1)
                                act.wait_ge(a_ex, 8 * t + 8)
                                S.activation(mx[:, b, 1, :], mx[:, b, 1, :], ACT.Exp).then_inc(a_es, 1)
                                for h in range(AH):
                                    i = 8 * t + h
                                    act.wait_ge(a_pt, i + 1)
                                    if i >= 2:
                                        act.wait_ge(a_pv, i - 1)
                                    S.activation(pT[:, h % 2, 0:nk[t]], pb[4 + h % 2][:, 0:nk[t]], ACT.Copy).then_inc(a_pe, 1)

        NLEV = 7
        CH = 12
        TPAD = TOK + 6
        TCONV = TOK + 2

        def stage_deltanet(l):
            (g_cw, g_cwt, g_cwe, g_pad, g_eps, g_cv, g_si, g_sq, g_ss, g_sr, g_nr, g_ktr, g_kte, g_bai) = [sem("g_" + n) for n in (
                "conv_w_in", "conv_w_transposed", "conv_w_evac", "pads_zeroed", "eps_set", "conv", "silu", "squared", "square_sum", "root",
                "normed", "kv_transposed", "kv_evac", "beta_decay")]
            (g_st_in, g_zero, g_D, g_KK, g_dm, g_E, g_QE, g_ket, g_A, g_at, g_atc, g_T, g_atm, g_X, g_Xc, g_Y, g_kb, g_W, g_Wc, g_vn, g_vnc,
             g_in, g_inc, g_it, g_O, g_up, g_S, g_out) = [sem("g_" + n) for n in (
                "state_in", "zeroed", "D", "KK_QK", "masked", "E", "E_products", "KE_transposed", "A", "A_transposed", "At_copied", "T",
                "At_level", "X", "X_copied", "Y", "kvw", "W", "W_copied", "vn", "vn_copied", "inter", "inter_scaled", "intra", "O", "update",
                "S", "state_out")]
            with ExitStack() as st:
                qkv = sb(st, "g_qkv", [P, CH, TPAD])
                kt = sb(st, "g_k", [P, NT, 512])
                vt = sb(st, "g_v", [P, NT, 512])
                jobs = []
                for n in range(3):
                    for c in range(4):
                        for o, w, at in ((0, P, 2), (P, TOK - P, P + 4)):
                            jobs.append((n, "cols", c, (o, w), qkv[:, 4 * n + c, at:at + w], 1.0))
                with ExitStack() as wst:
                    Wb = [sb(wst, f"g_W{i}", [P, KD, 512]) for i in range(W_BUFS)]
                    project("gproj", [(A["w_in"], O_GQKV + 512 * n, 512) for n in range(3)], jobs)(l, Wb)
                with ExitStack() as cst:
                    cwr = sb(cst, "g_cwr", [5, CH * P])
                    cw = sb(cst, "g_cw", [P, CH, 5])
                    cv = sb(cst, "g_cv", [P, 3, TCONV])
                    sq = sb(cst, "g_sq", [P, 2, TOK])
                    root = sb(cst, "g_root", [P, 2, TOK])
                    eps = sb(cst, "g_eps", [P, 2])
                    with nc.Block() as block:
                        @block.sync
                        def _(sp):
                            sp.dma_start(cwr[:, :], A["g_conv_w"][l, :, :]).then_inc(g_cw, 16)

                        @block.gpsimd
                        def _(pool):
                            for o, n in ((0, 2), (P + 2, 2), (TPAD - 2, 2)):
                                last = G.memset(qkv[:, :, o:o + n], 0.0)
                            last.then_inc(g_pad, 1)
                            G.memset(eps[:, 0:1], DH * EPS)
                            G.memset(eps[:, 1:2], EPS).then_inc(g_eps, 1)

                        @block.vector
                        def _(dve):
                            link = chain("dve", dve)
                            dve.wait_ge(g_cwt, 1)
                            V.tensor_copy(cw[:, :, :].rearrange("p c k -> p (c k)"), pb[6][:, 0:5 * CH]).then_inc(g_cwe, 1)
                            dve.wait_ge(g_cwe, 1)
                            dve.wait_ge(g_pad, 1)
                            for c in range(CH):
                                if c >= 3:
                                    dve.wait_ge(g_si, c - 2)
                                y = cv[:, c % 3, :]
                                link(V.tensor_scalar(y, qkv[:, c, 0:TCONV], cw[:, c, 0:1], None, ALU.mult))
                                for j in range(1, 4):
                                    link(V.scalar_tensor_tensor(out=y, in0=qkv[:, c, j:j + TCONV], scalar=cw[:, c, j:j + 1], in1=y,
                                                                op0=ALU.mult, op1=ALU.add))
                                V.scalar_tensor_tensor(out=y, in0=qkv[:, c, 4:4 + TCONV], scalar=cw[:, c, 4:5], in1=y,
                                                       op0=ALU.mult, op1=ALU.add).then_inc(g_cv, 1)
                            for c in range(8):
                                dve.wait_ge(g_sr, c + 1)
                                link(V.reciprocal(root[:, c % 2, :], root[:, c % 2, :]))
                                V.tensor_tensor(qkv[:, c, 0:TOK], qkv[:, c, 0:TOK], root[:, c % 2, :], ALU.mult).then_inc(g_nr, 1)
                            for i in range(2 * NT):
                                dve.wait_ge(g_ktr, i + 1)
                                dst = (vt, kt)[i // NT]
                                V.tensor_copy(dst[:, i % NT, :], pb[4 + i % 2][:, :]).then_inc(g_kte, 1)

                        @block.scalar
                        def _(act):
                            for c in range(CH):
                                act.wait_ge(g_cv, c + 1)
                                S.activation(qkv[:, c, 0:P], cv[:, c % 3, 0:P], ACT.Silu)
                                S.activation(qkv[:, c, P:TOK], cv[:, c % 3, P + 2:TCONV], ACT.Silu).then_inc(g_si, 1)
                            act.wait_ge(g_si, CH)
                            act.wait_ge(g_eps, 1)
                            for c in range(9):
                                if c < 8:
                                    if c >= 2:
                                        act.wait_ge(g_ss, c - 1)
                                    S.activation(sq[:, c % 2, :], qkv[:, c, 0:TOK], ACT.Square).then_inc(g_sq, 1)
                                if c:
                                    e = c - 1
                                    act.wait_ge(g_ss, c)
                                    if e >= 2:
                                        act.wait_ge(g_nr, e - 1)
                                    kw_ = dict(scale=float(DH) if e < 4 else 1.0, bias=eps[:, 0:1] if e < 4 else eps[:, 1:2])
                                    S.activation(root[:, e % 2, 0:P], pb[2 * (e % 2)][:, 0:P], ACT.Sqrt, **kw_)
                                    S.activation(root[:, e % 2, P:TOK], pb[2 * (e % 2) + 1][:, :], ACT.Sqrt, **kw_).then_inc(g_sr, 1)

                        @block.tensor
                        def _(pe):
                            pe.wait_ge(g_cw, 16)
                            for c in range(CH):
                                last = tr(pb[6][:, 5 * c:5 * c + 5], cwr[:, c * P:(c + 1) * P], ident[0:5, 0:5])
                            last.then_inc(g_cwt, 1)
                            for c in range(8):
                                pe.wait_ge(g_sq, c + 1)
                                if c >= 2:
                                    pe.wait_ge(g_sr, c - 1)
                                mm(pb[2 * (c % 2)][:, 0:P], ones, sq[:, c % 2, 0:P], start=True, stop=True)
                                mm(pb[2 * (c % 2) + 1][:, :], ones, sq[:, c % 2, P:TOK], start=True, stop=True).then_inc(g_ss, 1)
                            for i in range(2 * NT):
                                t, o = i % NT, (8, 4)[i // NT]
                                if i == NT:
                                    pe.wait_ge(g_nr, 8)
                                if i >= 2:
                                    pe.wait_ge(g_kte, i - 1)
                                for h in range(4):
                                    last = tr(pb[4 + i % 2][:, h * P:(h + 1) * P], qkv[:, o + h, t * P:(t + 1) * P], ident)
                                last.then_inc(g_ktr, 1)

                O = sb(st, "g_O", [P, NT, 512])
                qT = lambda h, c: qkv[:, h, c * P:(c + 1) * P]
                kT = lambda h, c: qkv[:, 4 + h, c * P:(c + 1) * P]
                sl = lambda c: slice(c * P, (c + 1) * P)
                tile = lambda d, p: (FT, BT)[d][p]
                both = (0, 1)
                with ExitStack() as sc:
                    buf = lambda n: [sb(sc, f"g_{n}{d}", [P, 512]) for d in both]
                    EX, AM, AtW, Tv, Tt, QE, kb, vb, kd, it = [buf(n) for n in ("EX", "AM", "AtW", "Tv", "Tt", "QE", "kb", "vb", "kd", "it")]
                    St = [[sb(sc, f"g_S{g}{d}", [P, 512]) for d in both] for g in both]
                    bai = sb(sc, "g_bai", [P, NT, 16])
                    bk = [[pb[4 * d + i] for i in range(4)] for d in both]
                    bc = lambda a: a[:, None, :].to_broadcast([P, 4, P])
                    lvl = lambda d, j: bc((levT if d else lev)[:, j, :])
                    lvlT = lambda d, j: bc((lev if d else levT)[:, j, :])
                    with nc.Block() as block:
                        @block.sync
                        def _(sp):
                            for d in both:
                                sp.dma_start(v4(St[1][d][:, :]), A["state_gdn_S"][0, l, d, :, :, :].rearrange("h d e -> d h e")).then_inc(g_st_in, 16)
                            sp.wait_ge(g_S, 2)
                            for d in both:
                                sp.dma_start(new_S[0, l, d, :, :, :].rearrange("h d e -> d h e"), v4(St[0][d][:, :])).then_inc(g_out, 16)
                            sp.wait_ge(g_out, 32)

                        @block.gpsimd
                        def _(pool):
                            for d in both:
                                G.memset(St[0][d][:, :], 0.0)
                            G.memset(O[:, :, :], 0.0).then_inc(g_zero, 1)
                            G.tensor_tensor(bai[:, :, :], cols[:, :, 0, :], cols[:, :, 3, :], ALU.mult).then_inc(g_bai, 1)
                            pool.wait_ge(g_bai, 1)
                            for p in range(NT):
                                for d in both:
                                    u, c, r = 2 * p + d, tile(d, p), 8 * d + 4
                                    if u >= 2:
                                        pool.wait_ge(g_up, u - 1)
                                    k3, v3 = v4(kt[:, c, :]), v4(vt[:, c, :])
                                    w = lambda a: a[:, :, None].to_broadcast([P, 4, DH])
                                    G.tensor_tensor(v4(kb[d][:, :]), k3, bai[:, c, r:r + 4, None].to_broadcast([P, 4, DH]), ALU.mult)
                                    G.tensor_tensor(v4(vb[d][:, :]), v3, cols[:, c, 3, r:r + 4, None].to_broadcast([P, 4, DH]), ALU.mult)
                                    G.tensor_tensor(v4(kd[d][:, :]), k3, cols[:, c, 1, r:r + 4, None].to_broadcast([P, 4, DH]), ALU.mult).then_inc(g_kb, 1)
                                for j in range(1, NLEV):
                                    for d in both:
                                        u = 2 * p + d
                                        if j == 1:
                                            pool.wait_ge(g_T, 14 * p + d + 1)
                                            pool.wait_ge(g_atc, u + 1)
                                        else:
                                            pool.wait_ge(g_X, 12 * p + 2 * (j - 2) + d + 1)
                                        G.tensor_tensor(v4(AM[d][:, :]), v4(AtW[d][:, :]), lvlT(d, j), ALU.mult).then_inc(g_atm, 1)

                        @block.tensor
                        def _(pe):
                            pe.wait_ge(g_zero, 1)
                            for p in range(NT):
                                for d in both:
                                    u, c = 2 * p + d, tile(d, p)
                                    r = slice(64 * d + 32, 64 * d + 64)
                                    B = bk[d]
                                    if u >= 2:
                                        pe.wait_ge(g_inc, u - 1)
                                    mm(B[0][:, :], betar[r, sl(c)], sel[r, :, :].rearrange("p h s -> p (h s)"), start=True, stop=False)
                                    for h in range(4):
                                        last = mm(B[0][:, sl(h)], sel[r, h, :], alpha[r, sl(c)], start=False, stop=(h == 3))
                                    last.then_inc(g_D, 1)
                                    if u >= 2:
                                        pe.wait_ge(g_S, u - 1)
                                        pe.wait_ge(g_vnc, u - 1)
                                    for h in range(4):
                                        mm(B[1][:, sl(h)], kT(h, c), kT(h, c), start=True, stop=True)
                                        last = mm(B[2][:, sl(h)], kT(h, c), qT(h, c), start=True, stop=True)
                                    last.then_inc(g_KK, 1)
                                for d in both:
                                    u, B = 2 * p + d, bk[d]
                                    pe.wait_ge(g_QE, u + 1)
                                    if u >= 2:
                                        pe.wait_ge(g_O, u - 1)
                                    for h in range(4):
                                        last = tr(B[3][:, sl(h)], Tv[d][:, sl(h)], ident)
                                    last.then_inc(g_ket, 1)
                                for d in both:
                                    u, B = 2 * p + d, bk[d]
                                    pe.wait_ge(g_A, u + 1)
                                    for h in range(4):
                                        last = tr(B[0][:, sl(h)], AM[d][:, sl(h)], ident)
                                    last.then_inc(g_at, 1)
                                for j in range(1, NLEV):
                                    for d in both:
                                        B = bk[d]
                                        n = 12 * p + 2 * (j - 1) + d
                                        pe.wait_ge(g_atm, n + 1)
                                        pe.wait_ge(g_T, 14 * p + 2 * (j - 1) + d + 1)
                                        for h in range(4):
                                            last = mm(B[1][:, sl(h)], AM[d][:, sl(h)], Tv[d][:, sl(h)], start=True, stop=True)
                                        last.then_inc(g_X, 1)
                                    for d in both:
                                        B = bk[d]
                                        n = 12 * p + 2 * (j - 1) + d
                                        pe.wait_ge(g_Xc, n + 1)
                                        for h in range(4):
                                            if j < NLEV - 1:
                                                mm(B[2][:, sl(h)], Tt[d][:, sl(h)], EX[d][:, sl(h)], start=True, stop=True)
                                            last = mm(B[3][:, sl(h)], EX[d][:, sl(h)], Tt[d][:, sl(h)], start=True, stop=True)
                                        last.then_inc(g_Y, 1)
                                for d in both:
                                    u, B = 2 * p + d, bk[d]
                                    pe.wait_ge(g_T, 14 * p + 2 * (NLEV - 1) + d + 1)
                                    pe.wait_ge(g_kb, u + 1)
                                    for h in range(4):
                                        last = mm(B[1][:, sl(h)], kb[d][:, sl(h)], Tt[d][:, sl(h)], start=True, stop=True)
                                    last.then_inc(g_W, 1)
                                if p == 1:
                                    pe.wait_ge(g_st_in, 32)
                                for d in both:
                                    u, c, B = 2 * p + d, tile(d, p), bk[d]
                                    Sd = St[min(p, 1)][d]
                                    for h in range(4):
                                        last = mm(B[0][:, sl(h)], qT(h, c), Sd[:, sl(h)], start=True, stop=True)
                                    last.then_inc(g_in, 1)
                                    pe.wait_ge(g_Wc, u + 1)
                                    for h in range(4):
                                        mm(B[2][:, sl(h)], Tt[d][:, sl(h)], vb[d][:, sl(h)], start=True, stop=False)
                                        last = mm(B[2][:, sl(h)], AtW[d][:, sl(h)], Sd[:, sl(h)], start=False, stop=True)
                                    last.then_inc(g_vn, 1)
                                for d in both:
                                    u, B = 2 * p + d, bk[d]
                                    pe.wait_ge(g_vnc, u + 1)
                                    for h in range(4):
                                        last = mm(B[3][:, sl(h)], QE[d][:, sl(h)], Tv[d][:, sl(h)], start=True, stop=True)
                                    last.then_inc(g_it, 1)
                                    for h in range(4):
                                        last = mm(B[1][:, sl(h)], kd[d][:, sl(h)], Tv[d][:, sl(h)], start=True, stop=True)
                                    last.then_inc(g_up, 1)

                        @block.scalar
                        def _(act):
                            for p in range(NT):
                                for d in both:
                                    act.wait_ge(g_dm, 2 * p + d + 1)
                                    S.activation(EX[d][:, :], EX[d][:, :], ACT.Exp).then_inc(g_E, 1)
                                for d in both:
                                    act.wait_ge(g_at, 2 * p + d + 1)
                                    S.activation(AtW[d][:, :], bk[d][0][:, :], ACT.Copy).then_inc(g_atc, 1)
                                for j in range(1, NLEV):
                                    for d in both:
                                        act.wait_ge(g_X, 12 * p + 2 * (j - 1) + d + 1)
                                        S.activation(EX[d][:, :], bk[d][1][:, :], ACT.Copy).then_inc(g_Xc, 1)
                                for d in both:
                                    u, c, B = 2 * p + d, tile(d, p), bk[d]
                                    act.wait_ge(g_W, u + 1)
                                    S.activation(AtW[d][:, :], B[1][:, :], ACT.Copy, scale=-1.0).then_inc(g_Wc, 1)
                                for d in both:
                                    u, c, B = 2 * p + d, tile(d, p), bk[d]
                                    act.wait_ge(g_in, u + 1)
                                    if u >= 2:
                                        act.wait_ge(g_O, u - 1)
                                    for h in range(4):
                                        last = S.activation(it[d][:, sl(h)], B[0][:, sl(h)], ACT.Copy, scale=cols[:, c, 0, 8 * d + 4 + h:8 * d + 5 + h])
                                    last.then_inc(g_inc, 1)

                        @block.vector
                        def _(dve):
                            link = chain("dve", dve)
                            for p in range(NT):
                                for d in both:
                                    dve.wait_ge(g_D, 2 * p + d + 1)
                                    V.tensor_tensor(v4(EX[d][:, :]), v4(bk[d][0][:, :]), bc(K("maskB" if d else "maskF")), ALU.min).then_inc(g_dm, 1)
                                for d in both:
                                    u, B = 2 * p + d, bk[d]
                                    dve.wait_ge(g_E, u + 1)
                                    dve.wait_ge(g_KK, u + 1)
                                    V.tensor_tensor(QE[d][:, :], EX[d][:, :], B[2][:, :], ALU.mult)
                                    V.tensor_tensor(Tv[d][:, :], EX[d][:, :], B[1][:, :], ALU.mult).then_inc(g_QE, 1)
                                for d in both:
                                    u, c, B = 2 * p + d, tile(d, p), bk[d]
                                    dve.wait_ge(g_ket, u + 1)
                                    for h in range(4):
                                        last = V.scalar_tensor_tensor(out=AM[d][:, sl(h)], in0=B[3][:, sl(h)], scalar=cols[:, c, 3, 8 * d + 4 + h:8 * d + 5 + h],
                                                                      in1=K("strictF" if d else "strictB"), op0=ALU.mult, op1=ALU.mult)
                                    last.then_inc(g_A, 1)
                                for d in both:
                                    u = 2 * p + d
                                    dve.wait_ge(g_A, u + 1)
                                    link(V.tensor_tensor(v4(Tv[d][:, :]), v4(AM[d][:, :]), lvl(d, 0), ALU.mult))
                                    link(V.tensor_tensor(v4(Tv[d][:, :]), bc(ident), v4(Tv[d][:, :]), ALU.subtract))
                                    dve.wait_ge(g_atc, u + 1)
                                    link(V.tensor_tensor(v4(Tt[d][:, :]), v4(AtW[d][:, :]), lvlT(d, 0), ALU.mult))
                                    V.tensor_tensor(v4(Tt[d][:, :]), bc(ident), v4(Tt[d][:, :]), ALU.subtract).then_inc(g_T, 1)
                                for j in range(1, NLEV):
                                    for d in both:
                                        B = bk[d]
                                        dve.wait_ge(g_Y, 12 * p + 2 * (j - 1) + d + 1)
                                        if j < NLEV - 1:
                                            V.tensor_tensor(Tv[d][:, :], Tv[d][:, :], B[2][:, :], ALU.subtract)
                                        V.tensor_tensor(Tt[d][:, :], Tt[d][:, :], B[3][:, :], ALU.subtract).then_inc(g_T, 1)
                                for d in both:
                                    u, B = 2 * p + d, bk[d]
                                    dve.wait_ge(g_vn, u + 1)
                                    V.tensor_copy(Tv[d][:, :], B[2][:, :]).then_inc(g_vnc, 1)
                                for d in both:
                                    u, c, B = 2 * p + d, tile(d, p), bk[d]
                                    dve.wait_ge(g_it, u + 1)
                                    dve.wait_ge(g_inc, u + 1)
                                    link(V.tensor_tensor(it[d][:, :], it[d][:, :], B[3][:, :], ALU.add))
                                    if p == 0 and d == 0:
                                        dve.wait_ge(g_zero, 1)
                                    V.tensor_tensor(O[:, c, :], O[:, c, :], it[d][:, :], ALU.add).then_inc(g_O, 1)
                                    dve.wait_ge(g_up, u + 1)
                                    Sd = St[min(p, 1)][d]
                                    for h in range(4):
                                        last = V.scalar_tensor_tensor(out=Sd[:, sl(h)], in0=Sd[:, sl(h)], scalar=decbc[:, c, 8 * d + 4 + h:8 * d + 5 + h],
                                                                      in1=B[1][:, sl(h)], op0=ALU.mult, op1=ALU.add)
                                    last.then_inc(g_S, 1)
                with ExitStack() as fst:
                    gz = sb(fst, "g_z", [P, NT, 512])
                    with ExitStack() as wst:
                        Wb = [sb(wst, f"gz_W{i}", [P, KD, 512]) for i in range(1)]
                        project("gz", [(A["w_in"], O_GZ, 512)], [(0, "rows", t, 512, gz[:, t, :], ACT.Silu) for t in range(NT)])(l, Wb)
                    finish_mixer(1, l, O, gz, A["g_norm_g"], DH)

        def stage_merge(l):
            e_w, e_wb = [[sem(f"e_{n}{i}") for i in range(2)] for n in ("gate_w_in", "branch_w_in")]
            (e_wo, e_gt, e_g, e_b, e_sg, e_pr, e_ad, e_tr, e_evA, e_evV, e_o, e_om, e_x) = [sem("e_" + n) for n in (
                "w_out_in", "gt_in", "gate_product", "branch_product", "sigmoid", "gated", "added", "transposed", "evac_act", "evac_dve",
                "out_product", "out_gated", "x_updated")]
            BR = (A["w_br_m"], A["w_br_g"], A["w_br_a"])
            with ExitStack() as st:
                mg = sb(st, "mg", [P, NT, DM])
                mT = sb(st, "mT", [P, KD, TOK])
                Wg = [sb(st, f"e_Wg{i}", [P, KD, 512]) for i in range(2)]
                Wr = [sb(st, f"e_Wr{i}", [P, 4, 512]) for i in range(2)]
                gt = sb(st, "e_gt", [P, 2, DM])
                sg = sb(st, "e_sg", [P, 4, 512])
                half = lambda j: slice(512 * j, 512 * j + 512)
                with nc.Block() as block:
                    @block.sync
                    def _(sp):
                        for n in range(6):
                            b, hf = n // 2, n % 2
                            if n >= 2:
                                sp.wait_ge(e_g, NT * (n - 1))
                                sp.wait_ge(e_b, NT * (n - 1))
                            sp.dma_start(Wg[n % 2][:, :, :], dram_cols(A["w_in"], l, O_GATE + 512 * n, 512)).then_inc(e_w[n % 2], 16)
                            sp.dma_start(Wr[n % 2][:, :, :], BR[b][l, :, half(hf)].rearrange("(k p) n -> p k n", p=P)).then_inc(e_wb[n % 2], 16)
                        for g in range(2):
                            sp.dma_start(gt[:, g, :], modd[g:g + 1, 2 * DM:3 * DM].to_broadcast([P, DM])).then_inc(e_gt, 16)
                        sp.wait_ge(e_g, NT * 6)
                        for hf in range(2):
                            sp.dma_start(Wg[hf][:, :, :], dram_cols(A["w_out"], l, 512 * hf, 512)).then_inc(e_wo, 16)

                    @block.tensor
                    def _(pe):
                        for n in range(6):
                            b = n // 2
                            pe.wait_ge(e_w[n % 2], 16 * (n // 2 + 1))
                            pe.wait_ge(e_wb[n % 2], 16 * (n // 2 + 1))
                            for t in range(NT):
                                i = NT * n + t
                                ts = slice(t * P, (t + 1) * P)
                                if i >= 2:
                                    pe.wait_ge(e_sg, i - 1)
                                for k in range(KD):
                                    last = mm(pb[2 * (i % 2)][:, :], hT[:, k, ts], Wg[n % 2][:, k, :], start=(k == 0), stop=(k == KD - 1))
                                last.then_inc(e_g, 1)
                                if i >= 2:
                                    pe.wait_ge(e_pr, i - 1)
                                for k in range(4):
                                    last = mm(pb[2 * (i % 2) + 1][:, :], yT[:, b, k, ts], Wr[n % 2][:, k, :], start=(k == 0), stop=(k == 3))
                                last.then_inc(e_b, 1)
                        for t in range(NT):
                            pe.wait_ge(e_ad, 5 * NT + t + 1)
                            if t >= 2:
                                pe.wait_ge(e_evA, t - 1)
                                pe.wait_ge(e_evV, t - 1)
                            for j in range(2):
                                for k in range(4):
                                    last = tr(pb[4 + 2 * (t % 2) + j][:, k * P:(k + 1) * P], mg[:, t, (4 * j + k) * P:(4 * j + k + 1) * P], ident)
                                last.then_inc(e_tr, 1)
                        pe.wait_ge(e_wo, 32)
                        pe.wait_ge(e_pr, 6 * NT)
                        pe.wait_ge(e_evA, NT)
                        pe.wait_ge(e_evV, NT)
                        for hf in range(2):
                            for t in range(NT):
                                i = NT * hf + t
                                if i >= 2:
                                    pe.wait_ge(e_om, i - 1)
                                for k in range(KD):
                                    last = mm(pb[i % 2][:, :], mT[:, k, t * P:(t + 1) * P], Wg[hf][:, k, :], start=(k == 0), stop=(k == KD - 1))
                                last.then_inc(e_o, 1)

                    @block.scalar
                    def _(act):
                        for i in range(6 * NT):
                            act.wait_ge(e_g, i + 1)
                            if i >= 4:
                                act.wait_ge(e_ad, i - 3)
                            S.activation(sg[:, i % 4, :], pb[2 * (i % 2)][:, :], ACT.Sigmoid).then_inc(e_sg, 1)
                        for t in range(NT):
                            act.wait_ge(e_tr, 2 * t + 1)
                            S.activation(mT[:, 0:4, t * P:(t + 1) * P], v4(pb[4 + 2 * (t % 2)][:, :]), ACT.Copy).then_inc(e_evA, 1)

                    @block.vector
                    def _(dve):
                        for i in range(6 * NT):
                            dve.wait_ge(e_sg, i + 1)
                            dve.wait_ge(e_b, i + 1)
                            V.tensor_tensor(sg[:, i % 4, :], sg[:, i % 4, :], pb[2 * (i % 2) + 1][:, :], ALU.mult).then_inc(e_pr, 1)
                        for t in range(NT):
                            dve.wait_ge(e_tr, 2 * t + 2)
                            V.tensor_copy(mT[:, 4:8, t * P:(t + 1) * P], v4(pb[4 + 2 * (t % 2) + 1][:, :])).then_inc(e_evV, 1)
                        dve.wait_ge(e_gt, 32)
                        for i in range(2 * NT):
                            hf, t = i // NT, i % NT
                            dve.wait_ge(e_o, i + 1)
                            if i >= 4:
                                dve.wait_ge(e_x, i - 3)
                            elif i == 0:
                                dve.wait_ge(e_ad, 6 * NT)
                            V.tensor_tensor(sg[:, i % 4, :], pb[i % 2][:, :], gt[:, min(t, 1), half(hf)], ALU.mult).then_inc(e_om, 1)

                    @block.gpsimd
                    def _(pool):
                        for i in range(6 * NT):
                            n, t = i // NT, i % NT
                            b, hf = n // 2, n % 2
                            dst = mg[:, t, half(hf)]
                            pool.wait_ge(e_pr, i + 1)
                            if b == 0:
                                G.tensor_copy(dst, sg[:, i % 4, :]).then_inc(e_ad, 1)
                            else:
                                if i >= 2 * NT:
                                    pool.wait_ge(e_ad, i - 2 * NT + 1)
                                G.tensor_tensor(dst, dst, sg[:, i % 4, :], ALU.add).then_inc(e_ad, 1)
                        for i in range(2 * NT):
                            hf, t = i // NT, i % NT
                            pool.wait_ge(e_om, i + 1)
                            G.tensor_tensor(x[:, t, half(hf)], x[:, t, half(hf)], sg[:, i % 4, :], ALU.add).then_inc(e_x, 1)

        NSC = 2 * PH

        def stage_scores(l, sc):
            p_w = [sem(f"p_w_in{i}") for i in range(3)]
            (p_k, p_kt, p_ke, p_q, p_qeA, p_qeV, p_s, p_seA, p_seV) = [sem("p_" + n) for n in (
                "keys_in", "keys_transposed", "keys_evac", "q", "q_evac_act", "q_evac_dve", "scores", "scores_evac_act", "scores_evac_dve")]
            with ExitStack() as st:
                W = [sb(st, f"p_W{i}", [P, KD, 512]) for i in range(3)]
                keys = sb(st, "p_keys", [P, NSC, P])
                kTs = sb(st, "p_kT", [P, NSC, P])
                q = sb(st, "p_q", [P, 2, TOK])
                with nc.Block() as block:
                    @block.sync
                    def _(sp):
                        for h in range(PH):
                            sp.dma_start(keys[:, 2 * h:2 * h + 2, :], A["p_keys"][l, h, :, :, :].rearrange("c k d -> k c d")).then_inc(p_k, 16)
                        for n in range(4):
                            if n >= 3:
                                sp.wait_ge(p_q, 8 * (n - 2))
                            sp.dma_start(W[n % 3][:, :, :], dram_cols(A["p_wq"], l, 512 * n, 512)).then_inc(p_w[n % 3], 16)

                    @block.tensor
                    def _(pe):
                        pe.wait_ge(p_k, 16 * PH)
                        for b in range(4):
                            for j in range(4):
                                last = tr(pb[b][:, j * P:(j + 1) * P], keys[:, 4 * b + j, :], ident)
                            last.then_inc(p_kt, 1)

                        def scores(i):
                            pe.wait_ge(p_qeA, i + 1)
                            pe.wait_ge(p_qeV, i + 1)
                            if i >= 2:
                                pe.wait_ge(p_seA, i - 1)
                                pe.wait_ge(p_seV, i - 1)
                            for t in range(NT):
                                bank = pb[4 + 2 * (i % 2)][:, t * P:(t + 1) * P] if t < 4 else pb[5 + 2 * (i % 2)][:, 0:P]
                                last = mm(bank, q[:, i % 2, t * P:(t + 1) * P], kTs[:, i, :], start=True, stop=True)
                            last.then_inc(p_s, 1)

                        for i in range(NSC):
                            n, c = i // 4, i % 4
                            if c == 0:
                                pe.wait_ge(p_w[n % 3], 16 * (n // 3 + 1))
                            if i == 0:
                                pe.wait_ge(p_ke, 4)
                            if i >= 2:
                                pe.wait_ge(p_qeA, i - 1)
                                pe.wait_ge(p_qeV, i - 1)
                            for j, (o, w) in enumerate(((0, P), (P, TOK - P))):
                                for k in range(KD):
                                    last = mm(pb[2 * (i % 2) + j][:, 0:w], W[n % 3][:, k, c * P:(c + 1) * P], hT[:, k, o:o + w],
                                              start=(k == 0), stop=(k == KD - 1))
                                last.then_inc(p_q, 1)
                            if i:
                                scores(i - 1)
                        scores(NSC - 1)

                    @block.scalar
                    def _(act):
                        for i in range(NSC + 1):
                            if i < NSC:
                                act.wait_ge(p_q, 2 * i + 2)
                                if i >= 2:
                                    act.wait_ge(p_s, i - 1)
                                S.activation(q[:, i % 2, P:TOK], pb[2 * (i % 2) + 1][:, :], ACT.Copy).then_inc(p_qeA, 1)
                            if i:
                                e = i - 1
                                act.wait_ge(p_s, i)
                                S.activation(sc[:, 0:4, e, :], v4(pb[4 + 2 * (e % 2)][:, :]), ACT.Copy).then_inc(p_seA, 1)

                    @block.vector
                    def _(dve):
                        for b in range(4):
                            dve.wait_ge(p_kt, b + 1)
                            V.tensor_copy(kTs[:, 4 * b:4 * b + 4, :], v4(pb[b][:, :])).then_inc(p_ke, 1)
                        for i in range(NSC + 1):
                            if i < NSC:
                                dve.wait_ge(p_q, 2 * i + 1)
                                if i >= 2:
                                    dve.wait_ge(p_s, i - 1)
                                V.tensor_copy(q[:, i % 2, 0:P], pb[2 * (i % 2)][:, 0:P]).then_inc(p_qeV, 1)
                            if i:
                                e = i - 1
                                dve.wait_ge(p_s, i)
                                V.tensor_copy(sc[:, 4, e, :], pb[5 + 2 * (e % 2)][:, 0:P]).then_inc(p_seV, 1)

        RING = 8
        NG = NT * PH

        def stage_experts(l, sc, h2):
            u_in = [sem(f"u_in{i}") for i in range(RING)]
            v_in = [sem(f"v_in{i}") for i in range(RING)]
            (x_gt, x_iota, x_idx, x_nm, x_ex, x_dot, x_gelu, x_coef, x_diag, x_vmm, x_add) = [sem("x_" + n) for n in (
                "gt_in", "iota_in", "indices", "neg_max", "exp", "dot", "gelu", "coef", "diag", "v_product", "x_updated")]
            table_u = A["p_u"].rearrange("l e d -> (l e) d")
            table_v = A["p_v"].rearrange("l e d -> (l e) d")
            with ExitStack() as st:
                ub = sb(st, "ub", [P, RING, DM])
                vb = sb(st, "vb", [P, RING, DM])
                junk = sb(st, "x_junk", [P, 2, DM])
                gt = sb(st, "x_gt2", [P, 2, DM])
                iota = sb(st, "x_iota", [P, PTOP])
                sv = sb(st, "x_sv", [P, 2, PTOP])
                si = sb(st, "x_si", [P, 2, PTOP], u32)
                sif = sb(st, "x_sif", [P, 2, PTOP])
                cand = sb(st, "x_cand", [P, PTOP, PTOP])
                fi = sb(st, "x_fi", [P, PTOP], u32)
                ab = sb(st, "x_ab", [P, 2, PTOP], u32)
                abf = sb(st, "x_abf", [P, 2, PTOP])
                eq = sb(st, "x_eq", [P, 2, PTOP, PTOP])
                e01 = sb(st, "x_e01", [P, 2, PTOP])
                ef = sb(st, "x_ef", [P, PTOP])
                fv = sb(st, "x_fv", [P, 4, PTOP])
                nm = sb(st, "x_nm", [P, 4, 3])
                idx = sb(st, "x_idx", [P, 4, PTOP], i32)
                dot = sb(st, "x_dots", [P, 4, PTOP])
                coef = sb(st, "x_coefs", [P, 4, PTOP])
                diag = sb(st, "x_diags", [P, RING, P])
                ybuf = sb(st, "x_y", [P, 2, 512])
                with nc.Block() as block:
                    @block.sync
                    def _(sp):
                        for g in range(2):
                            sp.dma_start(gt[:, g, :], modd[g:g + 1, 5 * DM:6 * DM].to_broadcast([P, DM])).then_inc(x_gt, 16)
                        sp.dma_start(iota[:, :], A["consts"][:, COFF["iota16"][0]:COFF["iota16"][0] + 16]).then_inc(x_iota, 16)

                    @block.gpsimd
                    def _(pool):
                        def gather(i, s, table, ring, in_, used):
                            n = PTOP * i + s
                            if s == 0:
                                pool.wait_ge(x_idx, i + 1)
                            if n >= RING:
                                pool.wait_ge(used, n - RING + 1)
                            G.indirect_dma_start(ring[:, n % RING, :], None, table,
                                                 bass.IndirectOffsetOnAxis(ap=idx[:, i % 4, s:s + 1], axis=0)).then_inc(in_[n % RING], 16)

                        for s in range(PTOP):
                            gather(0, s, table_u, ub, u_in, x_dot)
                        for i in range(NG):
                            for s in range(PTOP):
                                if i + 1 < NG:
                                    gather(i + 1, s, table_u, ub, u_in, x_dot)
                                gather(i, s, table_v, vb, v_in, x_vmm)

                    @block.vector
                    def _(dve):
                        link = chain("dve", dve)

                        def route(i):
                            t, h, b = i // PH, i % PH, i % 4
                            if i >= 4:
                                dve.wait_ge(x_vmm, PTOP * (i - 3))
                            rows = [sc[:, t, 2 * h + c, :] for c in range(2)]
                            for r in range(2):
                                o = slice(8 * r, 8 * r + 8)
                                V.max(sv[:, 0, o], rows[0])
                                link(V.max(sv[:, 1, o], rows[1]))
                                V.max_index(si[:, 0, o], sv[:, 0, o], rows[0])
                                link(V.max_index(si[:, 1, o], sv[:, 1, o], rows[1]))
                                if r == 0:
                                    V.match_replace(rows[0], sv[:, 0, o], rows[0], -3.0e38)
                                    link(V.match_replace(rows[1], sv[:, 1, o], rows[1], -3.0e38))
                            V.tensor_copy(sif[:, :, :], si[:, :, :])
                            link(V.tensor_tensor(cand[:, :, :], sv[:, 0, :, None].to_broadcast([P, PTOP, PTOP]),
                                                 sv[:, 1, None, :].to_broadcast([P, PTOP, PTOP]), ALU.add))
                            flat = cand[:, :, :].rearrange("p a b -> p (a b)")
                            for r in range(2):
                                o = slice(8 * r, 8 * r + 8)
                                link(V.max(fv[:, b, o], flat))
                                link(V.max_index(fi[:, o], fv[:, b, o], flat))
                                if r == 0:
                                    link(V.match_replace(flat, fv[:, b, o], flat, -3.0e38))
                            V.tensor_scalar(nm[:, b, 0:1], fv[:, b, 0:1], -1.0, None, ALU.mult).then_inc(x_nm, 1)
                            V.tensor_scalar(ab[:, 0, :], fi[:, :], 4, None, ALU.logical_shift_right)
                            link(V.tensor_scalar(ab[:, 1, :], fi[:, :], 15, None, ALU.bitwise_and))
                            link(V.tensor_copy(abf[:, :, :], ab[:, :, :]))
                            link(V.tensor_tensor(eq[:, :, :, :], abf[:, :, :, None].to_broadcast([P, 2, PTOP, PTOP]),
                                                 iota[:, None, None, :].to_broadcast([P, 2, PTOP, PTOP]), ALU.is_equal))
                            link(V.tensor_tensor(eq[:, :, :, :], eq[:, :, :, :], sif[:, :, None, :].to_broadcast([P, 2, PTOP, PTOP]), ALU.mult))
                            link(V.tensor_reduce(e01[:, :, :], eq[:, :, :, :], AX.X, ALU.add))
                            link(V.scalar_tensor_tensor(out=ef[:, :], in0=e01[:, 0, :], scalar=float(PK), in1=e01[:, 1, :], op0=ALU.mult, op1=ALU.add))
                            V.tensor_scalar(idx[:, b, :], ef[:, :], lbase[:, 0:1], None, ALU.add).then_inc(x_idx, 1)

                        def dots(i):
                            t, b = i // PH, i % 4
                            for s in range(PTOP):
                                n = PTOP * i + s
                                dve.wait_ge(u_in[n % RING], 16 * (n // RING + 1))
                                if n >= 2:
                                    dve.wait_ge(x_dot, n - 1)
                                V.tensor_tensor_reduce(out=junk[:, n % 2, :], in0=ub[:, n % RING, :], in1=h2[:, t, :], scale=1.0, scalar=0.0,
                                                       op0=ALU.mult, op1=ALU.add, accum_out=dot[:, b, s:s + 1]).then_inc(x_dot, 1)

                        def coefs(i):
                            b = i % 4
                            dve.wait_ge(x_ex, i + 1)
                            link(V.reciprocal(nm[:, b, 2:3], nm[:, b, 1:2]))
                            dve.wait_ge(x_gelu, i + 1)
                            V.scalar_tensor_tensor(out=coef[:, b, :], in0=dot[:, b, :], scalar=nm[:, b, 2:3], in1=fv[:, b, :],
                                                   op0=ALU.mult, op1=ALU.mult).then_inc(x_coef, 1)

                        def close(t):
                            dve.wait_ge(x_vmm, PTOP * PH * (t + 1))
                            for j in range(2):
                                o = slice(512 * j, 512 * j + 512)
                                link(V.tensor_tensor(ybuf[:, j, :], pb[2 * (t % 2) + j][:, :], gt[:, min(t, 1), o], ALU.mult))
                                V.tensor_tensor(x[:, t, o], x[:, t, o], ybuf[:, j, :], ALU.add).then_inc(x_add, 1)

                        dve.wait_ge(x_iota, 16)
                        dve.wait_ge(x_gt, 32)
                        route(0)
                        route(1)
                        dots(0)
                        coefs(0)
                        for i in range(NG):
                            if i + 2 < NG:
                                route(i + 2)
                            if i + 1 < NG:
                                dots(i + 1)
                                coefs(i + 1)
                            if i % PH == 1 and i > PH:
                                close(i // PH - 1)
                        close(NT - 1)

                    @block.scalar
                    def _(act):
                        def weights(i):
                            b = i % 4
                            act.wait_ge(x_nm, i + 1)
                            S.activation(fv[:, b, :], fv[:, b, :], ACT.Exp, bias=nm[:, b, 0:1], accum_out=nm[:, b, 1:2]).then_inc(x_ex, 1)

                        def gelu(i):
                            act.wait_ge(x_dot, PTOP * (i + 1))
                            S.activation(dot[:, i % 4, :], dot[:, i % 4, :], ACT.Gelu).then_inc(x_gelu, 1)

                        weights(0)
                        weights(1)
                        gelu(0)
                        for i in range(NG):
                            if i + 2 < NG:
                                weights(i + 2)
                            act.wait_ge(x_coef, i + 1)
                            for s in range(PTOP):
                                n = PTOP * i + s
                                if n >= RING:
                                    act.wait_ge(x_vmm, n - RING + 1)
                                S.activation(diag[:, n % RING, :], ident, ACT.Copy, scale=coef[:, i % 4, s:s + 1]).then_inc(x_diag, 1)
                            if i + 1 < NG:
                                gelu(i + 1)

                    @block.tensor
                    def _(pe):
                        for i in range(NG):
                            t, h = i // PH, i % PH
                            if h == 0 and t >= 2:
                                pe.wait_ge(x_add, 2 * (t - 1))
                            for s in range(PTOP):
                                n = PTOP * i + s
                                pe.wait_ge(x_diag, n + 1)
                                pe.wait_ge(v_in[n % RING], 16 * (n // RING + 1))
                                for j in range(2):
                                    last = mm(pb[2 * (t % 2) + j][:, :], diag[:, n % RING, :], vb[:, n % RING, 512 * j:512 * j + 512],
                                              start=(h == 0 and s == 0), stop=(h == PH - 1 and s == PTOP - 1))
                                last.then_inc(x_vmm, 1)

        def stage_peer(l):
            with ExitStack() as st:
                h2 = sb(st, "h2", [P, NT, DM])
                sc = sb(st, "p_sc", [P, NT, NSC, P])
                with stage():
                    stage_norm(1, h2)
                with stage():
                    stage_scores(l, sc)
                with stage():
                    stage_experts(l, sc, h2)
            with stage():
                nb = sem("next_base")
                with nc.Block() as block:
                    @block.vector
                    def _(dve):
                        V.tensor_scalar(lbase[:, :], lbase[:, :], float(NEXP), None, ALU.add).then_inc(nb, 1)
                        dve.wait_ge(nb, 1)

        def stage_output():
            y_out = sem("y_out")
            with nc.Block() as block:
                @block.sync
                def _(sp):
                    sp.dma_start(y_prompt[0, :, :], x[:, 0, :]).then_inc(y_out, 16)
                    sp.dma_start(y_sample[0, :, :].rearrange("(t p) d -> p t d", p=P), x[:, 1:NT, :]).then_inc(y_out, 16)
                    sp.wait_ge(y_out, 32)

        with nc.Fori(0, DEPTH) as l:
            layer(l)
        with stage():
            stage_output()


_INS = ["x_prompt", "x_sample", "state_mlstm_C", "state_mlstm_n", "state_mlstm_m", "state_gdn_S", "cache_attn_k",
        "cache_attn_v", "c", "c_ctx", "ada_w", "ada_b", "norm1_g", "norm2_g", "w_in", "m_ig_b", "m_fg_b", "m_norm_g",
        "g_conv_w", "g_A_log", "g_dt_bias", "g_norm_g", "a_qnorm_g", "a_knorm_g", "a_sink", "w_br_m", "w_br_g", "w_br_a",
        "w_out", "p_wq", "p_keys", "p_u", "p_v"]
_OUTS = [(1, P, DM), (1, 4 * P, DM), (1, DEPTH, 2, NH, DH, DH), (1, DEPTH, 2, NH, DH), (1, DEPTH, 2, NH),
         (1, DEPTH, 2, NH, DH, DH), (1, DEPTH, P, AKV, ADH), (1, DEPTH, P, AKV, ADH)]


def kernel(**inputs):
    import concourse.bacc as _bacc
    from concourse.bass_utils import run_bass_kernel_spmd as _run

    nc = _bacc.Bacc("TRN2", target_bir_lowering=False, num_devices=1)
    arrays, args, outs = {}, {}, []
    for name in _INS:
        a = np.ascontiguousarray(inputs[name])
        arrays[f"in_{name}"] = a
        args[name] = nc.dram_tensor(f"in_{name}", a.shape, mybir.dt.from_np(a.dtype), kind="ExternalInput").ap()
    arrays["in_consts"] = constants()
    args["consts"] = nc.dram_tensor("in_consts", (P, NCONST), mybir.dt.float32, kind="ExternalInput").ap()
    for i, shape in enumerate(_OUTS):
        outs.append(nc.dram_tensor(f"out_{i}", shape, mybir.dt.float32, kind="ExternalOutput").ap())
    scratch = {"mod": nc.dram_tensor("mod_rows", (2, 6 * DM), mybir.dt.float32, kind="Internal").ap()}
    program(nc, args, outs, scratch)
    r = _run(nc, [arrays], core_ids=[0])
    return tuple(r.results[0][f"out_{i}"] for i in range(len(_OUTS)))
```

```python
import math
import numpy as np
import concourse.bass as bass
from concourse import mybir
from contextlib import ExitStack, contextmanager

P = 128
DM = 1024
KD = DM // P
DEPTH = 2
NT = 5
TOK = NT * P
NH = 4
DH = 128
EPS = 1e-6
O_MQ, O_MK, O_MV, O_MI, O_MO = 0, 512, 1024, 1536, 1552
O_GQKV, O_GA, O_GZ = 2064, 3600, 3616
O_AQ, O_GATE = 4128, 4896
N_IN = 7968
AH, AKV, ADH = 8, 2, 64
A_SCALE = ADH ** -0.5
PH, PK, PTOP = 8, 128, 16
NEXP = PK * PK
BIG = 1.0e30

_LAYOUT = [("ident", 128), ("ones", 128), ("maskF", 128), ("maskB", 128), ("strictF", 128), ("strictB", 128),
           ("lev", 7 * 128), ("levT", 7 * 128), ("sel", 4 * 128), ("sel16", 16), ("sgn", 1), ("isM", 1),
           ("resetF", 640), ("resetB", 640), ("cos", 4 * 64), ("sin", 4 * 64), ("amask", 512), ("amask4", 384),
           ("iota16", 16)]
COFF = {}
_o = 0
for _n, _w in _LAYOUT:
    COFF[_n] = (_o, _w)
    _o += _w
NCONST = _o


def constants():
    c = np.zeros((P, NCONST), np.float32)

    def put(name, a):
        o, w = COFF[name]
        c[:, o:o + w] = np.asarray(a, np.float32).reshape(P, w)

    r = np.arange(P)
    row, col = r[:, None], r[None, :]
    put("ident", row == col)
    put("ones", np.ones((P, P)))
    put("maskF", np.where(row <= col, 0.0, -BIG))
    put("maskB", np.where(row >= col, 0.0, -BIG))
    put("strictF", row < col)
    put("strictB", row > col)
    lev = np.stack([((row >> j) % 2 == 1) & ((row >> j) == (col >> j) + 1) for j in range(7)], 1)
    put("lev", lev)
    put("levT", np.transpose(lev, (2, 1, 0)))
    sel = np.zeros((P, 4, P))
    sel16 = np.zeros((P, 16))
    sgn = np.zeros(P)
    for q in range(4):
        for h in range(4):
            sel[32 * q + h, h, :] = 1
            sel16[32 * q + h, 4 * q + h] = 1
            sgn[32 * q + h] = 1 if q % 2 else -1
    put("sel", sel)
    put("sel16", sel16)
    put("sgn", sgn)
    put("isM", (r // 32) % 2 == 0)
    t = np.arange(TOK)
    put("resetF", np.broadcast_to(t % P != 0, (P, TOK)))
    put("resetB", np.broadcast_to(t % P != P - 1, (P, TOK)))
    inv = 1.0 / (10000.0 ** (np.arange(0, 32, 2) / 32.0))
    pos = np.arange(4 * P)
    ra, ca = (pos // 64)[:, None] * inv, (pos % 64)[:, None] * inv
    cos = np.concatenate([np.cos(ra), np.cos(ra), np.cos(ca), np.cos(ca)], 1)
    sin = np.concatenate([-np.sin(ra), np.sin(ra), -np.sin(ca), np.sin(ca)], 1)
    put("cos", cos.reshape(4, P, 64).transpose(1, 0, 2))
    put("sin", sin.reshape(4, P, 64).transpose(1, 0, 2))
    before = np.where(col >= row, 0.0, -BIG)
    after = np.where(col <= row, 0.0, -BIG)
    z = np.zeros((P, P))
    put("amask", np.concatenate([before, z, after, z], 1))
    put("amask4", np.concatenate([before, z, z], 1))
    put("iota16", np.broadcast_to(np.arange(16), (P, 16)))
    return c


def program(nc, A, outs, scratch):
    f32 = mybir.dt.float32
    f32r = mybir.dt.float32r
    i32 = mybir.dt.int32
    u32 = mybir.dt.uint32
    ALU = mybir.AluOpType
    ACT = mybir.ActivationFunctionType
    AX = mybir.AxisListType
    mm = nc.tensor.matmul
    tr = nc.tensor.transpose
    ds = bass.ds
    V, S, G = nc.vector, nc.scalar, nc.gpsimd

    y_prompt, y_sample, new_C, new_n, new_m, new_S, new_k, new_v = outs
    modd = scratch["mod"]
    stage_sems = []
    stage_scope = []
    top = ExitStack()
    with top:
        def sb(scope, name, shape, dt=f32):
            return scope.enter_context(nc.sbuf_tensor(name, shape, dt))

        def sem(name):
            s = stage_scope[-1].enter_context(nc.semaphore(name))
            stage_sems.append(s)
            return s

        @contextmanager
        def stage():
            with ExitStack() as scope:
                stage_scope.append(scope)
                stage_sems.clear()
                chain_sem.clear()
                yield
                with nc.Block() as block:
                    @block.gpsimd
                    def _(pool):
                        pool.dma_reset()
                        for s in stage_sems:
                            pool.sem_clear(s)
                stage_scope.pop()

        pb = [top.enter_context(nc.psum_tensor(f"pb{i}", [P, 512], f32)) for i in range(8)]
        x = sb(top, "x", [P, NT, DM])
        ident = sb(top, "identity", [P, P])[:, :]
        CON_AT, CON_END = COFF["ones"][0], COFF["resetF"][0]
        condT = sb(top, "condT", [P, KD, 2])
        lbase = sb(top, "lbase", [P, 1])

        def K(name):
            o, w = COFF[name]
            return con[:, o - CON_AT:o - CON_AT + w]

        v4 = lambda a: a.rearrange("p (h s) -> p h s", h=4)

        def dram_cols(w, l, o, n):
            return w[l, :, o:o + n].rearrange("(k p) n -> p k n", p=P)

        chain_sem, chain_at = {}, {}

        def chain(name, eng):
            if name not in chain_sem:
                chain_sem[name], chain_at[name] = sem(f"{name}_chain"), 0

            def link(ins):
                chain_at[name] += 1
                ins.then_inc(chain_sem[name], 1)
                eng.wait_ge(chain_sem[name], chain_at[name])
            return link


        with stage():
            s_con = sem("constants_in")
            s_x = sem("x_in")
            s_cd = sem("cond_in")
            s_sil = sem("cond_done")
            s_lb = sem("base_cleared")
            with nc.Block() as block:
                @block.sync
                def _(sp):
                    sp.dma_start(ident[:, :], A["consts"][:, COFF["ident"][0]:COFF["ident"][0] + P]).then_inc(s_con, 16)
                    sp.dma_start(x[:, 0, :], A["x_prompt"][0, :, :]).then_inc(s_x, 16)
                    sp.dma_start(x[:, 1:NT, :], A["x_sample"][0, :, :].rearrange("(t p) d -> p t d", p=P)).then_inc(s_x, 16)
                    sp.wait_ge(s_con, 16)
                    sp.wait_ge(s_x, 32)

                @block.vector
                def _(dve):
                    V.memset(lbase[:, :], 0.0).then_inc(s_lb, 1)
                    dve.wait_ge(s_lb, 1)

                @block.scalar
                def _(act):
                    act.dma_start(condT[:, :, 0], A["c_ctx"].rearrange("(k p) -> p k", p=P), allow_slow_non_contiguous=True).then_inc(s_cd, 16)
                    act.dma_start(condT[:, :, 1], A["c"][0, :].rearrange("(k p) -> p k", p=P), allow_slow_non_contiguous=True).then_inc(s_cd, 16)
                    act.wait_ge(s_cd, 32)
                    S.activation(condT[:, :, :], condT[:, :, :], ACT.Silu).then_inc(s_sil, 1)

        hT = hS = con = ones = lev = levT = sel = yT = alpha = betar = cols = decbc = None

        def layer(l):
            nonlocal hT, hS, con, ones, lev, levT, sel, yT, alpha, betar, cols, decbc
            with stage():
                stage_modulation(l)
            with ExitStack() as mix:
                con = sb(mix, "con", [P, CON_END - CON_AT])
                ones = K("ones")
                lev, levT = K("lev").rearrange("p (j s) -> p j s", j=7), K("levT").rearrange("p (j s) -> p j s", j=7)
                sel = K("sel").rearrange("p (h s) -> p h s", h=4)
                hS = [sb(mix, f"hS_{n}", [P, KD, TOK], f32r) for n in ("hi", "lo")]
                yT = {}
                alpha = sb(mix, "alpha", [P, TOK])
                betar = sb(mix, "betar", [P, TOK])
                cols = sb(mix, "cols", [P, NT, 4, 16])
                decbc = sb(mix, "decbc", [P, NT, 16])
                with ExitStack() as exact:
                    hT = sb(exact, "hT", [P, KD, TOK])
                    with stage():
                        con_in = sem("con_in")

                        def load_constants(sp):
                            sp.dma_start(con[:, :], A["consts"][:, CON_AT:CON_END]).then_inc(con_in, 16)
                            sp.wait_ge(con_in, 16)

                        stage_norm(0, ahead=load_constants)
                    with stage():
                        stage_rows(l)
                for b, build in enumerate((stage_mlstm, stage_deltanet, stage_attention)):
                    yT[b] = sb(mix, f"yT{b}", [P, 4, TOK])
                    with stage():
                        build(l)
                with stage():
                    stage_merge(l)
            stage_peer(l)

        def stage_modulation(l):
            ada_in = [sem(f"ada_in{i}") for i in range(3)]
            ada_b_in, ada_done, mod_done, mod_out = sem("ada_b_in"), sem("ada_done"), sem("mod_done"), sem("mod_out")

            NCH = 6 * DM // 512
            with ExitStack() as st:
                W = [sb(st, f"adaW{i}", [P, KD, 512]) for i in range(3)]
                bias = sb(st, "adaB", [2, 6 * DM])
                gains = sb(st, "adaG", [2, 2, DM])
                mod = sb(st, "mod", [2, 6 * DM])
                with nc.Block() as block:
                    @block.sync
                    def _(sp):
                        for n in range(NCH):
                            if n >= 3:
                                sp.wait_ge(ada_done, n - 2)
                            sp.dma_start(W[n % 3][:, :, :], dram_cols(A["ada_w"], l, n * 512, 512)).then_inc(ada_in[n % 3], 16)
                        sp.wait_ge(mod_done, NCH + 2)
                        sp.dma_start(modd, mod[:, :]).then_inc(mod_out, 16)
                        sp.wait_ge(mod_out, 16)

                    @block.scalar
                    def _(act):
                        for j in range(2):
                            act.dma_start(bias[j:j + 1, :], A["ada_b"][l, None, :]).then_inc(ada_b_in, 16)
                            act.dma_start(gains[j:j + 1, 0, :], A["norm1_g"][l, None, :]).then_inc(ada_b_in, 16)
                            act.dma_start(gains[j:j + 1, 1, :], A["norm2_g"][l, None, :]).then_inc(ada_b_in, 16)

                    @block.tensor
                    def _(pe):
                        for n in range(NCH):
                            pe.wait_ge(ada_in[n % 3], 16 * (n // 3 + 1))
                            if n >= 2:
                                pe.wait_ge(mod_done, n - 1)
                            for k in range(KD):
                                last = mm(pb[n % 2][0:2, :], condT[:, k, :], W[n % 3][:, k, :], start=(k == 0), stop=(k == KD - 1))
                            last.then_inc(ada_done, 1)

                    @block.vector
                    def _(dve):
                        dve.wait_ge(ada_b_in, 96)
                        for n in range(NCH):
                            dve.wait_ge(ada_done, n + 1)
                            c = slice(n * 512, (n + 1) * 512)
                            V.tensor_tensor(mod[:, c], pb[n % 2][0:2, :], bias[:, c], ALU.add).then_inc(mod_done, 1)
                        dve.wait_ge(mod_done, NCH)
                        for j, o in enumerate((1, 4)):
                            V.scalar_tensor_tensor(out=mod[:, o * DM:(o + 1) * DM], in0=mod[:, o * DM:(o + 1) * DM], scalar=1.0,
                                                   in1=gains[:, j, :], op0=ALU.add, op1=ALU.mult).then_inc(mod_done, 1)

        def stage_norm(which, h_keep=None, ahead=None):
            s_in, s_sq, s_ms, s_rt, s_rs, s_mul, s_h, s_tr, s_evA, s_evV = [
                sem(n) for n in ("nrm_in", "nrm_sq", "nrm_ms", "nrm_root", "nrm_rstd", "nrm_mul", "nrm_h", "nrm_tr", "nrm_evA", "nrm_evV")]

            with ExitStack() as st:
                AB = sb(st, f"modAB{which}", [P, 2, 2, DM])
                junk = sb(st, f"nrm_junk{which}", [P, 2, DM])
                h = h_keep if h_keep is not None else sb(st, "h", [P, NT, DM])
                ss = sb(st, f"nrm_ss{which}", [P, 3, 8])
                with nc.Block() as block:
                    @block.sync
                    def _(sp):
                        for j, part in enumerate((3 * which + 1, 3 * which)):
                            for g in range(2):
                                sp.dma_start(AB[:, j, g, :], modd[g:g + 1, part * DM:(part + 1) * DM].to_broadcast([P, DM])).then_inc(s_in, 16)
                        if ahead:
                            ahead(sp)

                    @block.scalar
                    def _(act):
                        for t in range(NT):
                            if t >= 2:
                                act.wait_ge(s_sq, t - 1)
                            S.activation(junk[:, t % 2, :], x[:, t, :], ACT.Square, accum_out=ss[:, 0, t:t + 1]).then_inc(s_sq, 1)
                        act.wait_ge(s_ms, 1)
                        S.activation(ss[:, 1, 0:NT], ss[:, 2, 0:NT], ACT.Sqrt).then_inc(s_rt, 1)
                        for t in range(NT):
                            act.wait_ge(s_tr, 2 * t + 1)
                            S.activation(hT[:, 0:4, t * P:(t + 1) * P], v4(pb[2 * (t % 2)][:, :]), ACT.Copy).then_inc(s_evA, 1)

                    @block.vector
                    def _(dve):
                        dve.wait_ge(s_sq, NT)
                        V.tensor_scalar(ss[:, 2, 0:NT], ss[:, 0, 0:NT], 1.0 / DM, EPS, ALU.mult, ALU.add).then_inc(s_ms, 1)
                        dve.wait_ge(s_rt, 1)
                        V.reciprocal(ss[:, 0, 0:NT], ss[:, 1, 0:NT]).then_inc(s_rs, 1)
                        dve.wait_ge(s_rs, 1)
                        dve.wait_ge(s_in, 64)
                        for t in range(NT + 1):
                            if t < NT:
                                g = min(t, 1)
                                V.scalar_tensor_tensor(out=h[:, t, :], in0=x[:, t, :], scalar=ss[:, 0, t:t + 1], in1=AB[:, 0, g, :],
                                                       op0=ALU.mult, op1=ALU.mult).then_inc(s_mul, 1)
                                dve.wait_ge(s_mul, t + 1)
                                V.tensor_tensor(h[:, t, :], h[:, t, :], AB[:, 1, g, :], ALU.add).then_inc(s_h, 1)
                            if t >= 1:
                                dve.wait_ge(s_tr, 2 * t)
                                V.tensor_copy(hT[:, 4:8, (t - 1) * P:t * P], v4(pb[2 * ((t - 1) % 2) + 1][:, :])).then_inc(s_evV, 1)

                    @block.tensor
                    def _(pe):
                        for t in range(NT):
                            pe.wait_ge(s_h, t + 1)
                            if t >= 2:
                                pe.wait_ge(s_evA, t - 1)
                                pe.wait_ge(s_evV, t - 1)
                            for j in range(2):
                                for k in range(4):
                                    last = tr(pb[2 * (t % 2) + j][:, k * P:(k + 1) * P], h[:, t, (4 * j + k) * P:(4 * j + k + 1) * P], ident)
                                last.then_inc(s_tr, 1)

        def stage_rows(l):
            (r_w, r_wz, r_wc, r_clr, r_small, r_p1, r_p2, r_absz, r_exp, r_one, r_ln, r_ea, r_sg, r_mm, r_em, r_ai0, r_ai,
             r_wk0, r_wk, r_dsel, r_dec, r_tr, r_col, r_mout, r_hi, r_lo) = [sem("row_" + n) for n in (
                "weights_in", "weights_zeroed", "weights_placed", "cleared", "small_in", "product1", "product2", "abs_z", "exp_done",
                "one_added", "ln_done", "exp_a", "sigmoid", "m_done", "exp_m", "ai_arg", "ai_done", "wk_arg", "wk_done", "dec_sel",
                "dec_bcast", "transposed", "cols_done", "m_out", "h_hi", "h_lo")]

            with ExitStack() as st:
                w16 = sb(st, "w16", [P, 2, KD, 16])
                w1 = sb(st, "w1", [P, KD, P])
                w2 = sb(st, "w2", [P, KD, P])
                small = sb(st, "small", [P, 4])
                sc2 = sb(st, "sc2", [P, 2])
                rst = sb(st, "rst", [P, 2, TOK])
                Z, e_, LF, LI, SG, m_, b, AI, WK, EM = [sb(st, "row_" + n, [P, TOK]) for n in
                                                       ("Z", "e", "LF", "LI", "SG", "m", "b", "AI", "WK", "EM")]
                mp = sb(st, "mp", [P, 3, NT])
                dsel = sb(st, "dsel", [P, NT, 16])
                seg = lambda a: a[:, :].rearrange("p (c s) -> p c s", c=NT)
                with nc.Block() as block:
                    @block.sync
                    def _(sp):
                        for j, o in enumerate((O_MI, O_GA)):
                            sp.dma_start(w16[:, j, :, :], dram_cols(A["w_in"], l, o, 16)).then_inc(r_w, 16)
                        for j, n in enumerate(("resetF", "resetB")):
                            sp.dma_start(rst[:, j, :], A["consts"][:, COFF[n][0]:COFF[n][0] + TOK]).then_inc(r_small, 16)
                        sp.wait_ge(r_clr, 1)
                        for q in range(4):
                            d, isg = q // 2, q % 2
                            column = lambda a: a[l, d, :].rearrange("(h o) -> h o", o=1)
                            r = slice(32 * q, 32 * q + 4)
                            if isg:
                                sp.dma_start(small[r, 0:1], column(A["g_dt_bias"])).then_inc(r_small, 16)
                                sp.dma_start(small[r, 2:3], column(A["g_A_log"])).then_inc(r_small, 16)
                            else:
                                sp.dma_start(small[r, 0:1], column(A["m_fg_b"])).then_inc(r_small, 16)
                                sp.dma_start(small[r, 1:2], column(A["m_ig_b"])).then_inc(r_small, 16)
                                sp.dma_start(small[r, 3:4], column(A["state_mlstm_m"][0])).then_inc(r_small, 16)
                        sp.wait_ge(r_mm, 4)
                        for d, (r, e) in enumerate(((0, P - 1), (64, 0))):
                            sp.dma_start(new_m[0, l, d, :].rearrange("(h o) -> h o", o=1), m_[r:r + 4, e:e + 1]).then_inc(r_mout, 16)
                        sp.wait_ge(r_mout, 32)

                    @block.gpsimd
                    def _(pool):
                        G.memset(w1[:, :, :], 0.0).then_inc(r_wz, 1)
                        G.memset(w2[:, :, :], 0.0).then_inc(r_wz, 1)
                        pool.wait_ge(r_wz, 2)
                        pool.wait_ge(r_w, 32)
                        for q in range(4):
                            d, isg = q // 2, q % 2
                            lo = w16[:, isg, :, 4 * d:4 * d + 4]
                            hi = w16[:, isg, :, 8 + 4 * d:12 + 4 * d]
                            soft, other = (lo, hi) if isg else (hi, lo)
                            G.tensor_copy(w1[:, :, 32 * q:32 * q + 4], soft).then_inc(r_wc, 1)
                            G.tensor_copy(w2[:, :, 32 * q:32 * q + 4], other).then_inc(r_wc, 1)
                        for k in range(KD):
                            pool.wait_ge(r_hi, k + 1)
                            G.tensor_tensor(hS[1][:, k, :], hT[:, k, :], hS[0][:, k, :], ALU.subtract).then_inc(r_lo, 1)

                    @block.tensor
                    def _(pe):
                        pe.wait_ge(r_wc, 8)
                        for j, (w, done) in enumerate(((w1, r_p1), (w2, r_p2))):
                            for i, (o, n) in enumerate(((0, P), (P, TOK - P))):
                                for k in range(KD):
                                    last = mm(pb[2 * j + i][:, 0:n], w[:, k, :], hT[:, k, o:o + n], start=(k == 0), stop=(k == KD - 1))
                                last.then_inc(done, 1)
                        pe.wait_ge(r_dsel, 1)
                        mm(pb[4][:, 0:80], ones, dsel[:, :, :].rearrange("p c r -> p (c r)"), start=True, stop=True).then_inc(r_dec, 1)
                        pe.wait_ge(r_wk, 1)
                        pe.wait_ge(r_em, 1)
                        pe.wait_ge(r_sg, 2)
                        for t in range(NT):
                            if t >= 2:
                                pe.wait_ge(r_col, t - 1)
                            for j, a in enumerate((AI, WK, EM, SG)):
                                last = tr(pb[5 + t % 2][:, j * P:(j + 1) * P], a[:, t * P:(t + 1) * P], ident)
                            last.then_inc(r_tr, 1)

                    @block.scalar
                    def _(act):
                        for k in range(KD):
                            S.activation(hS[0][:, k, :], hT[:, k, :], ACT.Copy).then_inc(r_hi, 1)
                        act.wait_ge(r_small, 16 * 12)
                        S.activation(sc2[:, 1:2], small[:, 2:3], ACT.Exp).then_inc(r_ea, 1)
                        act.wait_ge(r_absz, 1)
                        S.activation(e_[:, :], e_[:, :], ACT.Exp, scale=-1.0).then_inc(r_exp, 1)
                        act.wait_ge(r_one, 1)
                        S.activation(e_[:, :], e_[:, :], ACT.Ln).then_inc(r_ln, 1)
                        act.wait_ge(r_p2, 2)
                        S.activation(SG[:, 0:P], pb[2][:, 0:P], ACT.Sigmoid).then_inc(r_sg, 1)
                        S.activation(SG[:, P:TOK], pb[3][:, :], ACT.Sigmoid).then_inc(r_sg, 1)
                        act.wait_ge(r_mm, 4)
                        S.activation(EM[:, :], m_[:, :], ACT.Exp, scale=-1.0).then_inc(r_em, 1)
                        act.wait_ge(r_ai0, 1)
                        S.activation(AI[:, :], AI[:, :], ACT.Exp).then_inc(r_ai, 1)
                        act.wait_ge(r_wk0, 1)
                        S.activation(WK[:, :], WK[:, :], ACT.Exp).then_inc(r_wk, 1)

                    @block.vector
                    def _(dve):
                        link = chain("dve", dve)
                        link(V.memset(m_[:, :], 0.0))
                        V.memset(mp[:, :, :], 0.0)
                        V.memset(small[:, :], 0.0).then_inc(r_clr, 1)
                        dve.wait_ge(r_small, 16 * 12)
                        link(V.tensor_tensor(sc2[:, 0:1], small[:, 0:1], K("sgn"), ALU.mult))
                        dve.wait_ge(r_p1, 2)
                        V.tensor_scalar(Z[:, 0:P], pb[0][:, 0:P], K("sgn"), sc2[:, 0:1], ALU.mult, ALU.add)
                        link(V.tensor_scalar(Z[:, P:TOK], pb[1][:, :], K("sgn"), sc2[:, 0:1], ALU.mult, ALU.add))
                        V.scalar_tensor_tensor(out=e_[:, :], in0=Z[:, :], scalar=-1.0, in1=Z[:, :], op0=ALU.mult, op1=ALU.max).then_inc(r_absz, 1)
                        dve.wait_ge(r_exp, 1)
                        V.tensor_scalar(e_[:, :], e_[:, :], 1.0, None, ALU.add).then_inc(r_one, 1)
                        dve.wait_ge(r_ln, 1)
                        link(V.scalar_tensor_tensor(out=LF[:, :], in0=Z[:, :], scalar=0.0, in1=e_[:, :], op0=ALU.max, op1=ALU.add))
                        dve.wait_ge(r_ea, 1)
                        link(V.tensor_scalar(LF[:, :], LF[:, :], sc2[:, 1:2], -1.0, ALU.mult, ALU.mult))
                        dve.wait_ge(r_sg, 2)
                        for o, n, bank in ((0, P, 2), (P, TOK - P, 3)):
                            link(V.tensor_scalar(LI[:, o:o + n], pb[bank][:, 0:n], small[:, 1:2], K("isM"), ALU.add, ALU.mult))
                        scan = V.tensor_tensor_scan
                        for r, step in ((slice(0, 32), 1), (slice(64, 96), -1)):
                            for o, n, init in ((0, P, 0.0), (P, TOK - P, small[r, 3:4])):
                                a = slice(o, o + n) if step == 1 else slice(o + n - 1, o - 1 if o else None, -1)
                                scan(out=m_[r, a], data0=LF[r, a], data1=LI[r, a], initial=init, op0=ALU.add, op1=ALU.max).then_inc(r_mm, 1)
                        dve.wait_ge(r_mm, 4)
                        link(scan(out=b[0:64, :], data0=rst[0:64, 0, :], data1=LF[0:64, :], initial=0.0, op0=ALU.mult, op1=ALU.add))
                        link(scan(out=b[64:P, ::-1], data0=rst[64:P, 1, ::-1], data1=LF[64:P, ::-1], initial=0.0, op0=ALU.mult, op1=ALU.add))
                        V.tensor_tensor(alpha[:, :], b[:, :], m_[:, :], ALU.subtract)
                        link(V.tensor_tensor(betar[:, :], LI[:, :], b[:, :], ALU.subtract))
                        V.tensor_copy(mp[0:64, 0, 1:2], small[0:64, 3:4])
                        V.tensor_copy(mp[0:64, 0, 2:NT], seg(m_)[0:64, 1:NT - 1, P - 1])
                        V.tensor_copy(mp[64:P, 0, NT - 1:NT], small[64:P, 3:4])
                        V.tensor_copy(mp[64:P, 0, 1:NT - 1], seg(m_)[64:P, 2:NT, 0])
                        V.tensor_copy(mp[0:64, 1, :], seg(alpha)[0:64, :, P - 1])
                        link(V.tensor_copy(mp[64:P, 1, :], seg(alpha)[64:P, :, 0]))
                        V.tensor_tensor(seg(AI), seg(alpha), mp[:, 0, :, None].to_broadcast([P, NT, P]), ALU.add).then_inc(r_ai0, 1)
                        V.tensor_tensor(seg(WK), seg(betar), mp[:, 1, :, None].to_broadcast([P, NT, P]), ALU.add).then_inc(r_wk0, 1)
                        dve.wait_ge(r_ai, 1)
                        V.tensor_copy(mp[0:64, 2, :], seg(AI)[0:64, :, P - 1])
                        link(V.tensor_copy(mp[64:P, 2, :], seg(AI)[64:P, :, 0]))
                        V.tensor_tensor(dsel[:, :, :], K("sel16")[:, None, :].to_broadcast([P, NT, 16]),
                                        mp[:, 2, :, None].to_broadcast([P, NT, 16]), ALU.mult).then_inc(r_dsel, 1)
                        dve.wait_ge(r_dec, 1)
                        V.tensor_copy(decbc[:, :, :].rearrange("p c r -> p (c r)"), pb[4][:, 0:80])
                        for t in range(NT):
                            dve.wait_ge(r_tr, t + 1)
                            src = pb[5 + t % 2][:, :].rearrange("p (j q h) -> p j q h", j=4, q=4)[:, :, :, 0:4]
                            V.tensor_copy(cols[:, t, :, :].rearrange("p j (q h) -> p j q h", q=4), src).then_inc(r_col, 1)

        W_BUFS, CW = 3, 256

        def product(out, lhs, rhs, n_k):
            for k in range(n_k):
                mm(out, lhs(0, k), rhs(0, k), start=(k == 0), stop=False)
                mm(out, lhs(0, k), rhs(1, k), start=False, stop=False)
                last = mm(out, lhs(1, k), rhs(0, k), start=False, stop=(k == n_k - 1))
            return last

        def weight_buffers(scope, name):
            return ([sb(scope, f"{name}_W{i}", [P, KD, CW]) for i in range(W_BUFS)],
                    [[sb(scope, f"{name}_W{part}{i}", [P, KD, CW], f32r) for part in ("hi", "lo")] for i in range(2)])

        HALVES = ((0, 320), (320, 320))

        def project(name, chunks, jobs):
            in_ = [sem(f"{name}_w_in{i}") for i in range(W_BUFS)]
            hi, lo, done, evA, evV = [sem(f"{name}_{n}") for n in ("w_hi", "w_lo", "product", "evac_act", "evac_dve")]
            on_act = [(j[5] in (ACT.Sigmoid, ACT.Silu)) or i % 2 == 0 for i, j in enumerate(jobs)]
            act_before = [sum(on_act[:i]) for i in range(len(jobs) + 1)]
            last_job = {j[0]: i for i, j in enumerate(jobs)}

            def run(l, Wb, Ws):
                with nc.Block() as block:
                    @block.sync
                    def _(sp):
                        for n, (w, o) in enumerate(chunks):
                            if n >= W_BUFS:
                                sp.wait_ge(lo, n - W_BUFS + 1)
                            sp.dma_start(Wb[n % W_BUFS][:, :, :], dram_cols(w, l, o, CW)).then_inc(in_[n % W_BUFS], 16)

                    @block.gpsimd
                    def _(pool):
                        for n in range(len(chunks)):
                            W, (Wh, Wl) = Wb[n % W_BUFS], Ws[n % 2]
                            pool.wait_ge(hi, n + 1)
                            G.tensor_tensor(Wl[:, :, :], W[:, :, :], Wh[:, :, :], ALU.subtract).then_inc(lo, 1)

                    @block.tensor
                    def _(pe):
                        for i, (n, kind, c, tokens, pieces, func) in enumerate(jobs):
                            pe.wait_ge(lo, n + 1)
                            if i >= 8:
                                pe.wait_ge(evA if on_act[i - 8] else evV,
                                           act_before[i - 7] if on_act[i - 8] else i - 7 - act_before[i - 7])
                            if kind == "rows":
                                last = product(pb[i % 8][:, 0:CW], lambda a, k: hS[a][:, k, c * P:(c + 1) * P], lambda a, k: Ws[n % 2][a][:, k, :], KD)
                            else:
                                o, w = tokens
                                last = product(pb[i % 8][:, 0:w], lambda a, k: Ws[n % 2][a][:, k, c * P:(c + 1) * P], lambda a, k: hS[a][:, k, o:o + w], KD)
                            last.then_inc(done, 1)

                    @block.scalar
                    def _(act):
                        def weights_hi(n):
                            act.wait_ge(in_[n % W_BUFS], 16 * (n // W_BUFS + 1))
                            if n >= 2:
                                act.wait_ge(done, last_job[n - 2] + 1)
                            S.activation(Ws[n % 2][0][:, :, :], Wb[n % W_BUFS][:, :, :], ACT.Copy).then_inc(hi, 1)

                        weights_hi(0)
                        for i, (n, kind, c, tokens, pieces, func) in enumerate(jobs):
                            if n + 1 < len(chunks) and (i == 0 or jobs[i - 1][0] != n):
                                weights_hi(n + 1)
                            if on_act[i]:
                                act.wait_ge(done, i + 1)
                                for out, a, b in pieces:
                                    src = pb[i % 8][:, a:b] if len(out.shape) == 2 else pb[i % 8][:, a:b].rearrange("p (h s) -> p h s", s=P)
                                    last = S.activation(out, src, ACT.Copy, scale=func) if isinstance(func, float) else S.activation(out, src, func)
                                last.then_inc(evA, 1)

                    @block.vector
                    def _(dve):
                        for i, (n, kind, c, tokens, pieces, func) in enumerate(jobs):
                            if not on_act[i]:
                                dve.wait_ge(done, i + 1)
                                for out, a, b in pieces:
                                    src = pb[i % 8][:, a:b] if len(out.shape) == 2 else pb[i % 8][:, a:b].rearrange("p (h s) -> p h s", s=P)
                                    last = V.tensor_scalar(out, src, func, None, ALU.mult)
                                last.then_inc(evV, 1)
            return run

        FT, BT = (0, 1, 2, 3, 4), (0, 4, 3, 2, 1)

        def stage_mlstm(l):
            (m_st_in, m_zero, m_kt, m_ktev, m_D, m_KQ, m_dm, m_E, m_S, m_inter, m_is, m_intra, m_num, m_kw, m_upd, m_C, m_out, m_O) = [
                sem("m_" + n) for n in ("state_in", "zeroed", "k_transposed", "k_tokens", "D", "KQ", "masked", "E", "S", "inter",
                                        "inter_scaled", "intra", "num", "k_weighted", "update", "C", "state_out", "O")]
            with ExitStack() as st:
                qT = sb(st, "m_qT", [P, 4, TOK])
                kT = sb(st, "m_kT", [P, 4, TOK])
                v1 = sb(st, "m_v1", [P, NT, 4, DH + 1])
                mo = sb(st, "m_o", [P, NT, 512])
                chunks = [(A["w_in"], o + CW * j) for o in (O_MQ, O_MK, O_MV, O_MO) for j in range(2)]
                jobs = []
                for n, (dst, scale) in enumerate(((qT, 1.0), (kT, DH ** -0.5))):
                    for c in range(4):
                        for o, w in HALVES:
                            jobs.append((2 * n + c // 2, "cols", c % 2, (o, w), [(dst[:, c, o:o + w], 0, w)], scale))
                jobs += [(4 + j, "rows", t, None, [(v1[:, t, 2 * j:2 * j + 2, 0:DH], 0, CW)], 1.0) for j in range(2) for t in range(NT)]
                jobs += [(6 + j, "rows", t, None, [(mo[:, t, CW * j:CW * j + CW], 0, CW)], ACT.Sigmoid) for j in range(2) for t in range(NT)]
                with ExitStack() as wst:
                    project("mproj", chunks, jobs)(l, *weight_buffers(wst, "m"))
                kt = sb(st, "m_k", [P, NT, 4, DH])
                O = sb(st, "m_O", [P, NT, 512])
                with ExitStack() as sc:
                    C = [[sb(sc, f"m_C{g}{d}", [P, 4, DH + 1]) for d in range(2)] for g in range(2)]
                    E = [sb(sc, f"m_E{d}", [P, 512]) for d in range(2)]
                    Sm = [sb(sc, f"m_S{d}", [P, 512]) for d in range(2)]
                    num = [sb(sc, f"m_num{d}", [P, 4, DH + 1]) for d in range(2)]
                    kw = [sb(sc, f"m_kw{d}", [P, 4, DH]) for d in range(2)]
                    den = [sb(sc, f"m_den{d}", [P, 4]) for d in range(2)]
                    bD, bKQ, bN = [pb[0], pb[4]], [pb[1], pb[5]], [(pb[2], pb[3]), (pb[6], pb[7])]
                    hp = lambda bank: bank[:, 0:2 * (DH + 1)].rearrange("p (h e) -> p h e", h=2)
                    tile = lambda d, p: (FT, BT)[d][p]
                    sl = lambda c: slice(c * P, (c + 1) * P)
                    units = [(p, d) for p in range(NT) for d in range(2)]
                    with nc.Block() as block:
                        @block.sync
                        def _(sp):
                            for d in range(2):
                                sp.dma_start(C[1][d][:, :, 0:DH], A["state_mlstm_C"][0, l, d, :, :, :].rearrange("h d e -> d h e")).then_inc(m_st_in, 16)
                                sp.dma_start(C[1][d][:, :, DH], A["state_mlstm_n"][0, l, d, :, :].rearrange("h d -> d h"),
                                             allow_slow_non_contiguous=True).then_inc(m_st_in, 16)
                            sp.wait_ge(m_C, 2)
                            for d in range(2):
                                sp.dma_start(new_C[0, l, d, :, :, :].rearrange("h d e -> d h e"), C[0][d][:, :, 0:DH]).then_inc(m_out, 16)
                                sp.dma_start(new_n[0, l, d, :, :].rearrange("h d -> d h"), C[0][d][:, :, DH],
                                             allow_slow_non_contiguous=True).then_inc(m_out, 16)
                            sp.wait_ge(m_out, 64)

                        @block.gpsimd
                        def _(pool):
                            for d in range(2):
                                G.memset(C[0][d][:, :, :], 0.0)
                            G.memset(v1[:, :, :, DH:DH + 1], 1.0)
                            G.memset(O[:, :, :], 0.0).then_inc(m_zero, 1)
                            for u, (p, d) in enumerate(units):
                                c = tile(d, p)
                                pool.wait_ge(m_ktev, NT)
                                if u >= 2:
                                    pool.wait_ge(m_upd, u - 1)
                                G.tensor_tensor(kw[d][:, :, :], kt[:, c, :, :],
                                                cols[:, c, 1, 8 * d:8 * d + 4, None].to_broadcast([P, 4, DH]), ALU.mult).then_inc(m_kw, 1)

                        @block.tensor
                        def _(pe):
                            for t in range(NT):
                                if t >= 2:
                                    pe.wait_ge(m_ktev, t - 1)
                                for h in range(4):
                                    last = tr(pb[6 + t % 2][:, h * P:(h + 1) * P], kT[:, h, sl(t)], ident)
                                last.then_inc(m_kt, 1)
                            pe.wait_ge(m_zero, 1)
                            for p in range(NT):
                                for d in range(2):
                                    u, c = 2 * p + d, tile(d, p)
                                    r = slice(64 * d, 64 * d + 32)
                                    if u >= 2:
                                        pe.wait_ge(m_dm, u - 1)
                                    elif u == 0:
                                        pe.wait_ge(m_ktev, NT)
                                    mm(bD[d][:, :], betar[r, sl(c)], sel[r, :, :].rearrange("p h s -> p (h s)"), start=True, stop=False)
                                    for h in range(4):
                                        last = mm(bD[d][:, sl(h)], sel[r, h, :], alpha[r, sl(c)], start=False, stop=(h == 3))
                                    last.then_inc(m_D, 1)
                                    if u >= 2:
                                        pe.wait_ge(m_S, u - 1)
                                    for h in range(4):
                                        last = mm(bKQ[d][:, sl(h)], kT[:, h, sl(c)], qT[:, h, sl(c)], start=True, stop=True)
                                    last.then_inc(m_KQ, 1)
                                if p == 1:
                                    pe.wait_ge(m_st_in, 64)
                                for d in range(2):
                                    u, c = 2 * p + d, tile(d, p)
                                    if u >= 2:
                                        pe.wait_ge(m_C, u - 1)
                                    for h in range(4):
                                        last = mm(hp(bN[d][h // 2])[:, h % 2, :], qT[:, h, sl(c)], C[min(p, 1)][d][:, h, :], start=True, stop=True)
                                    last.then_inc(m_inter, 1)
                                for d in range(2):
                                    u, c = 2 * p + d, tile(d, p)
                                    pe.wait_ge(m_S, u + 1)
                                    pe.wait_ge(m_is, u + 1)
                                    for h in range(4):
                                        last = mm(hp(bN[d][h // 2])[:, h % 2, :], Sm[d][:, sl(h)], v1[:, c, h, :], start=True, stop=True)
                                    last.then_inc(m_intra, 1)
                                for d in range(2):
                                    u, c = 2 * p + d, tile(d, p)
                                    pe.wait_ge(m_num, u + 1)
                                    pe.wait_ge(m_kw, u + 1)
                                    for h in range(4):
                                        last = mm(hp(bN[d][h // 2])[:, h % 2, :], kw[d][:, h, :], v1[:, c, h, :], start=True, stop=True)
                                    last.then_inc(m_upd, 1)

                        @block.scalar
                        def _(act):
                            for t in range(NT):
                                act.wait_ge(m_kt, t + 1)
                                S.activation(kt[:, t, :, :], v4(pb[6 + t % 2][:, :]), ACT.Copy).then_inc(m_ktev, 1)
                            for p in range(NT):
                                for d in range(2):
                                    act.wait_ge(m_dm, 2 * p + d + 1)
                                    S.activation(E[d][:, :], E[d][:, :], ACT.Exp).then_inc(m_E, 1)
                                for d in range(2):
                                    u, c = 2 * p + d, tile(d, p)
                                    act.wait_ge(m_inter, u + 1)
                                    if u >= 2:
                                        act.wait_ge(m_O, u - 1)
                                    for h in range(4):
                                        last = S.activation(num[d][:, h, :], hp(bN[d][h // 2])[:, h % 2, :], ACT.Copy,
                                                            scale=cols[:, c, 0, 8 * d + h:8 * d + h + 1])
                                    last.then_inc(m_is, 1)

                        @block.vector
                        def _(dve):
                            link = chain("dve", dve)
                            for p in range(NT):
                                for d in range(2):
                                    u = 2 * p + d
                                    dve.wait_ge(m_D, u + 1)
                                    mask = K("maskB" if d else "maskF")
                                    V.tensor_tensor(v4(E[d][:, :]), v4(bD[d][:, :]), mask[:, None, :].to_broadcast([P, 4, P]), ALU.min).then_inc(m_dm, 1)
                                for d in range(2):
                                    u = 2 * p + d
                                    dve.wait_ge(m_E, u + 1)
                                    dve.wait_ge(m_KQ, u + 1)
                                    V.tensor_tensor(Sm[d][:, :], E[d][:, :], bKQ[d][:, :], ALU.mult).then_inc(m_S, 1)
                                for d in range(2):
                                    u, c = 2 * p + d, tile(d, p)
                                    dve.wait_ge(m_intra, u + 1)
                                    for j in range(2):
                                        last = V.tensor_tensor(num[d][:, 2 * j:2 * j + 2, :], num[d][:, 2 * j:2 * j + 2, :], hp(bN[d][j]), ALU.add)
                                    last.then_inc(m_num, 1)
                                    dve.wait_ge(m_num, u + 1)
                                    dn = num[d][:, :, DH]
                                    link(V.scalar_tensor_tensor(out=den[d][:, :], in0=dn, scalar=-1.0, in1=dn, op0=ALU.mult, op1=ALU.max))
                                    link(V.tensor_tensor(den[d][:, :], den[d][:, :], cols[:, c, 2, 8 * d:8 * d + 4], ALU.max))
                                    link(V.reciprocal(den[d][:, :], den[d][:, :]))
                                    for h in range(4):
                                        o = O[:, c, sl(h)]
                                        last = V.scalar_tensor_tensor(out=o, in0=num[d][:, h, 0:DH], scalar=den[d][:, h:h + 1], in1=o,
                                                                      op0=ALU.mult, op1=ALU.add)
                                    last.then_inc(m_O, 1)
                                for d in range(2):
                                    u, c = 2 * p + d, tile(d, p)
                                    dve.wait_ge(m_upd, u + 1)
                                    Cd = C[min(p, 1)][d]
                                    for h in range(4):
                                        last = V.scalar_tensor_tensor(out=Cd[:, h, :], in0=Cd[:, h, :], scalar=decbc[:, c, 8 * d + h:8 * d + h + 1],
                                                                      in1=hp(bN[d][h // 2])[:, h % 2, :], op0=ALU.mult, op1=ALU.add)
                                    last.then_inc(m_C, 1)
                finish_mixer(0, l, O, mo, A["m_norm_g"], 512)

        def finish_mixer(which, l, O, gate, gain, width):
            s_in, s_sq, s_ms, s_rt, s_y, s_tr, s_ev = [sem(f"fin_{n}") for n in ("gain_in", "squared", "mean_square", "root", "gated", "transposed", "evac")]

            with ExitStack() as st:
                sq = sb(st, f"fin_sq{which}", [P, NT * 4, DH])
                g = sb(st, f"fin_g{which}", [P, width])
                ms = sb(st, f"fin_ms{which}", [P, NT * 4])
                Oh = O[:, :, :].rearrange("p t (h e) -> p (t h) e", h=4)
                with nc.Block() as block:
                    @block.sync
                    def _(sp):
                        sp.dma_start(g[:, :], gain[l, None, :].to_broadcast([P, width])).then_inc(s_in, 16)

                    @block.scalar
                    def _(act):
                        S.activation(sq[:, :, :], Oh, ACT.Square).then_inc(s_sq, 1)
                        act.wait_ge(s_ms, 1)
                        S.activation(ms[:, :], ms[:, :], ACT.Sqrt).then_inc(s_rt, 1)
                        for t in range(NT):
                            act.wait_ge(s_tr, t + 1)
                            S.activation(yT[which][:, :, t * P:(t + 1) * P], v4(pb[t % 2][:, :]), ACT.Copy).then_inc(s_ev, 1)

                    @block.vector
                    def _(dve):
                        link = chain("dve", dve)
                        dve.wait_ge(s_sq, 1)
                        link(V.tensor_reduce(ms[:, :], sq[:, :, :], AX.X, ALU.add))
                        V.tensor_scalar(ms[:, :], ms[:, :], 1.0 / DH, EPS, ALU.mult, ALU.add).then_inc(s_ms, 1)
                        dve.wait_ge(s_rt, 1)
                        link(V.reciprocal(ms[:, :], ms[:, :]))
                        dve.wait_ge(s_in, 16)
                        link(V.tensor_tensor(Oh, Oh, ms[:, :, None].to_broadcast([P, NT * 4, DH]), ALU.mult))
                        link(V.tensor_tensor(Oh, Oh, g[:, None, :].to_broadcast([P, NT * 4, DH]), ALU.mult) if width == DH else
                             V.tensor_tensor(O[:, :, :], O[:, :, :], g[:, None, :].to_broadcast([P, NT, 512]), ALU.mult))
                        for t in range(NT):
                            V.tensor_tensor(O[:, t, :], O[:, t, :], gate[:, t, :], ALU.mult).then_inc(s_y, 1)

                    @block.tensor
                    def _(pe):
                        for t in range(NT):
                            pe.wait_ge(s_y, t + 1)
                            if t >= 2:
                                pe.wait_ge(s_ev, t - 1)
                            for h in range(4):
                                last = tr(pb[t % 2][:, h * P:(h + 1) * P], O[:, t, h * P:(h + 1) * P], ident)
                            last.then_inc(s_tr, 1)

        QW, KVW = AH * ADH, AKV * ADH
        NQK = AH + AKV

        def stage_attention(l):
            (a_small, a_ctx, a_sq, a_ms, a_rt, a_nrm, a_rp, a_kv, a_dup, a_trq, a_evq, a_trk, a_evk, a_sc, a_msk, a_nm, a_df, a_ex, a_es, a_pt,
             a_pe, a_pv, a_o, a_ot, a_oe) = [sem("a_" + n) for n in (
                "small_in", "ctx_in", "squared", "mean_square", "root", "normed", "rotated", "kv_out", "k_doubled", "q_transposed", "q_evac",
                "k_transposed", "k_evac", "scores", "masked", "neg_max", "sink_diff", "exp", "exp_sink", "p_transposed", "p_evac", "pv", "o",
                "o_transposed", "o_evac")]
            with ExitStack() as st:
                a = sb(st, "a_qkv", [P, NT, QW + 2 * KVW])
                with ExitStack() as wst:
                    project("aproj", [(A["w_in"], O_AQ + CW * n) for n in range(3)],
                            [(n, "rows", t, None, [(a[:, t, CW * n:CW * n + CW], 0, CW)], 1.0) for n in range(3) for t in range(NT)])(
                                l, *weight_buffers(wst, "a"))
                rot = sb(st, "a_rot", [P, 2, 4, ADH])
                amask = sb(st, "a_mask", [P, 512 + 384])
                gq = sb(st, "a_gq", [P, ADH])
                gk = sb(st, "a_gk", [P, ADH])
                sink = sb(st, "a_sinks", [P, AH])
                kc = sb(st, "a_kc", [P, 2, KVW])
                sq = sb(st, "a_sq", [P, 2, NQK * ADH])
                ms = sb(st, "a_ms", [P, NT, NQK])
                kd = sb(st, "a_kd", [P, NT + 1, AKV, 2, ADH])
                qT = sb(st, "a_qT", [P, AH // 2, TOK])
                kT = sb(st, "a_kT", [P, AKV, TOK + P])
                with nc.Block() as block:
                    @block.sync
                    def _(sp):
                        sp.dma_start(gq[:, :], A["a_qnorm_g"][l, None, :].to_broadcast([P, ADH])).then_inc(a_small, 16)
                        sp.dma_start(gk[:, :], A["a_knorm_g"][l, None, :].to_broadcast([P, ADH])).then_inc(a_small, 16)
                        sp.dma_start(sink[:, :], A["a_sink"][l, None, :].to_broadcast([P, AH])).then_inc(a_small, 16)
                        for j, n in enumerate(("cos", "sin")):
                            sp.dma_start(rot[:, j, :, :].rearrange("p t e -> p (t e)"), A["consts"][:, COFF[n][0]:COFF[n][0] + 256]).then_inc(a_small, 16)
                        sp.dma_start(amask[:, :], A["consts"][:, COFF["amask"][0]:COFF["amask"][0] + 896]).then_inc(a_small, 16)
                        sp.dma_start(kc[:, 0, :], A["cache_attn_k"][0, l, :, :, :].rearrange("t h d -> t (h d)")).then_inc(a_ctx, 16)
                        sp.dma_start(kc[:, 1, :], A["cache_attn_v"][0, l, :, :, :].rearrange("t h d -> t (h d)")).then_inc(a_ctx, 16)
                        sp.wait_ge(a_nrm, 1)
                        sp.dma_start(new_k[0, l, :, :, :].rearrange("t h d -> t (h d)"), a[:, 0, QW:QW + KVW]).then_inc(a_kv, 16)
                        sp.dma_start(new_v[0, l, :, :, :].rearrange("t h d -> t (h d)"), a[:, 0, QW + KVW:]).then_inc(a_kv, 16)
                        sp.wait_ge(a_kv, 32)

                    @block.scalar
                    def _(act):
                        for t in range(NT):
                            if t >= 2:
                                act.wait_ge(a_ms, t - 1)
                            S.activation(sq[:, t % 2, :], a[:, t, 0:NQK * ADH], ACT.Square).then_inc(a_sq, 1)
                        act.wait_ge(a_ms, NT + 1)
                        S.activation(ms[:, :, :], ms[:, :, :], ACT.Sqrt).then_inc(a_rt, 1)
                        for t in range(NT):
                            act.wait_ge(a_trq, t + 1)
                            S.activation(qT[:, :, t * P:(t + 1) * P], v4(pb[t % 2][:, :]), ACT.Copy).then_inc(a_evq, 1)

                    @block.vector
                    def _(dve):
                        link = chain("dve", dve)
                        for t in range(NT):
                            dve.wait_ge(a_sq, t + 1)
                            V.tensor_reduce(ms[:, t, :], sq[:, t % 2, :].rearrange("p (h e) -> p h e", h=NQK), AX.X, ALU.add).then_inc(a_ms, 1)
                        dve.wait_ge(a_ms, NT)
                        V.tensor_scalar(ms[:, :, :], ms[:, :, :], 1.0 / ADH, EPS, ALU.mult, ALU.add).then_inc(a_ms, 1)
                        dve.wait_ge(a_rt, 1)
                        link(V.reciprocal(ms[:, :, :], ms[:, :, :]))
                        dve.wait_ge(a_small, 96)
                        for t in range(NT):
                            X = a[:, t, 0:NQK * ADH].rearrange("p (h e) -> p h e", h=NQK)
                            link(V.tensor_tensor(X, X, ms[:, t, :, None].to_broadcast([P, NQK, ADH]), ALU.mult))
                            V.tensor_tensor(X[:, 0:AH, :], X[:, 0:AH, :], gq[:, None, :].to_broadcast([P, AH, ADH]), ALU.mult)
                            V.tensor_tensor(X[:, AH:, :], X[:, AH:, :], gk[:, None, :].to_broadcast([P, AKV, ADH]), ALU.mult).then_inc(a_nrm, 1)
                            dve.wait_ge(a_nrm, t + 1)
                            if t > 0:
                                X4 = X.rearrange("p h (f j e) -> p h f j e", f=2, j=2)
                                Y4 = sq[:, t % 2, :].rearrange("p (h f j e) -> p h f j e", h=NQK, f=2, j=2)
                                sn = rot[:, 1, t - 1, :].rearrange("p (f j e) -> p f j e", f=2, j=2)
                                for j in range(2):
                                    link(V.tensor_tensor(Y4[:, :, :, j, :], X4[:, :, :, 1 - j, :],
                                                         sn[:, None, :, j, :].to_broadcast([P, NQK, 2, 16]), ALU.mult))
                                link(V.tensor_tensor(X, X, rot[:, 0, t - 1, None, :].to_broadcast([P, NQK, ADH]), ALU.mult))
                                V.tensor_tensor(a[:, t, 0:NQK * ADH], a[:, t, 0:NQK * ADH], sq[:, t % 2, :], ALU.add).then_inc(a_rp, 1)
                        for t in range(NT + 1):
                            dve.wait_ge(a_trk, t + 1)
                            V.tensor_copy(kT[:, :, t * P:(t + 1) * P], pb[2 + t % 2][:, 0:2 * P].rearrange("p (g s) -> p g s", g=AKV)).then_inc(a_evk, 1)

                    @block.gpsimd
                    def _(pool):
                        pool.wait_ge(a_ctx, 32)
                        for t in [NT] + list(range(NT)):
                            if t == 0:
                                pool.wait_ge(a_nrm, 1)
                            elif t < NT:
                                pool.wait_ge(a_rp, t)
                            src = (kc[:, 0, :] if t == NT else a[:, t, QW:QW + KVW]).rearrange("p (g e) -> p g e", g=AKV)
                            for j in range(2):
                                last = G.tensor_copy(kd[:, t, :, j, :], src)
                            last.then_inc(a_dup, 1)

                    @block.tensor
                    def _(pe):
                        for t in range(NT + 1):
                            pe.wait_ge(a_dup, NT + 1 if t == NT else t + 2)
                            if t < NT:
                                if t >= 2:
                                    pe.wait_ge(a_evq, t - 1)
                                for j in range(4):
                                    last = tr(pb[t % 2][:, j * P:(j + 1) * P], a[:, t, j * P:(j + 1) * P], ident)
                                last.then_inc(a_trq, 1)
                            if t >= 2:
                                pe.wait_ge(a_evk, t - 1)
                            for g in range(AKV):
                                last = tr(pb[2 + t % 2][:, g * P:(g + 1) * P], kd[:, t, g, :, :].rearrange("p j e -> p (j e)"), ident)
                            last.then_inc(a_trk, 1)

                with ExitStack() as sc_:
                    sc = sb(sc_, "a_sc", [P, 2, AH, 512])
                    pT = sb(sc_, "a_pT", [P, 2, 512])
                    Oa = sb(sc_, "a_O", [P, 2, 512])
                    mx = sb(sc_, "a_mx", [P, 2, 4, AH])
                    lo = (0, 1, 1, 2, 3)
                    hi = (0, 2, 3, 4, 4)
                    nloc = [(hi[t] - lo[t] + 1) * P for t in range(NT)]
                    nk = [nloc[t] + (P if t else 0) for t in range(NT)]
                    mask_at = (None, P, 0, 0, 512)
                    with nc.Block() as block:
                        @block.tensor
                        def _(pe):
                            def scores(t):
                                for h in range(AH):
                                    i = 8 * t + h
                                    if i >= 4:
                                        pe.wait_ge(a_msk, i - 3)
                                    r = slice(64 * (h % 2), 64 * (h % 2) + 64)
                                    q = qT[r, h // 2, t * P:(t + 1) * P]
                                    last = mm(pb[i % 4][:, 0:nloc[t]], q, kT[r, h // 4, lo[t] * P:(hi[t] + 1) * P], start=True, stop=True)
                                    if t:
                                        last = mm(pb[i % 4][:, nloc[t]:nk[t]], q, kT[r, h // 4, TOK:TOK + P], start=True, stop=True)
                                    last.then_inc(a_sc, 1)

                            def pv(t, h):
                                i = 8 * t + h
                                pe.wait_ge(a_pe, i + 1)
                                if h == 0 and t:
                                    pe.wait_ge(a_o, t)
                                n = nk[t] // P
                                for j in range(n):
                                    kt_ = lo[t] + j
                                    vv = kc[:, 1, :] if t and j == n - 1 else a[:, kt_, QW + KVW:]
                                    g = h // 4
                                    last = mm(pb[6][:, h * ADH:(h + 1) * ADH], pT[:, h % 2, j * P:(j + 1) * P], vv[:, g * ADH:(g + 1) * ADH],
                                              start=(j == 0), stop=(j == n - 1))
                                last.then_inc(a_pv, 1)

                            def o_transpose(t):
                                pe.wait_ge(a_o, t + 1)
                                if t:
                                    pe.wait_ge(a_oe, t)
                                for j in range(4):
                                    last = tr(pb[7][:, j * P:(j + 1) * P], Oa[:, t % 2, j * P:(j + 1) * P], ident)
                                last.then_inc(a_ot, 1)

                            scores(0)
                            for t in range(NT):
                                if t + 1 < NT:
                                    scores(t + 1)
                                if t:
                                    o_transpose(t - 1)
                                for h in range(AH):
                                    i = 8 * t + h
                                    pe.wait_ge(a_ex, i + 1)
                                    if i >= 2:
                                        pe.wait_ge(a_pe, i - 1)
                                    for j in range(nk[t] // P):
                                        last = tr(pb[4 + h % 2][:, j * P:(j + 1) * P], sc[:, t % 2, h, j * P:(j + 1) * P], ident)
                                    last.then_inc(a_pt, 1)
                                    if h:
                                        pv(t, h - 1)
                                pv(t, AH - 1)
                            o_transpose(NT - 1)

                        @block.vector
                        def _(dve):
                            link = chain("dve", dve)

                            def mask(t):
                                b = t % 2
                                if t >= 2:
                                    dve.wait_ge(a_pt, 8 * (t - 1))
                                for h in range(AH):
                                    i = 8 * t + h
                                    dve.wait_ge(a_sc, i + 1)
                                    if t:
                                        V.scalar_tensor_tensor(out=sc[:, b, h, 0:nk[t]], in0=pb[i % 4][:, 0:nk[t]], scalar=A_SCALE,
                                                               in1=amask[:, mask_at[t]:mask_at[t] + nk[t]], op0=ALU.mult, op1=ALU.add).then_inc(a_msk, 1)
                                    else:
                                        V.tensor_scalar(sc[:, b, h, 0:nk[t]], pb[i % 4][:, 0:nk[t]], A_SCALE, None, ALU.mult).then_inc(a_msk, 1)
                                dve.wait_ge(a_msk, 8 * t + 8)
                                link(V.tensor_reduce(mx[:, b, 0, :], sc[:, b, :, 0:nk[t]], AX.X, ALU.max))
                                link(V.tensor_tensor(mx[:, b, 0, :], mx[:, b, 0, :], sink[:, :], ALU.max))
                                V.tensor_tensor(mx[:, b, 1, :], sink[:, :], mx[:, b, 0, :], ALU.subtract).then_inc(a_df, 1)
                                dve.wait_ge(a_df, t + 1)
                                V.tensor_scalar(mx[:, b, 0, :], mx[:, b, 0, :], -1.0, None, ALU.mult).then_inc(a_nm, 1)

                            def o_evac(t):
                                dve.wait_ge(a_ot, t + 1)
                                V.tensor_copy(yT[2][:, :, t * P:(t + 1) * P], v4(pb[7][:, :])).then_inc(a_oe, 1)

                            mask(0)
                            for t in range(NT):
                                b = t % 2
                                if t + 1 < NT:
                                    mask(t + 1)
                                if t:
                                    o_evac(t - 1)
                                dve.wait_ge(a_es, t + 1)
                                link(V.tensor_tensor(mx[:, b, 3, :], mx[:, b, 2, :], mx[:, b, 1, :], ALU.add))
                                link(V.reciprocal(mx[:, b, 3, :], mx[:, b, 3, :]))
                                dve.wait_ge(a_pv, 8 * t + 8)
                                V.tensor_tensor(Oa[:, b, :].rearrange("p (h e) -> p h e", h=AH), pb[6][:, :].rearrange("p (h e) -> p h e", h=AH),
                                                mx[:, b, 3, :, None].to_broadcast([P, AH, ADH]), ALU.mult).then_inc(a_o, 1)
                            o_evac(NT - 1)

                        @block.scalar
                        def _(act):
                            for t in range(NT):
                                b = t % 2
                                act.wait_ge(a_nm, t + 1)
                                for h in range(AH):
                                    S.activation(sc[:, b, h, 0:nk[t]], sc[:, b, h, 0:nk[t]], ACT.Exp, bias=mx[:, b, 0, h:h + 1],
                                                 accum_out=mx[:, b, 2, h:h + 1]).then_inc(a_ex, 1)
                                act.wait_ge(a_ex, 8 * t + 8)
                                S.activation(mx[:, b, 1, :], mx[:, b, 1, :], ACT.Exp).then_inc(a_es, 1)
                                for h in range(AH):
                                    i = 8 * t + h
                                    act.wait_ge(a_pt, i + 1)
                                    if i >= 2:
                                        act.wait_ge(a_pv, i - 1)
                                    S.activation(pT[:, h % 2, 0:nk[t]], pb[4 + h % 2][:, 0:nk[t]], ACT.Copy).then_inc(a_pe, 1)

        NLEV = 7
        CH = 12
        TPAD = TOK + 6
        TCONV = TOK + 2

        def stage_deltanet(l):
            (g_cw, g_cwt, g_cwe, g_pad, g_eps, g_cv, g_si, g_sq, g_ss, g_sr, g_nr, g_ktr, g_kte, g_bai) = [sem("g_" + n) for n in (
                "conv_w_in", "conv_w_transposed", "conv_w_evac", "pads_zeroed", "eps_set", "conv", "silu", "squared", "square_sum", "root",
                "normed", "kv_transposed", "kv_evac", "beta_decay")]
            (g_st_in, g_zero, g_D, g_KK, g_dm, g_E, g_QE, g_ket, g_A, g_at, g_atc, g_T, g_atm, g_X, g_Xc, g_Y, g_kb, g_W, g_Wc, g_vn, g_vnc,
             g_in, g_inc, g_it, g_O, g_up, g_S, g_out) = [sem("g_" + n) for n in (
                "state_in", "zeroed", "D", "KK_QK", "masked", "E", "E_products", "KE_transposed", "A", "A_transposed", "At_copied", "T",
                "At_level", "X", "X_copied", "Y", "kvw", "W", "W_copied", "vn", "vn_copied", "inter", "inter_scaled", "intra", "O", "update",
                "S", "state_out")]
            with ExitStack() as st:
                O = sb(st, "g_O", [P, NT, 512])
                tokens = st.enter_context(ExitStack())
                qkv = sb(tokens, "g_qkv", [P, CH, TPAD])
                jobs = []
                for n in range(6):
                    for c in range(2):
                        y = qkv[:, 2 * n + c, :]
                        jobs.append((n, "cols", c, HALVES[0], [(y[:, 2:P + 2], 0, P), (y[:, P + 4:324], P, 320)], 1.0))
                        jobs.append((n, "cols", c, HALVES[1], [(y[:, 324:644], 0, 320)], 1.0))
                with ExitStack() as wst:
                    project("gproj", [(A["w_in"], O_GQKV + CW * n) for n in range(6)], jobs)(l, *weight_buffers(wst, "g"))
                kt = sb(tokens, "g_k", [P, NT, 512])
                vt = sb(tokens, "g_v", [P, NT, 512])
                with ExitStack() as cst:
                    cwr = sb(cst, "g_cwr", [5, CH * P])
                    cw = sb(cst, "g_cw", [P, CH, 5])
                    cv = sb(cst, "g_cv", [P, 3, TCONV])
                    sq = sb(cst, "g_sq", [P, 2, TOK])
                    root = sb(cst, "g_root", [P, 2, TOK])
                    eps = sb(cst, "g_eps", [P, 2])
                    with nc.Block() as block:
                        @block.sync
                        def _(sp):
                            sp.dma_start(cwr[:, :], A["g_conv_w"][l, :, :]).then_inc(g_cw, 16)

                        @block.gpsimd
                        def _(pool):
                            for o, n in ((0, 2), (P + 2, 2), (TPAD - 2, 2)):
                                last = G.memset(qkv[:, :, o:o + n], 0.0)
                            last.then_inc(g_pad, 1)
                            G.memset(eps[:, 0:1], DH * EPS)
                            G.memset(eps[:, 1:2], EPS).then_inc(g_eps, 1)

                        @block.vector
                        def _(dve):
                            link = chain("dve", dve)
                            dve.wait_ge(g_cwt, 1)
                            V.tensor_copy(cw[:, :, :].rearrange("p c k -> p (c k)"), pb[6][:, 0:5 * CH]).then_inc(g_cwe, 1)
                            dve.wait_ge(g_cwe, 1)
                            dve.wait_ge(g_pad, 1)
                            for c in range(CH):
                                if c >= 3:
                                    dve.wait_ge(g_si, c - 2)
                                y = cv[:, c % 3, :]
                                link(V.tensor_scalar(y, qkv[:, c, 0:TCONV], cw[:, c, 0:1], None, ALU.mult))
                                for j in range(1, 4):
                                    link(V.scalar_tensor_tensor(out=y, in0=qkv[:, c, j:j + TCONV], scalar=cw[:, c, j:j + 1], in1=y,
                                                                op0=ALU.mult, op1=ALU.add))
                                V.scalar_tensor_tensor(out=y, in0=qkv[:, c, 4:4 + TCONV], scalar=cw[:, c, 4:5], in1=y,
                                                       op0=ALU.mult, op1=ALU.add).then_inc(g_cv, 1)
                            for c in range(8):
                                dve.wait_ge(g_sr, c + 1)
                                link(V.reciprocal(root[:, c % 2, :], root[:, c % 2, :]))
                                V.tensor_tensor(qkv[:, c, 0:TOK], qkv[:, c, 0:TOK], root[:, c % 2, :], ALU.mult).then_inc(g_nr, 1)
                            for i in range(2 * NT):
                                dve.wait_ge(g_ktr, i + 1)
                                dst = (vt, kt)[i // NT]
                                V.tensor_copy(dst[:, i % NT, :], pb[4 + i % 2][:, :]).then_inc(g_kte, 1)

                        @block.scalar
                        def _(act):
                            for c in range(CH):
                                act.wait_ge(g_cv, c + 1)
                                S.activation(qkv[:, c, 0:P], cv[:, c % 3, 0:P], ACT.Silu)
                                S.activation(qkv[:, c, P:TOK], cv[:, c % 3, P + 2:TCONV], ACT.Silu).then_inc(g_si, 1)
                            act.wait_ge(g_si, CH)
                            act.wait_ge(g_eps, 1)
                            for c in range(9):
                                if c < 8:
                                    if c >= 2:
                                        act.wait_ge(g_ss, c - 1)
                                    S.activation(sq[:, c % 2, :], qkv[:, c, 0:TOK], ACT.Square).then_inc(g_sq, 1)
                                if c:
                                    e = c - 1
                                    act.wait_ge(g_ss, c)
                                    if e >= 2:
                                        act.wait_ge(g_nr, e - 1)
                                    kw_ = dict(scale=float(DH) if e < 4 else 1.0, bias=eps[:, 0:1] if e < 4 else eps[:, 1:2])
                                    S.activation(root[:, e % 2, 0:P], pb[2 * (e % 2)][:, 0:P], ACT.Sqrt, **kw_)
                                    S.activation(root[:, e % 2, P:TOK], pb[2 * (e % 2) + 1][:, :], ACT.Sqrt, **kw_).then_inc(g_sr, 1)

                        @block.tensor
                        def _(pe):
                            pe.wait_ge(g_cw, 16)
                            for c in range(CH):
                                last = tr(pb[6][:, 5 * c:5 * c + 5], cwr[:, c * P:(c + 1) * P], ident[0:5, 0:5])
                            last.then_inc(g_cwt, 1)
                            for c in range(8):
                                pe.wait_ge(g_sq, c + 1)
                                if c >= 2:
                                    pe.wait_ge(g_sr, c - 1)
                                mm(pb[2 * (c % 2)][:, 0:P], ones, sq[:, c % 2, 0:P], start=True, stop=True)
                                mm(pb[2 * (c % 2) + 1][:, :], ones, sq[:, c % 2, P:TOK], start=True, stop=True).then_inc(g_ss, 1)
                            for i in range(2 * NT):
                                t, o = i % NT, (8, 4)[i // NT]
                                if i == NT:
                                    pe.wait_ge(g_nr, 8)
                                if i >= 2:
                                    pe.wait_ge(g_kte, i - 1)
                                for h in range(4):
                                    last = tr(pb[4 + i % 2][:, h * P:(h + 1) * P], qkv[:, o + h, t * P:(t + 1) * P], ident)
                                last.then_inc(g_ktr, 1)

                qT = lambda h, c: qkv[:, h, c * P:(c + 1) * P]
                kT = lambda h, c: qkv[:, 4 + h, c * P:(c + 1) * P]
                sl = lambda c: slice(c * P, (c + 1) * P)
                tile = lambda d, p: (FT, BT)[d][p]
                both = (0, 1)
                with ExitStack() as sc:
                    buf = lambda n: [sb(sc, f"g_{n}{d}", [P, 512]) for d in both]
                    EX, AM, AtW, Tv, Tt, QE, kb, vb, kd, it = [buf(n) for n in ("EX", "AM", "AtW", "Tv", "Tt", "QE", "kb", "vb", "kd", "it")]
                    St = [[sb(sc, f"g_S{g}{d}", [P, 512]) for d in both] for g in both]
                    bai = sb(sc, "g_bai", [P, NT, 16])
                    bk = [[pb[4 * d + i] for i in range(4)] for d in both]
                    bc = lambda a: a[:, None, :].to_broadcast([P, 4, P])
                    lvl = lambda d, j: bc((levT if d else lev)[:, j, :])
                    lvlT = lambda d, j: bc((lev if d else levT)[:, j, :])
                    with nc.Block() as block:
                        @block.sync
                        def _(sp):
                            for d in both:
                                sp.dma_start(v4(St[1][d][:, :]), A["state_gdn_S"][0, l, d, :, :, :].rearrange("h d e -> d h e")).then_inc(g_st_in, 16)
                            sp.wait_ge(g_S, 2)
                            for d in both:
                                sp.dma_start(new_S[0, l, d, :, :, :].rearrange("h d e -> d h e"), v4(St[0][d][:, :])).then_inc(g_out, 16)
                            sp.wait_ge(g_out, 32)

                        @block.gpsimd
                        def _(pool):
                            for d in both:
                                G.memset(St[0][d][:, :], 0.0)
                            G.memset(O[:, :, :], 0.0).then_inc(g_zero, 1)
                            G.tensor_tensor(bai[:, :, :], cols[:, :, 0, :], cols[:, :, 3, :], ALU.mult).then_inc(g_bai, 1)
                            pool.wait_ge(g_bai, 1)
                            for p in range(NT):
                                for d in both:
                                    u, c, r = 2 * p + d, tile(d, p), 8 * d + 4
                                    if u >= 2:
                                        pool.wait_ge(g_up, u - 1)
                                    k3, v3 = v4(kt[:, c, :]), v4(vt[:, c, :])
                                    w = lambda a: a[:, :, None].to_broadcast([P, 4, DH])
                                    G.tensor_tensor(v4(kb[d][:, :]), k3, bai[:, c, r:r + 4, None].to_broadcast([P, 4, DH]), ALU.mult)
                                    G.tensor_tensor(v4(vb[d][:, :]), v3, cols[:, c, 3, r:r + 4, None].to_broadcast([P, 4, DH]), ALU.mult)
                                    G.tensor_tensor(v4(kd[d][:, :]), k3, cols[:, c, 1, r:r + 4, None].to_broadcast([P, 4, DH]), ALU.mult).then_inc(g_kb, 1)
                                for j in range(1, NLEV):
                                    for d in both:
                                        u = 2 * p + d
                                        if j == 1:
                                            pool.wait_ge(g_T, 14 * p + d + 1)
                                            pool.wait_ge(g_atc, u + 1)
                                        else:
                                            pool.wait_ge(g_X, 12 * p + 2 * (j - 2) + d + 1)
                                        G.tensor_tensor(v4(AM[d][:, :]), v4(AtW[d][:, :]), lvlT(d, j), ALU.mult).then_inc(g_atm, 1)

                        @block.tensor
                        def _(pe):
                            pe.wait_ge(g_zero, 1)
                            for p in range(NT):
                                for d in both:
                                    u, c = 2 * p + d, tile(d, p)
                                    r = slice(64 * d + 32, 64 * d + 64)
                                    B = bk[d]
                                    if u >= 2:
                                        pe.wait_ge(g_inc, u - 1)
                                    mm(B[0][:, :], betar[r, sl(c)], sel[r, :, :].rearrange("p h s -> p (h s)"), start=True, stop=False)
                                    for h in range(4):
                                        last = mm(B[0][:, sl(h)], sel[r, h, :], alpha[r, sl(c)], start=False, stop=(h == 3))
                                    last.then_inc(g_D, 1)
                                    if u >= 2:
                                        pe.wait_ge(g_S, u - 1)
                                        pe.wait_ge(g_vnc, u - 1)
                                    for h in range(4):
                                        mm(B[1][:, sl(h)], kT(h, c), kT(h, c), start=True, stop=True)
                                        last = mm(B[2][:, sl(h)], kT(h, c), qT(h, c), start=True, stop=True)
                                    last.then_inc(g_KK, 1)
                                for d in both:
                                    u, B = 2 * p + d, bk[d]
                                    pe.wait_ge(g_QE, u + 1)
                                    if u >= 2:
                                        pe.wait_ge(g_O, u - 1)
                                    for h in range(4):
                                        last = tr(B[3][:, sl(h)], Tv[d][:, sl(h)], ident)
                                    last.then_inc(g_ket, 1)
                                for d in both:
                                    u, B = 2 * p + d, bk[d]
                                    pe.wait_ge(g_A, u + 1)
                                    for h in range(4):
                                        last = tr(B[0][:, sl(h)], AM[d][:, sl(h)], ident)
                                    last.then_inc(g_at, 1)
                                for j in range(1, NLEV):
                                    for d in both:
                                        B = bk[d]
                                        n = 12 * p + 2 * (j - 1) + d
                                        pe.wait_ge(g_atm, n + 1)
                                        pe.wait_ge(g_T, 14 * p + 2 * (j - 1) + d + 1)
                                        for h in range(4):
                                            last = mm(B[1][:, sl(h)], AM[d][:, sl(h)], Tv[d][:, sl(h)], start=True, stop=True)
                                        last.then_inc(g_X, 1)
                                    for d in both:
                                        B = bk[d]
                                        n = 12 * p + 2 * (j - 1) + d
                                        pe.wait_ge(g_Xc, n + 1)
                                        for h in range(4):
                                            if j < NLEV - 1:
                                                mm(B[2][:, sl(h)], Tt[d][:, sl(h)], EX[d][:, sl(h)], start=True, stop=True)
                                            last = mm(B[3][:, sl(h)], EX[d][:, sl(h)], Tt[d][:, sl(h)], start=True, stop=True)
                                        last.then_inc(g_Y, 1)
                                for d in both:
                                    u, B = 2 * p + d, bk[d]
                                    pe.wait_ge(g_T, 14 * p + 2 * (NLEV - 1) + d + 1)
                                    pe.wait_ge(g_kb, u + 1)
                                    for h in range(4):
                                        last = mm(B[1][:, sl(h)], kb[d][:, sl(h)], Tt[d][:, sl(h)], start=True, stop=True)
                                    last.then_inc(g_W, 1)
                                if p == 1:
                                    pe.wait_ge(g_st_in, 32)
                                for d in both:
                                    u, c, B = 2 * p + d, tile(d, p), bk[d]
                                    Sd = St[min(p, 1)][d]
                                    for h in range(4):
                                        last = mm(B[0][:, sl(h)], qT(h, c), Sd[:, sl(h)], start=True, stop=True)
                                    last.then_inc(g_in, 1)
                                    pe.wait_ge(g_Wc, u + 1)
                                    for h in range(4):
                                        mm(B[2][:, sl(h)], Tt[d][:, sl(h)], vb[d][:, sl(h)], start=True, stop=False)
                                        last = mm(B[2][:, sl(h)], AtW[d][:, sl(h)], Sd[:, sl(h)], start=False, stop=True)
                                    last.then_inc(g_vn, 1)
                                for d in both:
                                    u, B = 2 * p + d, bk[d]
                                    pe.wait_ge(g_vnc, u + 1)
                                    for h in range(4):
                                        last = mm(B[3][:, sl(h)], QE[d][:, sl(h)], Tv[d][:, sl(h)], start=True, stop=True)
                                    last.then_inc(g_it, 1)
                                    for h in range(4):
                                        last = mm(B[1][:, sl(h)], kd[d][:, sl(h)], Tv[d][:, sl(h)], start=True, stop=True)
                                    last.then_inc(g_up, 1)

                        @block.scalar
                        def _(act):
                            for p in range(NT):
                                for d in both:
                                    act.wait_ge(g_dm, 2 * p + d + 1)
                                    S.activation(EX[d][:, :], EX[d][:, :], ACT.Exp).then_inc(g_E, 1)
                                for d in both:
                                    act.wait_ge(g_at, 2 * p + d + 1)
                                    S.activation(AtW[d][:, :], bk[d][0][:, :], ACT.Copy).then_inc(g_atc, 1)
                                for j in range(1, NLEV):
                                    for d in both:
                                        act.wait_ge(g_X, 12 * p + 2 * (j - 1) + d + 1)
                                        S.activation(EX[d][:, :], bk[d][1][:, :], ACT.Copy).then_inc(g_Xc, 1)
                                for d in both:
                                    u, c, B = 2 * p + d, tile(d, p), bk[d]
                                    act.wait_ge(g_W, u + 1)
                                    S.activation(AtW[d][:, :], B[1][:, :], ACT.Copy, scale=-1.0).then_inc(g_Wc, 1)
                                for d in both:
                                    u, c, B = 2 * p + d, tile(d, p), bk[d]
                                    act.wait_ge(g_in, u + 1)
                                    if u >= 2:
                                        act.wait_ge(g_O, u - 1)
                                    for h in range(4):
                                        last = S.activation(it[d][:, sl(h)], B[0][:, sl(h)], ACT.Copy, scale=cols[:, c, 0, 8 * d + 4 + h:8 * d + 5 + h])
                                    last.then_inc(g_inc, 1)

                        @block.vector
                        def _(dve):
                            link = chain("dve", dve)
                            for p in range(NT):
                                for d in both:
                                    dve.wait_ge(g_D, 2 * p + d + 1)
                                    V.tensor_tensor(v4(EX[d][:, :]), v4(bk[d][0][:, :]), bc(K("maskB" if d else "maskF")), ALU.min).then_inc(g_dm, 1)
                                for d in both:
                                    u, B = 2 * p + d, bk[d]
                                    dve.wait_ge(g_E, u + 1)
                                    dve.wait_ge(g_KK, u + 1)
                                    V.tensor_tensor(QE[d][:, :], EX[d][:, :], B[2][:, :], ALU.mult)
                                    V.tensor_tensor(Tv[d][:, :], EX[d][:, :], B[1][:, :], ALU.mult).then_inc(g_QE, 1)
                                for d in both:
                                    u, c, B = 2 * p + d, tile(d, p), bk[d]
                                    dve.wait_ge(g_ket, u + 1)
                                    for h in range(4):
                                        last = V.scalar_tensor_tensor(out=AM[d][:, sl(h)], in0=B[3][:, sl(h)], scalar=cols[:, c, 3, 8 * d + 4 + h:8 * d + 5 + h],
                                                                      in1=K("strictF" if d else "strictB"), op0=ALU.mult, op1=ALU.mult)
                                    last.then_inc(g_A, 1)
                                for d in both:
                                    u = 2 * p + d
                                    dve.wait_ge(g_A, u + 1)
                                    link(V.tensor_tensor(v4(Tv[d][:, :]), v4(AM[d][:, :]), lvl(d, 0), ALU.mult))
                                    link(V.tensor_tensor(v4(Tv[d][:, :]), bc(ident), v4(Tv[d][:, :]), ALU.subtract))
                                    dve.wait_ge(g_atc, u + 1)
                                    link(V.tensor_tensor(v4(Tt[d][:, :]), v4(AtW[d][:, :]), lvlT(d, 0), ALU.mult))
                                    V.tensor_tensor(v4(Tt[d][:, :]), bc(ident), v4(Tt[d][:, :]), ALU.subtract).then_inc(g_T, 1)
                                for j in range(1, NLEV):
                                    for d in both:
                                        B = bk[d]
                                        dve.wait_ge(g_Y, 12 * p + 2 * (j - 1) + d + 1)
                                        if j < NLEV - 1:
                                            V.tensor_tensor(Tv[d][:, :], Tv[d][:, :], B[2][:, :], ALU.subtract)
                                        V.tensor_tensor(Tt[d][:, :], Tt[d][:, :], B[3][:, :], ALU.subtract).then_inc(g_T, 1)
                                for d in both:
                                    u, B = 2 * p + d, bk[d]
                                    dve.wait_ge(g_vn, u + 1)
                                    V.tensor_copy(Tv[d][:, :], B[2][:, :]).then_inc(g_vnc, 1)
                                for d in both:
                                    u, c, B = 2 * p + d, tile(d, p), bk[d]
                                    dve.wait_ge(g_it, u + 1)
                                    dve.wait_ge(g_inc, u + 1)
                                    link(V.tensor_tensor(it[d][:, :], it[d][:, :], B[3][:, :], ALU.add))
                                    if p == 0 and d == 0:
                                        dve.wait_ge(g_zero, 1)
                                    V.tensor_tensor(O[:, c, :], O[:, c, :], it[d][:, :], ALU.add).then_inc(g_O, 1)
                                    dve.wait_ge(g_up, u + 1)
                                    Sd = St[min(p, 1)][d]
                                    for h in range(4):
                                        last = V.scalar_tensor_tensor(out=Sd[:, sl(h)], in0=Sd[:, sl(h)], scalar=decbc[:, c, 8 * d + 4 + h:8 * d + 5 + h],
                                                                      in1=B[1][:, sl(h)], op0=ALU.mult, op1=ALU.add)
                                    last.then_inc(g_S, 1)
                tokens.close()
                with ExitStack() as fst:
                    gz = sb(fst, "g_z", [P, NT, 512])
                    with ExitStack() as wst:
                        project("gz", [(A["w_in"], O_GZ + CW * n) for n in range(2)],
                                [(n, "rows", t, None, [(gz[:, t, CW * n:CW * n + CW], 0, CW)], ACT.Silu) for n in range(2) for t in range(NT)])(
                                    l, *weight_buffers(wst, "gz"))
                    finish_mixer(1, l, O, gz, A["g_norm_g"], DH)

        def stage_merge(l):
            e_w, e_wb = [[sem(f"e_{n}{i}") for i in range(2)] for n in ("gate_w_in", "branch_w_in")]
            (e_hi, e_lo, e_gt, e_g, e_b, e_sg, e_pr, e_ad, e_tr, e_mhi, e_mlo, e_o, e_om, e_x) = [sem("e_" + n) for n in (
                "w_hi", "w_lo", "gt_in", "gate_product", "branch_product", "sigmoid", "gated", "added", "transposed", "m_hi", "m_lo",
                "out_product", "out_gated", "x_updated")]
            BR = (A["w_br_m"], A["w_br_g"], A["w_br_a"])
            with ExitStack() as st:
                mg = sb(st, "mg", [P, NT, DM])
                Wg = [sb(st, f"e_Wg{i}", [P, KD, CW]) for i in range(2)]
                Ws = [[sb(st, f"e_W{part}{i}", [P, KD, CW], f32r) for part in ("hi", "lo")] for i in range(2)]
                Wr = [sb(st, f"e_Wr{i}", [P, 4, CW]) for i in range(2)]
                gt = sb(st, "e_gt", [P, 2, DM])
                sg = sb(st, "e_sg", [P, 4, CW])
                QB = DM // CW
                NG3 = 3 * QB
                cw = lambda q: slice(CW * q, CW * q + CW)
                with nc.Block() as block:
                    @block.sync
                    def _(sp):
                        for n in range(NG3 + QB):
                            if n >= 2:
                                sp.wait_ge(e_lo, n - 1)
                            if n < NG3:
                                sp.dma_start(Wg[n % 2][:, :, :], dram_cols(A["w_in"], l, O_GATE + CW * n, CW)).then_inc(e_w[n % 2], 16)
                                if n >= 2:
                                    sp.wait_ge(e_b, NT * (n - 1))
                                sp.dma_start(Wr[n % 2][:, :, :], BR[n // QB][l, :, cw(n % QB)].rearrange("(k p) n -> p k n", p=P)).then_inc(e_wb[n % 2], 16)
                            else:
                                sp.dma_start(Wg[n % 2][:, :, :], dram_cols(A["w_out"], l, CW * (n - NG3), CW)).then_inc(e_w[n % 2], 16)
                            if n == 1:
                                for g in range(2):
                                    sp.dma_start(gt[:, g, :], modd[g:g + 1, 2 * DM:3 * DM].to_broadcast([P, DM])).then_inc(e_gt, 16)

                    def products_of(n):
                        return (e_g, NT * (n + 1)) if n < NG3 else (e_o, NT * (n - NG3 + 1))

                    @block.tensor
                    def _(pe):
                        for n in range(NG3):
                            pe.wait_ge(e_lo, n + 1)
                            pe.wait_ge(e_wb[n % 2], 16 * (n // 2 + 1))
                            for t in range(NT):
                                i = NT * n + t
                                ts = slice(t * P, (t + 1) * P)
                                if i >= 2:
                                    pe.wait_ge(e_sg, i - 1)
                                product(pb[2 * (i % 2)][:, 0:CW], lambda a, k: hS[a][:, k, ts], lambda a, k: Ws[n % 2][a][:, k, :], KD).then_inc(e_g, 1)
                                if i >= 2:
                                    pe.wait_ge(e_pr, i - 1)
                                for k in range(4):
                                    last = mm(pb[2 * (i % 2) + 1][:, 0:CW], yT[n // QB][:, k, ts], Wr[n % 2][:, k, :], start=(k == 0), stop=(k == 3))
                                last.then_inc(e_b, 1)
                        for t in range(NT):
                            pe.wait_ge(e_ad, (NG3 - 1) * NT + t + 1)
                            if t >= 2:
                                pe.wait_ge(e_mlo, 2 * (t - 1))
                            for j in range(2):
                                for k in range(4):
                                    last = tr(pb[4 + 2 * (t % 2) + j][:, k * P:(k + 1) * P], mg[:, t, (4 * j + k) * P:(4 * j + k + 1) * P], ident)
                                last.then_inc(e_tr, 1)
                        pe.wait_ge(e_pr, NG3 * NT)
                        for q in range(QB):
                            n = NG3 + q
                            pe.wait_ge(e_lo, n + 1)
                            for t in range(NT):
                                i = NT * q + t
                                if q == 0:
                                    pe.wait_ge(e_mlo, 2 * (t + 1))
                                if i >= 2:
                                    pe.wait_ge(e_om, i - 1)
                                product(pb[i % 2][:, 0:CW], lambda a, k: hS[a][:, k, t * P:(t + 1) * P], lambda a, k: Ws[n % 2][a][:, k, :], KD).then_inc(e_o, 1)

                    @block.scalar
                    def _(act):
                        def weights_hi(n):
                            act.wait_ge(e_w[n % 2], 16 * (n // 2 + 1))
                            if n >= 2:
                                act.wait_ge(*products_of(n - 2))
                            S.activation(Ws[n % 2][0][:, :, :], Wg[n % 2][:, :, :], ACT.Copy).then_inc(e_hi, 1)

                        weights_hi(0)
                        for n in range(NG3):
                            weights_hi(n + 1)
                            for t in range(NT):
                                i = NT * n + t
                                act.wait_ge(e_g, i + 1)
                                if i >= 4:
                                    act.wait_ge(e_ad, i - 3)
                                S.activation(sg[:, i % 4, :], pb[2 * (i % 2)][:, 0:CW], ACT.Sigmoid).then_inc(e_sg, 1)
                        for t in range(NT):
                            for j in range(2):
                                act.wait_ge(e_tr, 2 * t + j + 1)
                                S.activation(hS[0][:, 4 * j:4 * j + 4, t * P:(t + 1) * P], v4(pb[4 + 2 * (t % 2) + j][:, :]), ACT.Copy).then_inc(e_mhi, 1)
                        for q in range(QB - 1):
                            weights_hi(NG3 + q + 1)

                    @block.vector
                    def _(dve):
                        def weights_lo(n):
                            dve.wait_ge(e_hi, n + 1)
                            V.tensor_tensor(Ws[n % 2][1][:, :, :], Wg[n % 2][:, :, :], Ws[n % 2][0][:, :, :], ALU.subtract).then_inc(e_lo, 1)

                        weights_lo(0)
                        for n in range(NG3):
                            weights_lo(n + 1)
                            for t in range(NT):
                                i = NT * n + t
                                dve.wait_ge(e_sg, i + 1)
                                dve.wait_ge(e_b, i + 1)
                                V.tensor_tensor(sg[:, i % 4, :], sg[:, i % 4, :], pb[2 * (i % 2) + 1][:, 0:CW], ALU.mult).then_inc(e_pr, 1)
                        for t in range(NT):
                            for j in range(2):
                                dve.wait_ge(e_mhi, 2 * t + j + 1)
                                sl_ = (slice(None), slice(4 * j, 4 * j + 4), slice(t * P, (t + 1) * P))
                                V.tensor_tensor(hS[1][sl_], v4(pb[4 + 2 * (t % 2) + j][:, :]), hS[0][sl_], ALU.subtract).then_inc(e_mlo, 1)
                        dve.wait_ge(e_gt, 32)
                        for q in range(QB):
                            if q < QB - 1:
                                weights_lo(NG3 + q + 1)
                            for t in range(NT):
                                i = NT * q + t
                                dve.wait_ge(e_o, i + 1)
                                if i >= 4:
                                    dve.wait_ge(e_x, i - 3)
                                elif i == 0:
                                    dve.wait_ge(e_ad, NG3 * NT)
                                V.tensor_tensor(sg[:, i % 4, :], pb[i % 2][:, 0:CW], gt[:, min(t, 1), cw(q)], ALU.mult).then_inc(e_om, 1)

                    @block.gpsimd
                    def _(pool):
                        for i in range(NG3 * NT):
                            n, t = i // NT, i % NT
                            dst = mg[:, t, cw(n % QB)]
                            pool.wait_ge(e_pr, i + 1)
                            if n < QB:
                                G.tensor_copy(dst, sg[:, i % 4, :]).then_inc(e_ad, 1)
                            else:
                                pool.wait_ge(e_ad, i - QB * NT + 1)
                                G.tensor_tensor(dst, dst, sg[:, i % 4, :], ALU.add).then_inc(e_ad, 1)
                        for i in range(QB * NT):
                            q, t = i // NT, i % NT
                            pool.wait_ge(e_om, i + 1)
                            G.tensor_tensor(x[:, t, cw(q)], x[:, t, cw(q)], sg[:, i % 4, :], ALU.add).then_inc(e_x, 1)

        RING = 6
        NG = NT * PH

        def stage_experts(l, h2, Wq, kT, wq_in, keys_in):
            u_in = [sem(f"u_in{i}") for i in range(RING)]
            v_in = [sem(f"v_in{i}") for i in range(RING)]
            (x_kt, x_ke, x_q, x_qe, x_s, x_se, x_gt, x_iota, x_idx, x_nm, x_ex, x_dot, x_gelu, x_coef, x_diag, x_vmm, x_add, x_rd) = [sem("x_" + n) for n in (
                "keys_transposed", "keys_evac", "q", "q_evac", "scores", "scores_evac", "gt_in", "iota_in", "indices", "neg_max", "exp", "dot", "gelu", "coef", "diag", "v_product", "x_updated", "scores_read")]
            table_u = A["p_u"].rearrange("l e d -> (l e) d")
            table_v = A["p_v"].rearrange("l e d -> (l e) d")
            with ExitStack() as st:
                ub = sb(st, "ub", [P, RING, DM])
                vb = sb(st, "vb", [P, RING, DM])
                qT = sb(st, "x_qT", [P, 2, P])
                sc = sb(st, "x_sc", [P, 3, 2, PK])
                gt = sb(st, "x_gt2", [P, DM])
                iota = sb(st, "x_iota", [P, PTOP])
                sv = sb(st, "x_sv", [P, 2, PTOP])
                si = sb(st, "x_si", [P, 2, PTOP], u32)
                sif = sb(st, "x_sif", [P, 2, PTOP])
                cand = sb(st, "x_cand", [P, PTOP, PTOP])
                fi = sb(st, "x_fi", [P, PTOP], u32)
                ab = sb(st, "x_ab", [P, 2, PTOP], u32)
                abf = sb(st, "x_abf", [P, 2, PTOP])
                eq = sb(st, "x_eq", [P, 2, PTOP, PTOP])
                e01 = sb(st, "x_e01", [P, 2, PTOP])
                ef = sb(st, "x_ef", [P, PTOP])
                fv = sb(st, "x_fv", [P, 4, PTOP])
                nm = sb(st, "x_nm", [P, 4, 3])
                idx = sb(st, "x_idx", [P, 4, PTOP], i32)
                dot = sb(st, "x_dots", [P, 4, PTOP])
                coef = sb(st, "x_coefs", [P, 4, PTOP])
                diag = sb(st, "x_diags", [P, RING, P])
                ybuf = sb(st, "x_y", [P, 512])
                with nc.Block() as block:
                    @block.sync
                    def _(sp):
                        for h in range(PH):
                            sp.dma_start(vb[:, h // 4, (h % 4) * 2 * P:(h % 4 + 1) * 2 * P].rearrange("p (c d) -> p c d", c=2),
                                         A["p_keys"][l, h, :, :, :].rearrange("c k d -> k c d")).then_inc(keys_in, 16)
                        sp.dma_start(gt[:, :], modd[0:1, 5 * DM:6 * DM].to_broadcast([P, DM])).then_inc(x_gt, 16)
                        sp.dma_start(iota[:, :], A["consts"][:, COFF["iota16"][0]:COFF["iota16"][0] + 16]).then_inc(x_iota, 16)
                        sp.wait_ge(x_add, 2)
                        sp.dma_start(gt[:, :], modd[1:2, 5 * DM:6 * DM].to_broadcast([P, DM])).then_inc(x_gt, 16)

                    @block.gpsimd
                    def _(pool):
                        def gather(i, s, table, ring, in_, used):
                            n = PTOP * i + s
                            if s == 0:
                                pool.wait_ge(x_idx, i + 1)
                            if n >= RING:
                                pool.wait_ge(used, n - RING + 1)
                            elif n == 0 and table is table_v:
                                pool.wait_ge(x_kt, 4)
                            G.indirect_dma_start(ring[:, n % RING, :], None, table,
                                                 bass.IndirectOffsetOnAxis(ap=idx[:, i % 4, s:s + 1], axis=0)).then_inc(in_[n % RING], 16)

                        for s in range(PTOP):
                            gather(0, s, table_u, ub, u_in, x_dot)
                        for i in range(NG):
                            for s in range(PTOP):
                                if i + 1 < NG:
                                    gather(i + 1, s, table_u, ub, u_in, x_dot)
                                gather(i, s, table_v, vb, v_in, x_vmm)

                    @block.vector
                    def _(dve):
                        link = chain("dve", dve)

                        def route(i):
                            b = i % 4
                            if i >= 4:
                                dve.wait_ge(x_vmm, PTOP * (i - 3))
                            rows = [sc[:, i % 3, c, :] for c in range(2)]
                            dve.wait_ge(x_se, i + 1)
                            for r in range(2):
                                o = slice(8 * r, 8 * r + 8)
                                V.max(sv[:, 0, o], rows[0])
                                link(V.max(sv[:, 1, o], rows[1]))
                                V.max_index(si[:, 0, o], sv[:, 0, o], rows[0])
                                link(V.max_index(si[:, 1, o], sv[:, 1, o], rows[1]))
                                if r == 0:
                                    V.match_replace(rows[0], sv[:, 0, o], rows[0], -3.0e38)
                                    link(V.match_replace(rows[1], sv[:, 1, o], rows[1], -3.0e38))
                            V.tensor_copy(sif[:, :, :], si[:, :, :]).then_inc(x_rd, 1)
                            link(V.tensor_tensor(cand[:, :, :], sv[:, 0, :, None].to_broadcast([P, PTOP, PTOP]),
                                                 sv[:, 1, None, :].to_broadcast([P, PTOP, PTOP]), ALU.add))
                            flat = cand[:, :, :].rearrange("p a b -> p (a b)")
                            for r in range(2):
                                o = slice(8 * r, 8 * r + 8)
                                link(V.max(fv[:, b, o], flat))
                                link(V.max_index(fi[:, o], fv[:, b, o], flat))
                                if r == 0:
                                    link(V.match_replace(flat, fv[:, b, o], flat, -3.0e38))
                            V.tensor_scalar(nm[:, b, 0:1], fv[:, b, 0:1], -1.0, None, ALU.mult).then_inc(x_nm, 1)
                            V.tensor_scalar(ab[:, 0, :], fi[:, :], 4, None, ALU.logical_shift_right)
                            link(V.tensor_scalar(ab[:, 1, :], fi[:, :], 15, None, ALU.bitwise_and))
                            link(V.tensor_copy(abf[:, :, :], ab[:, :, :]))
                            link(V.tensor_tensor(eq[:, :, :, :], abf[:, :, :, None].to_broadcast([P, 2, PTOP, PTOP]),
                                                 iota[:, None, None, :].to_broadcast([P, 2, PTOP, PTOP]), ALU.is_equal))
                            link(V.tensor_tensor(eq[:, :, :, :], eq[:, :, :, :], sif[:, :, None, :].to_broadcast([P, 2, PTOP, PTOP]), ALU.mult))
                            link(V.tensor_reduce(e01[:, :, :], eq[:, :, :, :], AX.X, ALU.add))
                            link(V.scalar_tensor_tensor(out=ef[:, :], in0=e01[:, 0, :], scalar=float(PK), in1=e01[:, 1, :], op0=ALU.mult, op1=ALU.add))
                            V.tensor_scalar(idx[:, b, :], ef[:, :], lbase[:, 0:1], None, ALU.add).then_inc(x_idx, 1)

                        def dots(i):
                            t, b = i // PH, i % 4
                            for s in range(PTOP):
                                n = PTOP * i + s
                                dve.wait_ge(u_in[n % RING], 16 * (n // RING + 1))
                                V.tensor_tensor_reduce(out=ub[:, n % RING, :], in0=ub[:, n % RING, :], in1=h2[:, t, :], scale=1.0, scalar=0.0,
                                                       op0=ALU.mult, op1=ALU.add, accum_out=dot[:, b, s:s + 1]).then_inc(x_dot, 1)

                        def coefs(i):
                            b = i % 4
                            dve.wait_ge(x_ex, i + 1)
                            link(V.reciprocal(nm[:, b, 2:3], nm[:, b, 1:2]))
                            dve.wait_ge(x_gelu, i + 1)
                            V.scalar_tensor_tensor(out=coef[:, b, :], in0=dot[:, b, :], scalar=nm[:, b, 2:3], in1=fv[:, b, :],
                                                   op0=ALU.mult, op1=ALU.mult).then_inc(x_coef, 1)

                        def close(t):
                            dve.wait_ge(x_vmm, PTOP * PH * (t + 1))
                            dve.wait_ge(x_gt, 16 * min(t + 1, 2))
                            for j in range(2):
                                o = slice(512 * j, 512 * j + 512)
                                link(V.tensor_tensor(ybuf[:, :], pb[2 * (t % 2) + j][:, :], gt[:, o], ALU.mult))
                                V.tensor_tensor(x[:, t, o], x[:, t, o], ybuf[:, :], ALU.add).then_inc(x_add, 1)
                                dve.wait_ge(x_add, 2 * t + j + 1)

                        for b in range(4):
                            dve.wait_ge(x_kt, b + 1)
                            V.tensor_copy(kT[:, 4 * b:4 * b + 4, :], v4(pb[b][:, :])).then_inc(x_ke, 1)
                        dve.wait_ge(x_iota, 16)
                        route(0)
                        route(1)
                        dots(0)
                        coefs(0)
                        for i in range(NG):
                            if i + 2 < NG:
                                route(i + 2)
                            if i + 1 < NG:
                                dots(i + 1)
                                coefs(i + 1)
                            if i % PH == 1 and i > PH:
                                close(i // PH - 1)
                        close(NT - 1)

                    @block.scalar
                    def _(act):
                        def weights(i):
                            b = i % 4
                            act.wait_ge(x_nm, i + 1)
                            S.activation(fv[:, b, :], fv[:, b, :], ACT.Exp, bias=nm[:, b, 0:1], accum_out=nm[:, b, 1:2]).then_inc(x_ex, 1)

                        def gelu(i):
                            act.wait_ge(x_dot, PTOP * (i + 1))
                            S.activation(dot[:, i % 4, :], dot[:, i % 4, :], ACT.Gelu).then_inc(x_gelu, 1)

                        def q_evac(i):
                            act.wait_ge(x_q, i + 1)
                            if i >= 1:
                                act.wait_ge(x_s, i)
                            S.activation(qT[:, :, :], pb[4 + i % 2][:, 0:2 * P].rearrange("p (c s) -> p c s", c=2), ACT.Copy).then_inc(x_qe, 1)

                        def sc_evac(i):
                            act.wait_ge(x_s, i + 1)
                            if i >= 3:
                                act.wait_ge(x_rd, i - 2)
                            S.activation(sc[:, i % 3, :, :], pb[6 + i % 2][:, 0:2 * P].rearrange("p (c s) -> p c s", c=2), ACT.Copy).then_inc(x_se, 1)

                        for i in range(3):
                            q_evac(i)
                            sc_evac(i)
                        weights(0)
                        weights(1)
                        gelu(0)
                        for i in range(NG):
                            if i + 3 < NG:
                                q_evac(i + 3)
                                sc_evac(i + 3)
                            if i + 2 < NG:
                                weights(i + 2)
                            act.wait_ge(x_coef, i + 1)
                            for s in range(PTOP):
                                n = PTOP * i + s
                                if n >= RING:
                                    act.wait_ge(x_vmm, n - RING + 1)
                                S.activation(diag[:, n % RING, :], ident[:, :], ACT.Copy, scale=coef[:, i % 4, s:s + 1]).then_inc(x_diag, 1)
                            if i + 1 < NG:
                                gelu(i + 1)

                    @block.tensor
                    def _(pe):
                        pe.wait_ge(keys_in, 16 * PH)
                        for b in range(4):
                            for j in range(4):
                                last = tr(pb[b][:, j * P:(j + 1) * P], vb[:, (4 * b + j) // KD, ((4 * b + j) % KD) * P:((4 * b + j) % KD + 1) * P], ident[:, :])
                            last.then_inc(x_kt, 1)
                        pe.wait_ge(x_ke, 4)

                        def q_product(i):
                            t, h = i // PH, i % PH
                            if i < PH and h % 2 == 0:
                                pe.wait_ge(wq_in[h // 2], 16)
                            if i >= 2:
                                pe.wait_ge(x_qe, i - 1)
                            for c in range(2):
                                for k in range(KD):
                                    last = mm(pb[4 + i % 2][:, c * P:(c + 1) * P], Wq[:, k, (2 * h + c) * P:(2 * h + c + 1) * P], hT[:, k, t * P:(t + 1) * P],
                                              start=(k == 0), stop=(k == KD - 1))
                            last.then_inc(x_q, 1)

                        def scores(i):
                            h = i % PH
                            pe.wait_ge(x_qe, i + 1)
                            if i >= 2:
                                pe.wait_ge(x_se, i - 1)
                            for c in range(2):
                                last = mm(pb[6 + i % 2][:, c * P:(c + 1) * P], qT[:, c, :], kT[:, 2 * h + c, :], start=True, stop=True)
                            last.then_inc(x_s, 1)

                        for i in range(3):
                            q_product(i)
                            scores(i)
                        for i in range(NG):
                            t, h = i // PH, i % PH
                            if i + 3 < NG:
                                q_product(i + 3)
                                scores(i + 3)
                            if h == 0 and t >= 2:
                                pe.wait_ge(x_add, 2 * (t - 1))
                            for s in range(PTOP):
                                n = PTOP * i + s
                                pe.wait_ge(x_diag, n + 1)
                                pe.wait_ge(v_in[n % RING], 16 * (n // RING + 1))
                                for j in range(2):
                                    last = mm(pb[2 * (t % 2) + j][:, :], diag[:, n % RING, :], vb[:, n % RING, 512 * j:512 * j + 512],
                                              start=(h == 0 and s == 0), stop=(h == PH - 1 and s == PTOP - 1))
                                last.then_inc(x_vmm, 1)

        def stage_peer(l):
            nonlocal hT
            with ExitStack() as st:
                hT = sb(st, "h2T", [P, KD, TOK])
                h2 = sb(st, "h2", [P, NT, DM])
                Wq = sb(st, "Wq", [P, KD, 2 * PH * P])
                kT = sb(st, "kT", [P, 2 * PH, PK])
                with stage():
                    wq_in = [sem(f"wq_in{n}") for n in range(4)]
                    keys_in = sem("keys_in")

                    def load_queries(sp):
                        for n in range(4):
                            sp.dma_start(Wq[:, :, 512 * n:512 * n + 512], dram_cols(A["p_wq"], l, 512 * n, 512)).then_inc(wq_in[n], 16)

                    stage_norm(1, h2, ahead=load_queries)
                    stage_experts(l, h2, Wq, kT, wq_in, keys_in)
            with stage():
                nb = sem("next_base")
                with nc.Block() as block:
                    @block.vector
                    def _(dve):
                        V.tensor_scalar(lbase[:, :], lbase[:, :], float(NEXP), None, ALU.add).then_inc(nb, 1)
                        dve.wait_ge(nb, 1)

        def stage_output():
            y_out = sem("y_out")
            with nc.Block() as block:
                @block.sync
                def _(sp):
                    sp.dma_start(y_prompt[0, :, :], x[:, 0, :]).then_inc(y_out, 16)
                    sp.dma_start(y_sample[0, :, :].rearrange("(t p) d -> p t d", p=P), x[:, 1:NT, :]).then_inc(y_out, 16)
                    sp.wait_ge(y_out, 32)

        with nc.Fori(0, DEPTH) as l:
            layer(l)
        with stage():
            stage_output()


_INS = ["x_prompt", "x_sample", "state_mlstm_C", "state_mlstm_n", "state_mlstm_m", "state_gdn_S", "cache_attn_k",
        "cache_attn_v", "c", "c_ctx", "ada_w", "ada_b", "norm1_g", "norm2_g", "w_in", "m_ig_b", "m_fg_b", "m_norm_g",
        "g_conv_w", "g_A_log", "g_dt_bias", "g_norm_g", "a_qnorm_g", "a_knorm_g", "a_sink", "w_br_m", "w_br_g", "w_br_a",
        "w_out", "p_wq", "p_keys", "p_u", "p_v"]
_OUTS = [(1, P, DM), (1, 4 * P, DM), (1, DEPTH, 2, NH, DH, DH), (1, DEPTH, 2, NH, DH), (1, DEPTH, 2, NH),
         (1, DEPTH, 2, NH, DH, DH), (1, DEPTH, P, AKV, ADH), (1, DEPTH, P, AKV, ADH)]


def kernel(**inputs):
    import concourse.bacc as _bacc
    from concourse.bass_utils import run_bass_kernel_spmd as _run

    nc = _bacc.Bacc("TRN2", target_bir_lowering=False, num_devices=1)
    arrays, args, outs = {}, {}, []
    for name in _INS:
        a = np.ascontiguousarray(inputs[name])
        arrays[f"in_{name}"] = a
        args[name] = nc.dram_tensor(f"in_{name}", a.shape, mybir.dt.from_np(a.dtype), kind="ExternalInput").ap()
    arrays["in_consts"] = constants()
    args["consts"] = nc.dram_tensor("in_consts", (P, NCONST), mybir.dt.float32, kind="ExternalInput").ap()
    for i, shape in enumerate(_OUTS):
        outs.append(nc.dram_tensor(f"out_{i}", shape, mybir.dt.float32, kind="ExternalOutput").ap())
    scratch = {"mod": nc.dram_tensor("mod_rows", (2, 6 * DM), mybir.dt.float32, kind="Internal").ap()}
    program(nc, args, outs, scratch)
    r = _run(nc, [arrays], core_ids=[0])
    return tuple(r.results[0][f"out_{i}"] for i in range(len(_OUTS)))
```
